# Optimizing a Trainium2 kernel written in Bass

```python
import jax, jax.numpy as jnp
from jax import lax
import numpy as np

D_MODEL = 1024
BATCH = 1
SEQ = 512
DEPTH = 1
DEC_BATCH = 8
DEC_SEQ = 8
PAST_LEN = 2048
PAGE_SIZE = 128

HEAD_DIM = 64
D_ATTN = D_MODEL // 2
N_HEADS = D_ATTN // HEAD_DIM
N_KV_HEADS = N_HEADS // 4
GQA_GROUP = N_HEADS // N_KV_HEADS
KV_DIM = N_KV_HEADS * HEAD_DIM
N_BRANCH = 3
CMP_LEN = 32
CMP_STRIDE = 16
CMP_HIDDEN = HEAD_DIM
SEL_BLOCK = 64
N_SEL = 16
WINDOW = 512
ROT_DIM = HEAD_DIM // 4
ROPE_THETA = 500000.0
D_CONV = D_MODEL - D_ATTN
CONV_W = 3
D_MIX = D_ATTN + D_CONV
D_FF = ((8 * D_MODEL + 3 * 256 - 1) // (3 * 256)) * 256
N_IN = D_ATTN + 2 * N_BRANCH * KV_DIM + N_BRANCH * N_HEADS + 3 * D_CONV
Q_BLOCK = 64
EPS = 1e-6
NEG_INF = -1e30
SEL_BONUS = 1e3

kernel_name = 'hymba_nsa_shortconv_adaln_step'

def rmsnorm(x, g):
    xf = x.astype(jnp.float32)
    y = xf * lax.rsqrt(jnp.mean(xf * xf, axis=-1, keepdims=True) + EPS)
    return (y * g.astype(jnp.float32)).astype(x.dtype)

def rope(x, pos):
    half = ROT_DIM // 2
    inv = ROPE_THETA ** (-jnp.arange(half, dtype=jnp.float32) * 2.0 / ROT_DIM)
    ang = pos.astype(jnp.float32)[:, None] * inv[None, :]
    cos = jnp.cos(ang)[:, None, :].astype(x.dtype)
    sin = jnp.sin(ang)[:, None, :].astype(x.dtype)
    x1, x2 = x[..., :half], x[..., half:ROT_DIM]
    return jnp.concatenate([x1 * cos - x2 * sin, x2 * cos + x1 * sin, x[..., ROT_DIM:]], axis=-1)

def masked_softmax(s, mask):
    s = jnp.where(mask, s, NEG_INF)
    m = jnp.max(s, axis=-1, keepdims=True)
    e = jnp.where(mask, jnp.exp(s - m), 0.0)
    return e / jnp.maximum(jnp.sum(e, axis=-1, keepdims=True), 1e-30)

def adaln(c, w_ada, b_ada):
    mod = jax.nn.silu(c) @ w_ada + b_ada
    return jnp.split(mod[:, None, :], 6, axis=-1)

def modulate(x, g, shift, scale):
    return rmsnorm(x, g) * (1.0 + scale) + shift

def project(h, pos, w_in, q_norm_g, k_norm_g):
    b, t, _ = h.shape
    sizes = [D_ATTN] + [KV_DIM] * 6 + [N_BRANCH * N_HEADS] + [D_CONV] * 3
    offs = np.cumsum(sizes)[:-1].tolist()
    q, kc, vc, ks, vs, kw, vw, g, hc, bg, cg = jnp.split(h @ w_in, offs, axis=-1)
    heads = lambda z: z.reshape(b, t, -1, HEAD_DIM)
    q = rope(rmsnorm(heads(q), q_norm_g), pos)
    ks = rope(rmsnorm(heads(ks), k_norm_g[1]), pos)
    kw = rope(rmsnorm(heads(kw), k_norm_g[2]), pos)
    gates = jax.nn.sigmoid(g).reshape(b, t, N_HEADS, N_BRANCH)
    u = cg * hc
    return q, heads(kc), heads(vc), ks, heads(vs), kw, heads(vw), gates, u, bg

def compress(rows, pe, w1, w2):
    b, t = rows.shape[:2]
    r_n = CMP_LEN // CMP_STRIDE
    n_ch = t // CMP_STRIDE
    nc = n_ch - r_n + 1
    chunks = rows[:, :n_ch * CMP_STRIDE].reshape(b, n_ch, CMP_STRIDE, N_KV_HEADS, HEAD_DIM)
    chunks = chunks.transpose(0, 1, 3, 2, 4).reshape(b, n_ch, N_KV_HEADS, CMP_STRIDE * HEAD_DIM)
    proj = jnp.einsum('bnkf,rfh->rbnkh', chunks, w1.reshape(r_n, CMP_STRIDE * HEAD_DIM, CMP_HIDDEN))
    pre = sum(proj[r][:, r:r + nc] for r in range(r_n)) + pe.reshape(-1) @ w1
    out = jax.nn.silu(pre) @ w2
    end = jnp.arange(nc) * CMP_STRIDE + CMP_LEN - 1
    return out, end

def compressed_tokens(kc_raw, vc_raw, k_gain, pe, w_ck1, w_ck2, w_cv1, w_cv2):
    kc, end = compress(kc_raw, pe, w_ck1, w_ck2)
    vc, _ = compress(vc_raw, pe, w_cv1, w_cv2)
    return rope(rmsnorm(kc, k_gain), end), vc, end

def to_blocks(rows):
    b, t = rows.shape[:2]
    ns = -(-t // SEL_BLOCK)
    rows = jnp.pad(rows, ((0, 0), (0, ns * SEL_BLOCK - t), (0, 0), (0, 0)))
    return rows.reshape(b, ns, SEL_BLOCK, N_KV_HEADS, HEAD_DIM).transpose(0, 3, 1, 2, 4)

def nsa_attend(q, q_pos, kc, vc, kc_end, ksb, vsb, kw, vw, kw_pos, gates):
    b, nq = q.shape[:2]
    scale = HEAD_DIM ** -0.5
    qh = q.reshape(b, nq, N_KV_HEADS, GQA_GROUP, HEAD_DIM).transpose(0, 2, 3, 1, 4)
    s = jnp.einsum('bkgqd,bnkd->bkgqn', qh, kc).astype(jnp.float32) * scale
    p_cmp = masked_softmax(s, kc_end[None, :] <= q_pos[:, None])
    o_cmp = jnp.einsum('bkgqn,bnkd->bkgqd', p_cmp.astype(vc.dtype), vc)
    ns = ksb.shape[2]
    blk = jnp.arange(ns)
    c_start = kc_end - (CMP_LEN - 1)
    overlap = ((c_start[:, None] < (blk[None, :] + 1) * SEL_BLOCK)
               & (c_start[:, None] + CMP_LEN > blk[None, :] * SEL_BLOCK)).astype(jnp.float32)
    imp = jnp.einsum('bkgqn,nj->bkqj', p_cmp, overlap)
    cur = (q_pos // SEL_BLOCK)[:, None]
    forced = (blk[None, :] == 0) | (blk[None, :] == cur) | (blk[None, :] == cur - 1)
    causal_blk = blk[None, :] * SEL_BLOCK <= q_pos[:, None]
    score = jnp.where(causal_blk, imp + SEL_BONUS * forced.astype(jnp.float32), NEG_INF)
    n_sel = min(N_SEL, ns)
    _, idx = lax.top_k(score, n_sel)
    take = jax.vmap(jax.vmap(lambda rows, i: rows[i]))
    k_sel = take(ksb, idx).reshape(b, N_KV_HEADS, nq, n_sel * SEL_BLOCK, HEAD_DIM)
    v_sel = take(vsb, idx).reshape(b, N_KV_HEADS, nq, n_sel * SEL_BLOCK, HEAD_DIM)
    pos_sel = (idx[..., None] * SEL_BLOCK + jnp.arange(SEL_BLOCK)).reshape(b, N_KV_HEADS, nq, n_sel * SEL_BLOCK)
    s = jnp.einsum('bkgqd,bkqmd->bkgqm', qh, k_sel).astype(jnp.float32) * scale
    p_slc = masked_softmax(s, (pos_sel <= q_pos[:, None])[:, :, None])
    o_slc = jnp.einsum('bkgqm,bkqmd->bkgqd', p_slc.astype(v_sel.dtype), v_sel)
    s = jnp.einsum('bkgqd,blkd->bkgql', qh, kw).astype(jnp.float32) * scale
    dist = q_pos[:, None] - kw_pos[None, :]
    p_win = masked_softmax(s, (dist >= 0) & (dist < WINDOW) & (kw_pos[None, :] >= 0))
    o_win = jnp.einsum('bkgql,blkd->bkgqd', p_win.astype(vw.dtype), vw)
    o = jnp.stack([o_cmp, o_slc, o_win], axis=-1)
    o = o.transpose(0, 3, 1, 2, 4, 5).reshape(b, nq, N_HEADS, HEAD_DIM, N_BRANCH)
    return jnp.einsum('bqhdc,bqhc->bqhd', o, gates.astype(o.dtype))

def short_conv(u, prev, w_conv):
    ext = jnp.concatenate([prev, u], axis=1)
    t = u.shape[1]
    y = sum(ext[:, k:k + t] * w_conv[k] for k in range(CONV_W))
    return y, ext[:, -(CONV_W - 1):]

def mix_out(o_attn, conv_y, attn_out_g, conv_out_g, w_o):
    b, t = conv_y.shape[:2]
    a = rmsnorm(o_attn.reshape(b, t, D_ATTN), attn_out_g)
    v = rmsnorm(conv_y, conv_out_g)
    return jnp.concatenate([a, v], axis=-1) @ w_o

def swiglu(h, w_gu, w_down):
    g, u = jnp.split(h @ w_gu, 2, axis=-1)
    return (jax.nn.silu(g) * u) @ w_down

def gather_past(pool, page_table, new_rows):
    b = page_table.shape[0]
    old = pool[page_table].reshape(b, -1, N_KV_HEADS, HEAD_DIM)
    return jnp.concatenate([old, new_rows], axis=1)

def setup_inputs(seed: int = 0) -> dict:
    key = jax.random.key(seed)
    k = jax.random.split(key, 32)
    n_pages = PAST_LEN // PAGE_SIZE
    n_pool = (5 * DEC_BATCH * n_pages + 3) // 4
    w_buf = min(WINDOW, PAST_LEN)

    def nrm(kk, shape, s=1.0):
        return jax.random.normal(kk, shape, jnp.float32) * s

    def gain(kk, shape):
        return 1.0 + 0.02 * jax.random.normal(kk, shape, jnp.float32)

    page_table = jax.random.permutation(k[0], n_pool)[:DEC_BATCH * n_pages].reshape(DEC_BATCH, n_pages).astype(jnp.int32)
    pool = (DEPTH, n_pool, PAGE_SIZE, N_KV_HEADS, HEAD_DIM)
    return {
        'x_prompt': nrm(k[1], (BATCH, SEQ, D_MODEL)),
        'x_sample': nrm(k[2], (DEC_BATCH, DEC_SEQ, D_MODEL)),
        'cache_k_cmp': nrm(k[3], pool),
        'cache_v_cmp': nrm(k[4], pool),
        'cache_k_slc': nrm(k[5], pool),
        'cache_v_slc': nrm(k[6], pool),
        'state_k_win': nrm(k[7], (DEPTH, DEC_BATCH, w_buf, N_KV_HEADS, HEAD_DIM)),
        'state_v_win': nrm(k[8], (DEPTH, DEC_BATCH, w_buf, N_KV_HEADS, HEAD_DIM)),
        'state_conv': nrm(k[9], (DEPTH, DEC_BATCH, CONV_W - 1, D_CONV)),
        'page_table': page_table,
        'c_prompt': nrm(k[10], (BATCH, D_MODEL)),
        'c_sample': nrm(k[11], (DEC_BATCH, D_MODEL)),
        'w_ada': nrm(k[12], (DEPTH, D_MODEL, 6 * D_MODEL), 0.5 * D_MODEL ** -0.5),
        'b_ada': nrm(k[13], (DEPTH, 6 * D_MODEL), 0.01),
        'ln1_g': gain(k[14], (DEPTH, D_MODEL)),
        'w_in': nrm(k[15], (DEPTH, D_MODEL, N_IN), D_MODEL ** -0.5),
        'q_norm_g': gain(k[16], (DEPTH, HEAD_DIM)),
        'k_norm_g': gain(k[17], (DEPTH, N_BRANCH, HEAD_DIM)),
        'pe_cmp': nrm(k[18], (DEPTH, CMP_LEN, HEAD_DIM), 0.1),
        'w_ck1': nrm(k[19], (DEPTH, CMP_LEN * HEAD_DIM, CMP_HIDDEN), (CMP_LEN * HEAD_DIM) ** -0.5),
        'w_ck2': nrm(k[20], (DEPTH, CMP_HIDDEN, HEAD_DIM), CMP_HIDDEN ** -0.5),
        'w_cv1': nrm(k[21], (DEPTH, CMP_LEN * HEAD_DIM, CMP_HIDDEN), (CMP_LEN * HEAD_DIM) ** -0.5),
        'w_cv2': nrm(k[22], (DEPTH, CMP_HIDDEN, HEAD_DIM), CMP_HIDDEN ** -0.5),
        'w_conv': nrm(k[23], (DEPTH, CONV_W, D_CONV), CONV_W ** -0.5),
        'attn_out_g': gain(k[24], (DEPTH, D_ATTN)),
        'conv_out_g': gain(k[25], (DEPTH, D_CONV)),
        'w_o': nrm(k[26], (DEPTH, D_MIX, D_MODEL), D_MIX ** -0.5),
        'ln2_g': gain(k[27], (DEPTH, D_MODEL)),
        'w_gu': nrm(k[28], (DEPTH, D_MODEL, 2 * D_FF), D_MODEL ** -0.5),
        'w_down': nrm(k[29], (DEPTH, D_FF, D_MODEL), D_FF ** -0.5),
    }

def reference(x_prompt, x_sample, cache_k_cmp, cache_v_cmp, cache_k_slc, cache_v_slc, state_k_win, state_v_win,
              state_conv, page_table, c_prompt, c_sample, w_ada, b_ada, ln1_g, w_in, q_norm_g, k_norm_g, pe_cmp,
              w_ck1, w_ck2, w_cv1, w_cv2, w_conv, attn_out_g, conv_out_g, w_o, ln2_g, w_gu, w_down):
    bp, tp = x_prompt.shape[:2]
    ts = x_sample.shape[1]
    past = page_table.shape[1] * cache_k_cmp.shape[2]
    wbuf = state_k_win.shape[2]
    pos_p = jnp.arange(tp)
    pos_s = past + jnp.arange(ts)
    xp, xs = x_prompt, x_sample
    per_layer = []
    for l in range(DEPTH):
        sh1, sc1, g1, sh2, sc2, g2 = adaln(c_prompt, w_ada[l], b_ada[l])
        q, kc_r, vc_r, ks, vs, kw, vw, gates, u, bg = project(modulate(xp, ln1_g[l], sh1, sc1), pos_p,
                                                              w_in[l], q_norm_g[l], k_norm_g[l])
        kc, vc, kc_end = compressed_tokens(kc_r, vc_r, k_norm_g[l, 0], pe_cmp[l], w_ck1[l], w_ck2[l], w_cv1[l], w_cv2[l])
        ksb, vsb = to_blocks(ks), to_blocks(vs)
        kwp = jnp.pad(kw, ((0, 0), (WINDOW, 0), (0, 0), (0, 0)))
        vwp = jnp.pad(vw, ((0, 0), (WINDOW, 0), (0, 0), (0, 0)))

        def prompt_block(s0):
            qc = lax.dynamic_slice_in_dim(q, s0, Q_BLOCK, 1)
            gc = lax.dynamic_slice_in_dim(gates, s0, Q_BLOCK, 1)
            kwc = lax.dynamic_slice_in_dim(kwp, s0, WINDOW + Q_BLOCK, 1)
            vwc = lax.dynamic_slice_in_dim(vwp, s0, WINDOW + Q_BLOCK, 1)
            q_pos = s0 + jnp.arange(Q_BLOCK)
            kw_pos = s0 - WINDOW + jnp.arange(WINDOW + Q_BLOCK)
            return nsa_attend(qc, q_pos, kc, vc, kc_end, ksb, vsb, kwc, vwc, kw_pos, gc)

        o = lax.map(prompt_block, jnp.arange(0, tp, Q_BLOCK))
        o = o.transpose(1, 0, 2, 3, 4).reshape(bp, tp, N_HEADS, HEAD_DIM)
        cy, p_conv_l = short_conv(u, jnp.zeros((bp, CONV_W - 1, D_CONV), u.dtype), w_conv[l])
        xp = xp + g1 * mix_out(o, bg * cy, attn_out_g[l], conv_out_g[l], w_o[l])
        xp = xp + g2 * swiglu(modulate(xp, ln2_g[l], sh2, sc2), w_gu[l], w_down[l])
        pw = min(WINDOW, tp)
        prompt_state = (kc_r, vc_r, ks, vs, kw[:, tp - pw:], vw[:, tp - pw:], p_conv_l)

        sh1, sc1, g1, sh2, sc2, g2 = adaln(c_sample, w_ada[l], b_ada[l])
        q, kc_r, vc_r, ks, vs, kw, vw, gates, u, bg = project(modulate(xs, ln1_g[l], sh1, sc1), pos_s,
                                                              w_in[l], q_norm_g[l], k_norm_g[l])
        kc, vc, kc_end = compressed_tokens(gather_past(cache_k_cmp[l], page_table, kc_r),
                                           gather_past(cache_v_cmp[l], page_table, vc_r),
                                           k_norm_g[l, 0], pe_cmp[l], w_ck1[l], w_ck2[l], w_cv1[l], w_cv2[l])
        ksb = to_blocks(gather_past(cache_k_slc[l], page_table, ks))
        vsb = to_blocks(gather_past(cache_v_slc[l], page_table, vs))
        kw_all = jnp.concatenate([state_k_win[l], kw], axis=1)
        vw_all = jnp.concatenate([state_v_win[l], vw], axis=1)
        kw_pos = past - wbuf + jnp.arange(wbuf + ts)
        o = nsa_attend(q, pos_s, kc, vc, kc_end, ksb, vsb, kw_all, vw_all, kw_pos, gates)
        cy, s_conv_l = short_conv(u, state_conv[l], w_conv[l])
        xs = xs + g1 * mix_out(o, bg * cy, attn_out_g[l], conv_out_g[l], w_o[l])
        xs = xs + g2 * swiglu(modulate(xs, ln2_g[l], sh2, sc2), w_gu[l], w_down[l])
        sample_state = (kc_r, vc_r, ks, vs, kw_all[:, ts:], vw_all[:, ts:], s_conv_l)
        per_layer.append(prompt_state + sample_state)

    (p_k_cmp, p_v_cmp, p_k_slc, p_v_slc, p_k_win, p_v_win, p_conv,
     s_k_cmp, s_v_cmp, s_k_slc, s_v_slc, s_k_win, s_v_win, s_conv) = [jnp.stack(z) for z in zip(*per_layer)]
    return (xp, xs, p_k_cmp, p_v_cmp, p_k_slc, p_v_slc, p_k_win, p_v_win, p_conv,
            s_k_cmp, s_v_cmp, s_k_slc, s_v_slc, s_k_win, s_v_win, s_conv)


_drawn_inputs = setup_inputs


def setup_inputs(seed=0):
    import zlib

    import numpy as np

    out = dict(_drawn_inputs(seed))
    spreads = {}
    factors = {'b_ada': 3.031,
     'q_norm_g': 6.967,
     'k_norm_g': 3.054,
     'attn_out_g': 8.0,
     'conv_out_g': 8.0,
     'ln2_g': 8.0}
    for name, (base, spread) in spreads.items():
        noise = np.random.default_rng([zlib.crc32(name.encode()), seed]).standard_normal(out[name].shape)
        drawn = base * np.exp(spread * noise) if base else spread * noise
        out[name] = __import__('jax').numpy.asarray(drawn.astype(out[name].dtype))
    for name, factor in factors.items():
        out[name] = (out[name] * factor).astype(out[name].dtype)
    return out
```

```python
from contextlib import ExitStack

import concourse.bass as bass
import numpy as np
from concourse import mybir

ALU = mybir.AluOpType
ACT = mybir.ActivationFunctionType
AX = mybir.AxisListType.X
F32 = mybir.dt.float32
I32 = mybir.dt.int32
U32 = mybir.dt.uint32

D = 1024
SEQ, NB, NQ = 512, 8, 8
TS = NB * NQ
TOK = SEQ + TS
HALF = TOK // 2
HD, NH, NKV, G = 64, 8, 2, 4
KV = NKV * HD
PAST = 2048
CH = PAST // 16
NC = CH - 1
PCH = SEQ // 16
PNC = PCH - 1
NF = 2816
NFT = NF // 128
NC1 = 30
NSEL_FREE = 13
EPS = 1e-6
NEG = -1e30
QS = HD ** -0.5
WR = 4
CR = 4
TM = [128, 128, 128, 128, TS]
TQ, TKC, TVC, TKS, TVS, TKW, TVW, TG, TEND = 0, 512, 640, 768, 896, 1024, 1152, 1280, 1304

C_ID, C_ROPE, C_ROPEC, C_CAUS, C_CMB, C_CM01, C_NEW, C_WIN, C_OVL, C_TRI, C_SEL, C_ONE, C_P8, C_END = np.cumsum(
    [0, 128, 80, 16, 512, 124, 124, 256, 512, 32, 900, 192, 128, 1]).tolist()


def constants():
    c = np.zeros((128, C_END), np.float32)
    p = np.arange(128)
    c[:, C_ID:C_ID + 128] = np.eye(128)
    inv = np.float32(500000.0) ** (-np.arange(8, dtype=np.float32) * np.float32(2.0) / np.float32(16))

    def cs(pos):
        ang = pos.astype(np.float32)[:, None] * inv[None, :]
        return np.concatenate([np.cos(ang), np.sin(ang)], 1)

    for t in range(5):
        c[:, C_ROPE + 16 * t:C_ROPE + 16 * t + 16] = cs(t * 128 + p if t < 4 else PAST + p % NQ)
    c[:, C_ROPEC:C_ROPEC + 16] = cs(p * 16 + 31)
    c[:, C_CAUS + 384:C_CAUS + 512] = np.where(p[None, :] <= p[:, None], 0, NEG)
    n = np.arange(PNC)
    for t in range(4):
        ok = n[None, :] * 16 + 31 <= (t * 128 + p)[:, None]
        c[:, C_CMB + PNC * t:C_CMB + PNC * (t + 1)] = np.where(ok, 0, NEG)
        c[:, C_CM01 + PNC * t:C_CM01 + PNC * (t + 1)] = ok
    b2, q = p // 64, p % 8
    k = np.arange(TS)
    for gp in range(4):
        ok = (k[None, :] // 8 == (2 * gp + b2)[:, None]) & (k[None, :] % 8 <= q[:, None])
        c[:, C_NEW + 64 * gp:C_NEW + 64 * gp + 64] = np.where(ok, 0, NEG)
    i = np.arange(512)
    c[:, C_WIN:C_WIN + 512] = np.where((4 * (i % 128) + i // 128)[None, :] > q[:, None], 0, NEG)
    j = np.arange(32)
    c[:, C_OVL:C_OVL + 32] = (p[:, None] * 16 < (j[None, :] + 1) * 64) & (p[:, None] * 16 + 32 > j[None, :] * 64)
    t30 = np.arange(NC1)
    c[:, C_TRI:C_TRI + 900] = (t30[None, :] < t30[:, None]).reshape(1, 900)
    c[0, C_SEL:C_SEL + 128] = 1
    c[1 + np.arange(TS) // 8, C_SEL + 128 + np.arange(TS)] = 1
    c[:, C_ONE:C_ONE + 128] = 1
    c[:, C_P8] = p % 8
    return c


def plan_banks():
    ring, wide = [], []
    ring += [("rows",), ("cT",), ("sconv",)]
    ring += [("xT", t, h) for t in range(5) for h in range(2)]
    ring += [("peb", x) for x in range(2)]
    for n in range(12):
        ring.append(("ada", n))
        if n == 3:
            ring.append(("mod", 0))
    ring.append(("mod", 1))
    ring += [("in", n, t) for n in range(3) for t in range(5)]
    ring += [("cv", n, m, h) for n in range(3) for m in range(4) for h in range(2)]
    ring += [("ulast",), ("yss", 0), ("yss", 1)]
    for u in range(19):
        if u < 18:
            ring += [("xt", u, i) for i in range(4)]
        if u:
            ring.append(("cmp", u - 1))
        if u < 18:
            ring.append(("pre", u))
    ring += [("kct", i) for i in range(3)]
    ring += [("qT", g, s) for g in range(4) for s in range(2)]
    ring += [("kT", x) for x in range(2)] + [("kTn",)]
    for gp in range(4):
        ring += [("cS", gp), ("cPT", gp), ("imp", gp)]
        wide.append(("cO", gp))
    for gp in range(4):
        for c in range(5):
            ring += [("T", gp, c, b) for b in range(2)]
            if c:
                ring.append(("S", gp, c - 1))
        ring += [("S", gp, 4), ("Sn", gp)]
        ring += [("PT", gp, i) for i in range(6)]
        wide += [("O", gp, 0), ("O", gp, 1)]
    for t in range(4):
        ring += [("pcS", t, 0), ("pcS", t, 1), ("pcPT", t, 0), ("pcPT", t, 1)]
        wide.append(("pO", t, 0))
        for br in range(2):
            wide.append(("pO", t, 1 + br))
            for i in range(NH + 1):
                if i < NH:
                    ring.append(("pS", t, br, i))
                if i:
                    ring.append(("pPT", t, br, i - 1))
    ring += [("oT", t) for t in range(5)]
    ring += [("gate", 0, n, s) for n in range(2) for s in range(2)]
    ring += [("wo", n, t) for n in range(2) for t in range(5)]
    ring += [("hT", t, h) for t in range(5) for h in range(2)]
    ring += [("gate", 1, n, s) for n in range(2) for s in range(2)]
    ring += [("gu", i, x, h) for i in range(NFT) for x in range(2) for h in range(2)]
    ring += [("dn", n, t) for n in range(2) for t in range(5)]
    at = {k: (i % 6, i // 6) for i, k in enumerate(ring)}
    at.update({k: (6 + i % 2, i // 2) for i, k in enumerate(wide)})
    return at


def plan_weights():
    c = [(("ada", n, kh), ("ada", n)) for n in range(12) for kh in range(2)]
    c += [(("in", n, kh), ("in", n, 4)) for n in range(3) for kh in range(2)]
    c += [(("cv", n, kh), ("cv", n, 3, 1)) for n in range(3) for kh in range(2)]
    c += [(("wo", n, kh), ("wo", n, 4)) for n in range(2) for kh in range(2)]
    c += [(("gu", n, kh), ("gu", 2 * n + 1, 1, 1)) for n in range(NFT // 2) for kh in range(2)]
    c += [(("dn", n, kc), None) for n in range(2) for kc in range(6)]
    return c


def decoder_kernel(nc, a, o):
    at = plan_banks()
    chunks = plan_weights()
    chunk_of = {k: i for i, (k, _) in enumerate(chunks)}

    with ExitStack() as ctx:
        def sb(name, cols, dt=F32, parts=128):
            return ctx.enter_context(nc.sbuf_tensor(name, [parts, cols], dt))

        def sem(name):
            return ctx.enter_context(nc.semaphore(name))

        bank = [ctx.enter_context(nc.psum_tensor(f"bank{i}", [128, 512], F32)) for i in range(8)]
        bank_filled = [sem(f"bank_filled{i}") for i in range(8)]
        bank_free = [sem(f"bank_free{i}") for i in range(8)]

        cst = sb("cst", C_END)
        hbuf = sb("hbuf", 8 * TOK)
        hT = hbuf[:, :].rearrange("p (k n) -> p k n", k=8)
        xcmp = hbuf[:, 0:4096].rearrange("p (u j k c) -> p u j k c", u=2, j=8, k=2)
        kTc = hbuf[:, 0:2048].rearrange("p (b s n) -> p b s n", b=2, s=2)
        pT = hbuf[:, 2048:4096].rearrange("p (s n) -> p s n", s=16)
        pTn = hbuf[0:TS, 4096:4352].rearrange("p (x n) -> p x n", x=2)
        ppT = hbuf[:, 0:1024].rearrange("p (s k n) -> p s k n", s=2, k=4)
        ppTc = hbuf[0:PNC, 1024:2048].rearrange("p (h n) -> p h n", h=8)
        proj = sb("proj", 5 * TEND)
        pj = proj[:, :].rearrange("p (t n) -> p t n", t=5)
        xs = proj[:, 0:5 * D].rearrange("p (t n) -> p t n", t=5)
        wring = sb("wring", WR * 2048)
        wch = wring[:, :].rearrange("p (r k n) -> p r k n", r=WR, k=4)
        arena = sb("arena", NFT * TOK)
        actT = arena[:, :].rearrange("p (i n) -> p i n", i=NFT)
        cring = arena[:, 0:CR * 2048].rearrange("p (r n) -> p r n", r=CR)
        xin = arena[:, 0:5 * D].rearrange("p (t n) -> p t n", t=5)
        xnb = arena[:, 5 * D:7 * D].rearrange("p (s n) -> p s n", s=2)
        late = arena[:, CR * 2048:NFT * TOK]
        hcT = late[:, 0:4 * TOK].rearrange("p (f n) -> p f n", f=4)
        yrs = late[:, 4 * TOK:5 * TOK]
        modss = late[0:9, 0:4096]
        sqb = late[:, 0:2048]
        ropb = late[:, 2048:3072]
        ssb, wsb = late[:, 0:2112], late[:, 2112:2688]
        csb, ctb, rk1, rk2 = late[:, 0:NC], late[0:NC, 128:256], late[:, 256:1156], late[:, 1156:2056]
        cpg = late[0:NC, 2056:2088].rearrange("p (a q) -> p a q", a=4)
        cpx = late[0:NC, 3072:3200]
        pTw = late[:, 2688:3200].rearrange("p (s n) -> p s n", s=4)
        psb = late[:, 2688:3712].rearrange("p (s n) -> p s n", s=2)
        x1t = late[:, 2688:3712].rearrange("p (s n) -> p s n", s=2)
        osm = late[0:TS, 0:1536].rearrange("p (h c n) -> p h c n", h=8, c=3)
        otmp = late[:, 1536:2048]
        ulr = late[0:18, 3800:4312]
        uvT = sb("uvT", 4 * TOK)
        uT = uvT[:, :].rearrange("p (f n) -> p f n", f=4)
        oT = uT
        crow, scrow = uvT[0:9, 0:D], uvT[0:9, D:2 * D]
        sgb = uvT[:, 0:2 * TOK].rearrange("p (s n) -> p s n", s=2)
        yt = uvT[:, 2 * TOK:2 * TOK + 1024].rearrange("p (s n) -> p s n", s=2)
        vTt = sb("vTt", 4 * TOK)
        vT = vTt[:, :].rearrange("p (f n) -> p f n", f=4)
        stc = vTt[0:16, 0:512]
        att = sb("att", 7168)
        w1v = att[:, 0:2048].rearrange("p (x j r h) -> p x j r h", x=2, j=8, r=2)
        qTp = att[:, 0:2048].rearrange("p (g n) -> p g n", g=4)
        gbc = att[:, 0:2048].rearrange("p (s n) -> p s n", s=2)
        qblk = att[:, 2048:2560]
        kTp = att[:, 2560:3584].rearrange("p (x n) -> p x n", x=2)
        kTn = att[:, 3584:3712].rearrange("p (x n) -> p x n", x=2)
        kcm = att[:, 3712:4864].rearrange("p (b n) -> p b n", b=9)
        vcm = att[:, 4864:6016].rearrange("p (b n) -> p b n", b=9)
        kcT = att[:, 6016:7168].rearrange("p (b n) -> p b n", b=9)
        grow = sb("grow", 2048, parts=9)
        rowb = sb("rowb", 128, parts=52)
        winb = sb("winb", 2048)
        wnd = winb[:, :].rearrange("p (x b n) -> p x b n", x=2, b=2)
        w2 = sb("w2", 128, parts=64)
        colT = sb("colT", 52)
        cT = sb("cT", 72)
        stT = sb("stT", 64)
        modt = sb("modt", 288)
        mod = modt[:, :].rearrange("p (l x k b) -> p l x k b", l=2, x=2, k=8)
        gains = sb("gains", 256)
        ulast = sb("ulast", 72)
        gat = sb("gat", 120)
        gate = gat[:, :].rearrange("p (t h c) -> p t h c", t=5, h=8)
        small = sb("small", 256)
        selb = sb("selb", 512)
        sel32 = sb("sel32", 32)
        imps = sb("imps", NC1)
        slv = late[0:64, 3072:3584]
        half = slv[:, 0:2 * NC].rearrange("p (k n) -> p k n", k=2)
        slu = slv[:, 256:256 + 2 * NC].rearrange("p (k n) -> p k n", k=2)
        orows = uvT[:, 0:4 * 192]
        orow = orows[:, :].rearrange("p (g c n) -> p g c n", g=4, c=3)
        pti = sb("pti", 8, I32)
        idx = sb("idx", 8, U32)
        pebt = sb("pebt", 2, parts=64)
        pct = sb("pct", 8 * PNC)
        pcp = pct[:, :].rearrange("p (h n) -> p h n", h=8)
        epst = sb("epst", 1)
        ident = cst[:, C_ID:C_ID + 128]
        o_rows = nc.dram_tensor("o_rows", [NB, NH, NQ, 192], F32).ap()

        consts_loaded, gains_loaded, c_loaded, comp_w_loaded, bias_loaded, conv_state_loaded, pages_loaded = (
            sem(n) for n in ("consts_loaded", "gains_loaded", "c_loaded", "comp_w_loaded", "bias_loaded",
                             "conv_state_loaded", "pages_loaded"))
        x_loaded = [sem(f"x_loaded{t}") for t in range(5)]
        w_loaded = [sem(f"w_loaded{i}") for i in range(WR)]
        cache_loaded = [sem(f"cache_loaded{i}") for i in range(CR)]
        win_loaded, xin_loaded, rows_back, rows_out, stored, kvc_stored = (
            sem(n) for n in ("win_loaded", "xin_loaded", "rows_back", "rows_out", "stored", "kvc_stored"))
        dve_step, act_step = sem("dve_step"), sem("act_step")
        (cleared, scrow_ready, x_square, x_root, xn_ready, idx_ready, hT_ready, u_end_ready, y_ready, y_square, y_inv,
         vT_ready, v_scaled, half_ready, pre_ready, silu_ready, nrm_square, nrm_root, nrm_done, gate_exp, gates_ready,
         c_exp, c_prob, c_group, sel_ready, s_min, s_exp, o_row, p_in, p_exp, p_prob, p_soft, attn_ready, a_square,
         a_root, a_ready, x1_ready, x1_square, x1_root, x1n_ready, dn_read, out_ready) = (sem(n) for n in (
            "cleared scrow_ready x_square x_root xn_ready idx_ready hT_ready u_end_ready y_ready y_square y_inv "
            "vT_ready v_scaled half_ready pre_ready silu_ready nrm_square nrm_root nrm_done gate_exp gates_ready "
            "c_exp c_prob c_group sel_ready s_min s_exp o_row p_in p_exp p_prob p_soft attn_ready a_square "
            "a_root a_ready x1_ready x1_square x1_root x1n_ready dn_read out_ready").split())

        def ps(key):
            return bank[at[key][0]]

        def want_free(eng, key):
            b, n = at[key]
            if n:
                eng.wait_ge(bank_free[b], n)

        def want_filled(eng, key):
            b, n = at[key]
            eng.wait_ge(bank_filled[b], n + 1)

        def want_emptied(eng, key):
            b, n = at[key]
            eng.wait_ge(bank_free[b], n + 1)

        def fills(ins, key):
            ins.then_inc(bank_filled[at[key][0]], 1)

        def frees(ins, key):
            ins.then_inc(bank_free[at[key][0]], 1)

        def loads_of(i):
            return 32 if chunks[i][0][0] == "gu" else 16

        def weights(pe, key):
            i = chunk_of[key]
            pe.wait_ge(w_loaded[i % WR], sum(loads_of(j) for j in range(i % WR, i + 1, WR)))
            return wch[:, i % WR]

        caches = [(("cache_k_cmp", "cache_v_cmp")[u % 2], u // 2, ("xt", u, 3)) for u in range(16)]
        caches += [("p_k_cmp", None, ("xt", 16, 3)), ("p_v_cmp", None, ("xt", 17, 3))]
        for gp in range(4):
            caches += [("cache_k_slc", 2 * gp + b, ("T", gp, 3, b)) for b in range(2)]
            caches += [("cache_v_slc", 2 * gp + b, ("O", gp, 0)) for b in range(2)]

        def cache(eng, i):
            eng.wait_ge(cache_loaded[i % CR], 16 * (i // CR + 1))
            return cring[:, i % CR, :].rearrange("p (s n) -> p s n", s=16)

        def tok_rows(name_p, name_s, t):
            return a[name_p][0, 128 * t:128 * t + 128, :] if t < 4 else a[name_s].rearrange("b q d -> (b q) d")

        def out_rows(name):
            return o[name].rearrange("l b (t p) k d -> p (l b t) (k d)", p=128)

        block = ctx.enter_context(nc.Block())

        @block.sync
        def _(sp):
            for t in range(5):
                sp.dma_start(xs[0:TM[t], t, :], tok_rows("x_prompt", "x_sample", t)).then_inc(x_loaded[t], 16)
            for dst, c0, w in ((modss[:, 0:2048], 0, 2048), (modss[:, 2048:4096], 3 * D, 2048),
                               (grow[:, 0:D], 2 * D, D), (grow[:, D:2 * D], 5 * D, D)):
                sp.dma_start(dst, a["b_ada"][0:1, c0:c0 + w].to_broadcast([9, w])).then_inc(bias_loaded, 16)

            def load(i):
                if i >= WR:
                    (kind, n, kh), last = chunks[i - WR]
                    if last is None:
                        sp.wait_ge(dn_read, 5 * n + kh + 1)
                    else:
                        want_filled(sp, last)
                (kind, n, kh), _ = chunks[i]
                dst, k0, nk, w = wch[:, i % WR], 512 * kh, 4, 512
                if kind == "gu":
                    for x in range(2):
                        c0 = x * NF + 256 * n
                        sp.dma_start(dst[:, :, 256 * x:256 * x + 256],
                                     a["w_gu"][0, k0:k0 + 512, c0:c0 + 256].rearrange("(k p) n -> p k n", p=128)
                                     ).then_inc(w_loaded[i % WR], 16)
                    return
                src, c0 = a[{"ada": "w_ada", "in": "w_in", "cv": "w_in", "wo": "w_o", "dn": "w_down"}[kind]], 512 * n
                if kind == "in":
                    w = min(512, TEND - c0)
                if kind == "cv":
                    c0 = TEND + 512 * (0, 2, 1)[n]
                if kind == "dn" and kh == 5:
                    nk = NFT - 20
                sp.dma_start(dst[:, 0:nk, 0:w],
                             src[0, k0:k0 + 128 * nk, c0:c0 + w].rearrange("(k p) n -> p k n", p=128)
                             ).then_inc(w_loaded[i % WR], 16)

            done = chunk_of["wo", 0, 0]
            for i in range(done):
                load(i)
            count = 0

            def store(dst, src):
                sp.dma_start(dst, src).then_inc(stored, 16)
                return 1

            for t in range(5):
                want_emptied(sp, ("in", 1, t))
            for c0, name in ((TKC, "p_k_cmp"), (TVC, "p_v_cmp")):
                sp.dma_start(out_rows(name), pj[:, 0:4, c0:c0 + 128]).then_inc(kvc_stored, 16)
            for c0, name in ((TKC, "s_k_cmp"), (TVC, "s_v_cmp"), (TVS, "s_v_slc")):
                count += store(o[name].rearrange("l b q k d -> (l b q) (k d)"), pj[0:TS, 4, c0:c0 + 128])
            count += store(out_rows("p_v_slc"), pj[:, 0:4, TVS:TVS + 128])
            for t in range(5):
                want_emptied(sp, ("in", 2, t))
            count += store(out_rows("p_v_win"), pj[:, 0:4, TVW:TVW + 128])
            for w in ("k", "v"):
                count += store(o[f"s_{w}_win"][0, :, 0:SEQ - NQ].rearrange("b t k d -> b (t k d)"),
                               a[f"state_{w}_win"][0, :, NQ:SEQ].rearrange("b t k d -> b (t k d)"))
            for b in range(NB):
                count += store(o["s_v_win"][0, b, SEQ - NQ:SEQ].rearrange("q k d -> q (k d)"),
                               pj[NQ * b:NQ * b + NQ, 4, TVW:TVW + 128])
            sp.wait_ge(nrm_done, 6)
            for c0, name in ((TKS, "p_k_slc"), (TKW, "p_k_win")):
                count += store(out_rows(name), pj[:, 0:4, c0:c0 + 128])
            count += store(o["s_k_slc"].rearrange("l b q k d -> (l b q) (k d)"), pj[0:TS, 4, TKS:TKS + 128])
            for b in range(NB):
                count += store(o["s_k_win"][0, b, SEQ - NQ:SEQ].rearrange("q k d -> q (k d)"),
                               pj[NQ * b:NQ * b + NQ, 4, TKW:TKW + 128])
            want_emptied(sp, ("ulast",))
            count += store(o["p_conv"].rearrange("l b r f -> (l b r) f"), ulr[0:2, :])
            count += store(o["s_conv"].rearrange("l b r f -> (l b r) f"), ulr[2:18, :])
            assert count == N_STORED
            for i in range(done, done + WR):
                load(i)
            for gp in range(4):
                sp.wait_ge(o_row, gp + 1)
                sp.dma_start(o_rows[2 * gp:2 * gp + 2].rearrange("b h q n -> (b h q) n"),
                             orows[:, 192 * gp:192 * gp + 192]).then_inc(rows_out, 16)
            sp.wait_ge(rows_out, 64)
            for b in range(NB):
                sp.dma_start(late[NQ * b:NQ * b + NQ, 0:1536].rearrange("q (h n) -> q h n", h=8),
                             o_rows[b].rearrange("h q n -> q h n")).then_inc(rows_back, 16)
            want_filled(sp, ("O", 3, 1))
            for t in range(5):
                sp.dma_start(xin[0:TM[t], t, :], tok_rows("x_prompt", "x_sample", t)).then_inc(xin_loaded, 16)
            for i in range(done + WR, len(chunks)):
                load(i)
            for n in range(2):
                for t in range(5):
                    sp.wait_ge(out_ready, 5 * n + t + 1)
                    dst = o["y_prompt"][0, 128 * t:128 * t + 128, :] if t < 4 else o["y_sample"].rearrange("b q d -> (b q) d")
                    count += store(dst[:, 512 * n:512 * n + 512], xs[0:TM[t], t, 512 * n:512 * n + 512])
            sp.wait_ge(kvc_stored, 32)
            sp.wait_ge(stored, 16 * count)

        @block.gpsimd
        def _(pool):
            for b in range(NB):
                pt = a["page_table"]
                pool.dma_start(pti[:, b:b + 1], bass.AP(pt.tensor, 16 * b, [[1, 16], [0, 8], [1, 1]])).then_inc(pages_loaded, 16)
            pool.wait_ge(idx_ready, 1)
            loaded = 0

            def window(gp):
                for x, w in enumerate("kv"):
                    if gp:
                        want_filled(pool, ("O", gp - 1, 1))
                    for b in range(2):
                        pool.dma_start(wnd[:, x, b, :], a[f"state_{w}_win"][0, 2 * gp + b].rearrange("(c s) k d -> c (s k d)", s=4)
                                       ).then_inc(win_loaded, 16)

            for i, (name, b, last) in enumerate(caches):
                if i >= CR:
                    want_filled(pool, caches[i - CR][2])
                slot = cring[:, i % CR, :]
                if b is None:
                    pool.wait_ge(kvc_stored, 32)
                    pool.dma_start(slot[0:PCH, :], o[name].rearrange("l b (c s) k d -> (l b c) (s k d)", s=16)
                                   ).then_inc(cache_loaded[i % CR], 16)
                else:
                    pool.indirect_dma_start(slot, None, a[name].rearrange("l n (c s) k d -> (l n c) (s k d)", s=16),
                                            bass.IndirectOffsetOnAxis(idx[:, b:b + 1], 0)).then_inc(cache_loaded[i % CR], 16)
                if i == 18:
                    window(0)
                if i >= 22 and (i - 22) % 4 == 0:
                    window((i - 18) // 4)

        def spread_chunks(copy, u, i, n):
            key = ("xt", u, i)
            for k in range(2):
                ins = copy(xcmp[64 * (i % 2):64 * (i % 2) + 64, u % 2, 4 * (i // 2):4 * (i // 2) + 4, k, 0:n],
                           ps(key)[64 * k:64 * k + 64, :].rearrange("p (j c) -> p j c", j=4)[:, :, 0:n])
            frees(ins, key)

        def second_half(act, t):
            want_filled(act, ("hT", t, 1))
            for k in range(4, 8):
                ins = act.activation(hT[:, k, 128 * t:128 * t + 128], ps(("hT", t, 1))[:, 128 * (k - 4):128 * (k - 3)],
                                     ACT.Identity, bias=mod[:, 1, 1, k, 0:1], scale=mod[:, 1, 0, k, 0:1])
            frees(ins, ("hT", t, 1))

        @block.scalar
        def _(act):
            steps = [0]

            def link(ins):
                steps[0] += 1
                ins.then_inc(act_step, 1)
                act.wait_ge(act_step, steps[0])

            act.dma_start(cst[:, :], a["consts"]).then_inc(consts_loaded, 16)
            act.dma_start(crow[0:1, :], a["c_prompt"]).then_inc(c_loaded, 16)
            act.dma_start(crow[1:9, :], a["c_sample"]).then_inc(c_loaded, 16)
            r0 = 0
            for name, n in (("ln1_g", 8), ("ln2_g", 8), ("attn_out_g", 4), ("conv_out_g", 4)):
                act.dma_start(rowb[r0:r0 + n, :], a[name].rearrange("l (k p) -> (l k) p", p=128)).then_inc(gains_loaded, 16)
                r0 += n
            act.dma_start(rowb[24:36, :], a["w_conv"].rearrange("l w (k p) -> (l w k) p", p=128)).then_inc(gains_loaded, 16)
            act.dma_start(rowb[36:52, :], a["pe_cmp"].rearrange("l (k s) d -> (l k) (s d)", s=2)).then_inc(gains_loaded, 16)
            act.dma_start(gains[:, 0:64], a["q_norm_g"].to_broadcast([128, 64])).then_inc(gains_loaded, 16)
            for i in range(3):
                act.dma_start(gains[:, 64 + 64 * i:128 + 64 * i], a["k_norm_g"][0, i:i + 1, :].to_broadcast([128, 64])
                              ).then_inc(gains_loaded, 16)
            act.dma_start(stc, a["state_conv"].rearrange("l b r f -> (l b r) f")).then_inc(conv_state_loaded, 16)
            for x, w in enumerate(("w_ck1", "w_cv1")):
                for r in range(2):
                    act.dma_start(w1v[:, x, :, r, :], a[w][0, 1024 * r:1024 * r + 1024, :].rearrange("(j p) h -> p j h", p=128)
                                  ).then_inc(comp_w_loaded, 16)
            for x, w in enumerate(("w_ck2", "w_cv2")):
                act.dma_start(w2[:, 64 * x:64 * x + 64], a[w][0]).then_inc(comp_w_loaded, 16)

            act.wait_ge(c_loaded, 32)
            act.activation(scrow, crow, ACT.Silu).then_inc(scrow_ready, 1)
            act.wait_ge(cleared, 1)
            for t in range(5):
                act.wait_ge(x_loaded[t], 16)
                if t:
                    act.wait_ge(x_square, t)
                act.activation(hbuf[0:TM[t], 0:D], xs[0:TM[t], t, :], ACT.Square, accum_out=small[0:TM[t], t:t + 1]
                               ).then_inc(x_square, 1)
            act.wait_ge(x_square, 5)
            act.activation(small[:, 8:13], small[:, 0:5], ACT.Sqrt, bias=epst[:, 0:1], scale=1.0 / D).then_inc(x_root, 1)
            for t in range(5):
                want_filled(act, ("xT", t, 1))
                frees(act.copy(hT[:, 4:8, 128 * t:128 * t + TM[t]],
                               ps(("xT", t, 1))[:, 0:4 * TM[t]].rearrange("p (k n) -> p k n", k=4)), ("xT", t, 1))
            for n in range(3):
                if n == 1:
                    continue
                w = min(512, TEND - 512 * n)
                for t in range(5):
                    want_filled(act, ("in", n, t))
                    dst, src = pj[0:TM[t], t, 512 * n:512 * n + w], ps(("in", n, t))[0:TM[t], 0:w]
                    if n == 0:
                        dst = dst.rearrange("p (g k d) -> p g k d", g=4, k=2)
                        src = src.rearrange("p (k g d) -> p g k d", k=2, g=4)
                    frees(act.copy(dst, src), ("in", n, t))
            for m in range(4):
                for h in range(2):
                    want_filled(act, ("cv", 0, m, h))
                    frees(act.copy(hcT[:, m, HALF * h:HALF * h + HALF], ps(("cv", 0, m, h))[:, 0:HALF]), ("cv", 0, m, h))
            for m in range(4):
                act.wait_ge(y_ready, m + 1)
                act.activation(hcT[:, m, :], vT[:, m, :], ACT.Square).then_inc(y_square, 1)
            want_filled(act, ("ulast",))
            frees(act.copy(ulr, ps(("ulast",))[0:18, :]), ("ulast",))
            for h in range(2):
                want_filled(act, ("yss", h))
                frees(act.activation(yrs[:, HALF * h:HALF * h + HALF], ps(("yss", h))[:, 0:HALF], ACT.Sqrt,
                                     bias=epst[:, 0:1], scale=1.0 / 512), ("yss", h))

            def nrm(i):
                act.wait_ge(nrm_square, i + 1)
                P, n = NORMS[i][1], NORMS[i][2]
                act.activation(small[0:P, 64:64 + n], small[0:P, 32:32 + n], ACT.Sqrt, bias=epst[0:P, 0:1], scale=1.0 / HD
                               ).then_inc(nrm_root, 1)

            for u in range(18):
                n, m = (CH, NC) if u < 16 else (PCH, PNC)
                for i in (0, 2):
                    if u >= 2:
                        want_filled(act, ("pre", u - 2))
                    want_filled(act, ("xt", u, i))
                    spread_chunks(act.copy, u, i, n)
                if u in NORM_AT:
                    nrm(NORM_AT.index(u))
                want_filled(act, ("pre", u))
                if u:
                    act.wait_ge(silu_ready, u)
                act.copy(half[:, :, 0:m], ps(("pre", u))[64:128, 0:2 * n].rearrange("p (k c) -> p k c", k=2)[:, :, 1:n]
                         ).then_inc(half_ready, 1)
                want_emptied(act, ("pre", u))
                if u:
                    want_filled(act, ("cmp", u - 1))
                x = u % 2
                act.activation(slu[:, :, 0:m], half[:, :, 0:m], ACT.Silu, bias=pebt[:, x:x + 1]).then_inc(silu_ready, 1)
            nrm(6)
            nrm(7)
            act.activation(gat[:, 0:96].rearrange("p (t n) -> p t n", t=4), pj[:, 0:4, TG:TEND], ACT.Exp, scale=-1.0).then_inc(gate_exp, 1)
            act.activation(gat[0:TS, 96:120], pj[0:TS, 4, TG:TEND], ACT.Exp, scale=-1.0).then_inc(gate_exp, 1)
            for i in range(3):
                want_filled(act, ("kct", i))
                nb, m = (4, NC) if i < 2 else (1, PNC)
                frees(act.copy(kcT[:, 4 * i:4 * i + nb, 0:m],
                               ps(("kct", i))[:, :].rearrange("p (b n) -> p b n", b=4)[:, 0:nb, 0:m]), ("kct", i))
            for g in range(G):
                want_filled(act, ("qT", g, 0))
                frees(act.copy(qTp[:, g, :], ps(("qT", g, 0))[:, :]), ("qT", g, 0))
            for x in range(2):
                want_filled(act, ("kT", x))
                frees(act.copy(kTp[:, x, :], ps(("kT", x))[:, :]), ("kT", x))
            for gp in range(4):
                want_emptied(act, ("cS", gp))
                act.activation(csb, csb, ACT.Exp, bias=small[:, 100:101], scale=-1.0, accum_out=small[:, 101:102]).then_inc(c_exp, 1)
                want_filled(act, ("cPT", gp))
                if gp:
                    want_filled(act, ("cO", gp - 1))
                frees(act.copy(ctb, ps(("cPT", gp))[0:NC, 0:128]), ("cPT", gp))
                want_filled(act, ("cO", gp))
                for i in range(4):
                    r = slice(32 * i, 32 * i + 32)
                    ins = act.copy(orow[r, gp, 0, :], ps(("cO", gp))[r, 64 * (i % 2):64 * (i % 2) + 64])
                frees(ins, ("cO", gp))
            for gp in range(4):
                for c in range(5):
                    want_filled(act, ("T", gp, c, 0))
                    if c >= 2:
                        want_filled(act, ("S", gp, c - 2))
                    elif gp:
                        want_filled(act, ("S", gp - 1, c + 3))
                    frees(act.copy(kTc[:, 0, c % 2, :], ps(("T", gp, c, 0))[:, :]), ("T", gp, c, 0))
                act.wait_ge(s_min, gp + 1)
                act.activation(ssb, ssb, ACT.Exp, bias=small[:, 112:113], scale=-1.0, accum_out=small[:, 114:115]).then_inc(s_exp, 1)
                act.activation(wsb, wsb, ACT.Exp, bias=small[:, 113:114], scale=-1.0, accum_out=small[:, 115:116]).then_inc(s_exp, 1)
                for i in (0, 2, 4):
                    want_filled(act, ("PT", gp, i))
                    dst = pTw if i == 4 else pT[:, 4 * i:4 * i + 4, :]
                    frees(act.copy(dst, ps(("PT", gp, i))[:, :].rearrange("p (s n) -> p s n", s=4)), ("PT", gp, i))
            for t in range(4):
                act.wait_ge(p_in, t + 1)
                act.activation(pct[:, :], pct[:, :], ACT.Exp, scale=QS).then_inc(p_exp, 1)
                for hh in range(2):
                    want_filled(act, ("pcPT", t, hh))
                    frees(act.copy(ppTc[:, 4 * hh:4 * hh + 4, :],
                                   ps(("pcPT", t, hh))[0:PNC, :].rearrange("p (h n) -> p h n", h=4)), ("pcPT", t, hh))
                for br in range(2):
                    for i in range(NH + 1):
                        if i < NH:
                            want_emptied(act, ("pS", t, br, i))
                            w = 128 * (t + 1)
                            c0 = 128 + 8 * br + i
                            act.activation(psb[:, i % 2, 0:w], psb[:, i % 2, 0:w], ACT.Exp, bias=small[:, 144 + i:145 + i],
                                           scale=-1.0, accum_out=small[:, c0:c0 + 1]).then_inc(p_soft, 1)
                        if i:
                            want_filled(act, ("pPT", t, br, i - 1))
                            frees(act.copy(ppT[:, (i - 1) % 2, 0:t + 1, :],
                                           ps(("pPT", t, br, i - 1))[:, 0:128 * (t + 1)].rearrange("p (k n) -> p k n", n=128)),
                                  ("pPT", t, br, i - 1))
            for t in range(5):
                act.wait_ge(attn_ready, t + 1)
                if t:
                    act.wait_ge(a_square, t)
                act.activation(psb[0:TM[t], 0, :], pj[0:TM[t], t, 0:512], ACT.Square, accum_out=small[0:TM[t], t:t + 1]
                               ).then_inc(a_square, 1)
            act.wait_ge(a_square, 5)
            act.activation(small[:, 8:13], small[:, 0:5], ACT.Sqrt, bias=epst[:, 0:1], scale=1.0 / 512).then_inc(a_root, 1)

            def gates_rows(l):
                for n in range(2):
                    for s in range(2):
                        P = 128 if s == 0 else TS
                        want_filled(act, ("gate", l, n, s))
                        frees(act.copy(gbc[0:P, s, 512 * n:512 * n + 512], ps(("gate", l, n, s))[0:P, :]), ("gate", l, n, s))

            gates_rows(0)
            for t in range(5):
                act.wait_ge(x1_ready, 5 + t + 1)
                if t:
                    act.wait_ge(x1_square, t)
                act.activation(late[0:TM[t], 0:D], xs[0:TM[t], t, :], ACT.Square, accum_out=small[0:TM[t], 16 + t:17 + t]
                               ).then_inc(x1_square, 1)
                act.wait_ge(x1_square, t + 1)
                act.activation(small[0:TM[t], 24 + t:25 + t], small[0:TM[t], 16 + t:17 + t], ACT.Sqrt,
                               bias=epst[0:TM[t], 0:1], scale=1.0 / D).then_inc(x1_root, 1)
                if t >= 1:
                    second_half(act, t - 1)
            gates_rows(1)
            for i in range(NFT):
                for h in range(2):
                    want_filled(act, ("gu", i, 0, h))
                    if i >= 2:
                        want_emptied(act, ("gu", i - 2, 1, h))
                    frees(act.activation(sgb[:, i % 2, HALF * h:HALF * h + HALF], ps(("gu", i, 0, h))[:, 0:HALF], ACT.Silu),
                          ("gu", i, 0, h))

        @block.vector
        def _(dve):
            steps = [0]

            def link(ins):
                steps[0] += 1
                ins.then_inc(dve_step, 1)
                dve.wait_ge(dve_step, steps[0])

            link(dve.memset(epst[:, :], EPS))
            link(dve.memset(small[:, :], 1.0))
            link(dve.memset(sel32[:, :], 0.0))
            dve.memset(qblk, 0.0).then_inc(cleared, 1)
            dve.wait_ge(cleared, 1)
            dve.wait_ge(consts_loaded, 16)
            dve.wait_ge(pages_loaded, 128)
            dve.scalar_tensor_tensor(idx[:, :], pti[:, :], 8.0, cst[:, C_P8:C_P8 + 1].to_broadcast([128, 8]), ALU.mult, ALU.add
                                     ).then_inc(idx_ready, 1)

            def evac(key, dst, src):
                want_filled(dve, key)
                frees(dve.tensor_copy(dst, src), key)

            evac(("rows",), colT[:, :], ps(("rows",))[:, 0:52])
            evac(("cT",), cT[:, :], ps(("cT",))[:, 0:72])
            evac(("sconv",), stT[:, :], ps(("sconv",))[:, 0:64])
            dve.wait_ge(x_root, 1)
            link(dve.reciprocal(small[:, 16:21], small[:, 8:13]))
            for t in range(5):
                dve.tensor_scalar(xs[0:TM[t], t, :], xs[0:TM[t], t, :], small[0:TM[t], 16 + t:17 + t], None, ALU.mult
                                  ).then_inc(xn_ready, 1)
            for t in range(5):
                evac(("xT", t, 0), hT[:, 0:4, 128 * t:128 * t + TM[t]],
                     ps(("xT", t, 0))[:, 0:4 * TM[t]].rearrange("p (k n) -> p k n", k=4))
            for x in range(2):
                evac(("peb", x), pebt[:, x:x + 1], ps(("peb", x))[0:64, 0:1])

            dve.wait_ge(bias_loaded, 64)

            def mod_cols(l):
                key = ("mod", l)
                want_filled(dve, key)
                v = ps(key)[:, 0:144].rearrange("p (x k b) -> p x k b", x=2, k=8)
                link(dve.tensor_copy(mod[:, l, 1], v[:, 0]))
                frees(dve.scalar_tensor_tensor(mod[:, l, 0], v[:, 1], 1.0,
                                               colT[:, 8 * l:8 * l + 8].unsqueeze(2).to_broadcast([128, 8, 9]),
                                               ALU.add, ALU.mult), key)

            for n in range(12):
                if n < 4:
                    dst = modss[:, 512 * n:512 * n + 512]
                elif n < 6:
                    dst = grow[:, 512 * (n - 4):512 * (n - 3)]
                elif n < 10:
                    dst = modss[:, 2048 + 512 * (n - 6):2048 + 512 * (n - 5)]
                else:
                    dst = grow[:, 1024 + 512 * (n - 10):1024 + 512 * (n - 9)]
                want_filled(dve, ("ada", n))
                frees(dve.tensor_tensor(dst, ps(("ada", n))[0:9, :], dst, ALU.add), ("ada", n))
                if n == 3:
                    mod_cols(0)
                    for t in range(5):
                        want_emptied(dve, ("xT", t, 0))
                        want_emptied(dve, ("xT", t, 1))
                    want_emptied(dve, ("mod", 0))
                    sv = hT[:, :, SEQ:TOK].rearrange("p k (b q) -> p k b q", b=8)
                    link(dve.tensor_tensor(sv, sv, mod[:, 0, 0, :, 1:9].unsqueeze(3).to_broadcast([128, 8, 8, 8]), ALU.mult))
                    link(dve.tensor_tensor(sv, sv, mod[:, 0, 1, :, 1:9].unsqueeze(3).to_broadcast([128, 8, 8, 8]), ALU.add))
                    for k in range(8):
                        dve.tensor_scalar(hT[:, k, 0:SEQ], hT[:, k, 0:SEQ], mod[:, 0, 0, k, 0:1], mod[:, 0, 1, k, 0:1],
                                          ALU.mult, ALU.add).then_inc(hT_ready, 1)
            mod_cols(1)
            for t in range(5):
                evac(("in", 1, t), pj[0:TM[t], t, 512:1024], ps(("in", 1, t))[0:TM[t], :])

            def conv(m):
                w = [colT[:, 24 + 4 * k + m:25 + 4 * k + m] for k in range(3)]
                y, u = vT[:, m, :], uT[:, m, :]
                ys, us = (z[:, SEQ:TOK].rearrange("p (b q) -> p b q", b=8) for z in (y, u))
                st = stT[:, 16 * m:16 * m + 16].rearrange("p (b r) -> p b r", b=8)

                def tap(dst, src, k):
                    link(dve.scalar_tensor_tensor(dst, src, w[k], dst, ALU.mult, ALU.add))

                link(dve.tensor_scalar(y, u, w[2], None, ALU.mult))
                tap(y[:, 1:SEQ], u[:, 0:SEQ - 1], 1)
                tap(y[:, 2:SEQ], u[:, 0:SEQ - 2], 0)
                tap(ys[:, :, 1:8], us[:, :, 0:7], 1)
                tap(ys[:, :, 2:8], us[:, :, 0:6], 0)
                tap(ys[:, :, 0:1], st[:, :, 1:2], 1)
                tap(ys[:, :, 0:2], st, 0)

            for m in range(4):
                for h in range(2):
                    key = ("cv", 1, m, h)
                    want_filled(dve, key)
                    want_emptied(dve, ("cv", 0, m, h))
                    frees(dve.tensor_tensor(uT[:, m, HALF * h:HALF * h + HALF], ps(key)[:, 0:HALF],
                                            hcT[:, m, HALF * h:HALF * h + HALF], ALU.mult), key)
                want_emptied(dve, ("cv", 1, m, 0))
                want_emptied(dve, ("cv", 1, m, 1))
                conv(m)
            ul = ulast[:, :].rearrange("p (m c) -> p m c", m=4)
            link(dve.tensor_copy(ul[:, :, 0:2], uT[:, :, SEQ - 2:SEQ]))
            for m in range(4):
                dve.tensor_copy(ul[:, m, 2:18].rearrange("p (b r) -> p b r", b=8),
                                uT[:, m, SEQ:TOK].rearrange("p (b q) -> p b q", b=8)[:, :, 6:8]).then_inc(u_end_ready, 1)
            for m in range(4):
                for h in range(2):
                    key = ("cv", 2, m, h)
                    want_filled(dve, key)
                    y = vT[:, m, HALF * h:HALF * h + HALF]
                    frees(dve.tensor_tensor(y, ps(key)[:, 0:HALF], y, ALU.mult), key)
                want_emptied(dve, ("cv", 2, m, 1))
                dve.tensor_copy(small[:, 250:251], vT[:, m, 0:1]).then_inc(y_ready, 1)
                dve.wait_ge(y_ready, m + 1)
            want_emptied(dve, ("yss", 0))
            want_emptied(dve, ("yss", 1))
            link(dve.reciprocal(yrs, yrs))
            for m in range(4):
                dve.scalar_tensor_tensor(vT[:, m, :], vT[:, m, :], colT[:, 20 + m:21 + m], yrs, ALU.mult, ALU.mult
                                         ).then_inc(vT_ready, 1)
            dve.wait_ge(vT_ready, 4)

            def norm_rope(i):
                name, P, n, t0, nt, nh, gain = NORMS[i]
                if name == "kcm":
                    for b in range(t0, t0 + nt):
                        want_emptied(dve, ("cmp", 2 * b))
                    v = kcm[0:P, t0:t0 + nt, :]
                else:
                    for t in range(t0, t0 + nt):
                        want_emptied(dve, ("in", {"q": 0, "ks": 1, "kw": 2}[name], t))
                    c0 = {"q": TQ, "ks": TKS, "kw": TKW}[name]
                    v = pj[0:P, t0:t0 + nt, c0:c0 + 64 * nh]
                v = v.rearrange("p t (h d) -> p t h d", h=nh)
                q = sqb[0:P, 0:64 * n].rearrange("p (t h d) -> p t h d", t=nt, h=nh)
                link(dve.tensor_tensor(q, v, v, ALU.mult))
                dve.tensor_reduce(small[0:P, 32:32 + n], q, AX, ALU.add).then_inc(nrm_square, 1)
                dve.wait_ge(nrm_root, i + 1)
                link(dve.reciprocal(small[0:P, 32:32 + n], small[0:P, 64:64 + n]))
                rs = small[0:P, 32:32 + n].rearrange("p (t h) -> p t h", t=nt).unsqueeze(3).to_broadcast([P, nt, nh, 64])
                link(dve.tensor_tensor(v, v, rs, ALU.mult))
                gn = gains[0:P, 64 * gain:64 * gain + 64].unsqueeze(1).unsqueeze(1).to_broadcast([P, nt, nh, 64])
                link(dve.tensor_tensor(v, v, gn, ALU.mult))
                if name == "kcm":
                    cs = cst[0:P, C_ROPEC:C_ROPEC + 16].unsqueeze(1).to_broadcast([P, nt, 16])
                else:
                    cs = cst[0:P, C_ROPE + 16 * t0:C_ROPE + 16 * (t0 + nt)].rearrange("p (t c) -> p t c", t=nt)
                cos, sin = (cs[:, :, x:x + 8].unsqueeze(2).to_broadcast([P, nt, nh, 8]) for x in (0, 8))
                x1, x2 = v[:, :, :, 0:8], v[:, :, :, 8:16]
                r = [ropb[0:P, 256 * j:256 * j + 8 * n].rearrange("p (t h d) -> p t h d", t=nt, h=nh) for j in range(4)]
                dve.tensor_tensor(r[0], x1, cos, ALU.mult)
                dve.tensor_tensor(r[1], x2, sin, ALU.mult)
                dve.tensor_tensor(r[2], x2, cos, ALU.mult)
                link(dve.tensor_tensor(r[3], x1, sin, ALU.mult))
                dve.tensor_tensor(x1, r[0], r[1], ALU.subtract)
                dve.tensor_tensor(x2, r[2], r[3], ALU.add).then_inc(nrm_done, 1)
                dve.wait_ge(nrm_done, i + 1)

            def cmp_evac(u):
                b, x, m = u // 2, u % 2, (NC if u < 16 else PNC)
                evac(("cmp", u), (vcm if x else kcm)[0:m, b, :], ps(("cmp", u))[0:m, 0:128])

            for u in range(18):
                n, m = (CH, NC) if u < 16 else (PCH, PNC)
                for i in (1, 3):
                    if u >= 2:
                        want_filled(dve, ("pre", u - 2))
                    want_filled(dve, ("xt", u, i))
                    spread_chunks(dve.tensor_copy, u, i, n)
                if u:
                    cmp_evac(u - 1)
                if u in NORM_AT:
                    norm_rope(NORM_AT.index(u))
                want_filled(dve, ("pre", u))
                dve.wait_ge(half_ready, u + 1)
                frees(dve.tensor_tensor(half[:, :, 0:m], half[:, :, 0:m],
                                        ps(("pre", u))[0:64, 0:2 * n].rearrange("p (k c) -> p k c", k=2)[:, :, 0:m], ALU.add),
                      ("pre", u))
            cmp_evac(17)
            norm_rope(6)
            norm_rope(7)
            dve.wait_ge(gate_exp, 2)
            for z in (gat[:, 0:96], gat[0:TS, 96:120]):
                link(dve.tensor_scalar(z, z, 1.0, None, ALU.add))
                link(dve.reciprocal(z, z))
            qv = qblk.rearrange("p (b k g q) -> p b k g q", b=8, k=2, g=4)
            for g in range(G):
                key = ("qT", g, 1)
                want_filled(dve, key)
                for k in range(2):
                    r = slice(64 * k, 64 * k + 64)
                    ins = dve.tensor_copy(qv[r, :, k, g, :], ps(key)[r, 0:TS].rearrange("p (b q) -> p b q", b=8))
                frees(ins, key)
            evac(("kTn",), kTn, ps(("kTn",))[:, 0:128].rearrange("p (x n) -> p x n", x=2))

            for gp in range(4):
                key = ("cS", gp)
                want_filled(dve, key)
                if gp:
                    want_filled(dve, ("cPT", gp - 1))
                frees(dve.tensor_tensor_reduce(csb, ps(key)[:, 0:NC], cst[:, C_CAUS:C_CAUS + NC], -QS, 3e38, ALU.add, ALU.min,
                                               small[:, 100:101]), key)
                dve.wait_ge(c_exp, gp + 1)
                link(dve.reciprocal(small[:, 102:103], small[:, 101:102]))
                dve.tensor_scalar(csb, csb, small[:, 102:103], None, ALU.mult).then_inc(c_prob, 1)
                want_emptied(dve, ("cPT", gp))
                link(dve.tensor_reduce(cpg, ctb.rearrange("p (a g q) -> p a q g", a=4, g=4), AX, ALU.add))
                dve.tensor_copy(cpx.rearrange("p (a g q) -> p a g q", a=4, g=4), cpg.unsqueeze(2).to_broadcast([NC, 4, 4, 8])
                                ).then_inc(c_group, 1)
                evac(("imp", gp), imps[:, :], ps(("imp", gp))[:, 1:31])
                want_emptied(dve, ("imp", gp))
                vi = imps[:, :].unsqueeze(1).to_broadcast([128, NC1, NC1])
                vj = imps[:, :].unsqueeze(2).to_broadcast([128, NC1, NC1])
                r1, r2 = (z.rearrange("p (j i) -> p j i", j=NC1) for z in (rk1, rk2))
                dve.tensor_tensor(r1, vi, vj, ALU.is_gt)
                link(dve.tensor_tensor(r2, vi, vj, ALU.is_equal))
                link(dve.tensor_tensor(rk2, rk2, cst[:, C_TRI:C_TRI + 900], ALU.mult))
                link(dve.tensor_tensor(rk1, rk1, rk2, ALU.add))
                link(dve.tensor_reduce(sel32[:, 1:31], r1, AX, ALU.add))
                link(dve.tensor_scalar(sel32[:, 1:31], sel32[:, 1:31], NSEL_FREE - 0.5, NEG, ALU.is_gt, ALU.mult))
                link(dve.tensor_copy(selb[:, 128 * gp:128 * gp + 128].rearrange("p (j c) -> p j c", j=32),
                                     sel32[:, :].unsqueeze(2).to_broadcast([128, 32, 4])))

            for gp in range(4):
                if gp:
                    want_filled(dve, ("PT", gp - 1, 5))

                def masked(key, dst, src, mask, col):
                    want_filled(dve, key)
                    return dve.tensor_tensor_reduce(dst, src, mask, -QS, 3e38, ALU.add, ALU.min, small[:, 104 + col:105 + col])

                def scores(c):
                    key = ("S", gp, c)
                    if c < 4:
                        m = selb[:, 128 * gp:128 * gp + 128].unsqueeze(1).to_broadcast([128, 4, 128])
                        ins = masked(key, ssb[:, 512 * c:512 * c + 512].rearrange("p (s n) -> p s n", s=4),
                                     ps(key)[:, :].rearrange("p (s n) -> p s n", s=4), m, c)
                    else:
                        ins = masked(key, wsb[:, 0:512], ps(key)[:, :], cst[:, C_WIN:C_WIN + 512], 5)
                    frees(ins, key)

                for c in range(5):
                    if c >= 2:
                        want_filled(dve, ("S", gp, c - 2))
                    elif gp:
                        want_filled(dve, ("S", gp - 1, c + 3))
                    evac(("T", gp, c, 1), kTc[:, 1, c % 2, :], ps(("T", gp, c, 1))[:, :])
                    if c:
                        scores(c - 1)
                scores(4)
                nm = cst[:, C_NEW + 64 * gp:C_NEW + 64 * gp + 64]
                masked(("Sn", gp), ssb[:, 2048:2112], ps(("Sn", gp))[:, 0:64], nm, 4)
                frees(masked(("Sn", gp), wsb[:, 512:576], ps(("Sn", gp))[:, 64:128], nm, 6), ("Sn", gp))
                want_emptied(dve, ("Sn", gp))
                dve.tensor_reduce(small[:, 112:113], small[:, 104:109], AX, ALU.min)
                dve.tensor_reduce(small[:, 113:114], small[:, 109:111], AX, ALU.min).then_inc(s_min, 1)
                for i in (1, 3, 5):
                    key = ("PT", gp, i)
                    if i == 5:
                        evac(key, pTn, ps(key)[0:TS, 0:256].rearrange("p (x n) -> p x n", x=2))
                    else:
                        evac(key, pT[:, 4 * i:4 * i + 4, :], ps(key)[:, :].rearrange("p (s n) -> p s n", s=4))
                dve.wait_ge(s_exp, 2 * gp + 2)
                link(dve.reciprocal(small[:, 116:118], small[:, 114:116]))
                for x in range(2):
                    key = ("O", gp, x)
                    want_filled(dve, key)
                    for i in range(4):
                        r = slice(32 * i, 32 * i + 32)
                        ins = dve.tensor_scalar(orow[r, gp, 1 + x, :], ps(key)[r, 64 * (i % 2):64 * (i % 2) + 64],
                                                small[r, 116 + x:117 + x], None, ALU.mult)
                    frees(ins, key)
                want_emptied(dve, ("cO", gp))
                want_emptied(dve, ("O", gp, 1))
                dve.tensor_copy(small[:, 251:252], orow[:, gp, 2, 0:1]).then_inc(o_row, 1)

            for t in range(4):
                w = 128 * (t + 1)
                if t:
                    want_filled(dve, ("pcPT", t - 1, 1))
                mb = cst[:, C_CMB + PNC * t:C_CMB + PNC * (t + 1)].unsqueeze(1).to_broadcast([128, 4, PNC])
                for k in range(NKV):
                    key = ("pcS", t, k)
                    want_filled(dve, key)
                    frees(dve.tensor_tensor(pcp[:, 4 * k:4 * k + 4, :], ps(key)[:, 0:4 * PNC].rearrange("p (h n) -> p h n", h=4),
                                            mb, ALU.add), key)
                    want_emptied(dve, key)
                link(dve.tensor_reduce(small[:, 160:168], pcp, AX, ALU.max))
                dve.tensor_tensor(pcp, pcp, small[:, 160:168].unsqueeze(2).to_broadcast([128, 8, PNC]), ALU.subtract
                                  ).then_inc(p_in, 1)
                dve.wait_ge(p_exp, t + 1)
                m01 = cst[:, C_CM01 + PNC * t:C_CM01 + PNC * (t + 1)].unsqueeze(1).to_broadcast([128, 8, PNC])
                link(dve.tensor_tensor(pcp, pcp, m01, ALU.mult))
                link(dve.tensor_reduce(small[:, 160:168], pcp, AX, ALU.add))
                link(dve.tensor_scalar(small[:, 160:168], small[:, 160:168], 1e-30, None, ALU.max))
                link(dve.reciprocal(small[:, 160:168], small[:, 160:168]))
                dve.tensor_tensor(pcp, pcp, small[:, 160:168].unsqueeze(2).to_broadcast([128, 8, PNC]), ALU.mult
                                  ).then_inc(p_prob, 1)
                ov = pj[:, t, 0:512].rearrange("p (h d) -> p h d", h=8)
                ot = otmp.rearrange("p (h d) -> p h d", h=8)

                def add_branch(x):
                    key = ("pO", t, x)
                    cf = small[:, 168 + 8 * x:176 + 8 * x]
                    if x:
                        dve.wait_ge(p_soft, 8 * (2 * t + x))
                        link(dve.reciprocal(cf, small[:, 120 + 8 * x:128 + 8 * x]))
                        link(dve.tensor_tensor(cf, cf, gate[:, t, :, x], ALU.mult))
                        cf = cf.unsqueeze(2).to_broadcast([128, 8, 64])
                    else:
                        cf = gate[:, t, :, 0:1].to_broadcast([128, 8, 64])
                    want_filled(dve, key)
                    frees(dve.tensor_tensor(ot if x else ov, ps(key)[:, :].rearrange("p (h d) -> p h d", h=8), cf, ALU.mult), key)
                    want_emptied(dve, key)
                    if x == 1:
                        link(dve.tensor_tensor(ov, ov, ot, ALU.add))
                    if x == 2:
                        dve.tensor_tensor(ov, ov, ot, ALU.add).then_inc(attn_ready, 1)

                add_branch(0)
                for br in range(2):
                    for i in range(NH):
                        key = ("pS", t, br, i)
                        want_filled(dve, key)
                        if i >= 2:
                            want_filled(dve, ("pPT", t, br, i - 2))
                        elif br or t:
                            want_filled(dve, ("pPT", t - (1 - br), 1 - br, 6 + i))
                        frees(dve.tensor_tensor_reduce(psb[:, i % 2, 0:w], ps(key)[:, 0:w],
                                                       cst[:, C_CAUS + 512 - w:C_CAUS + 512], -QS, 3e38, ALU.add, ALU.min,
                                                       small[:, 144 + i:145 + i]), key)
                    add_branch(1 + br)
            dve.wait_ge(rows_back, 128)
            ov = pj[0:TS, 4, 0:512].rearrange("p (h d) -> p h d", h=8)
            ot = otmp[0:TS, :].rearrange("p (h d) -> p h d", h=8)
            for x in range(3):
                cf = gate[0:TS, 4, :, x:x + 1].to_broadcast([TS, 8, 64])
                link(dve.tensor_tensor(ot if x else ov, osm[:, :, x, :], cf, ALU.mult))
                if x == 1:
                    link(dve.tensor_tensor(ov, ov, ot, ALU.add))
                if x == 2:
                    dve.tensor_tensor(ov, ov, ot, ALU.add).then_inc(attn_ready, 1)
            dve.wait_ge(a_root, 1)
            link(dve.reciprocal(small[:, 16:21], small[:, 8:13]))
            for t in range(5):
                dve.tensor_scalar(pj[0:TM[t], t, 0:512], pj[0:TM[t], t, 0:512], small[0:TM[t], 16 + t:17 + t], None, ALU.mult
                                  ).then_inc(a_ready, 1)
            for t in range(5):
                key = ("oT", t)
                want_filled(dve, key)
                frees(dve.tensor_tensor(oT[:, :, 128 * t:128 * t + TM[t]],
                                        ps(key)[:, 0:4 * TM[t]].rearrange("p (k n) -> p k n", k=4),
                                        colT[:, 16:20].unsqueeze(2).to_broadcast([128, 4, TM[t]]), ALU.mult), key)
            dve.wait_ge(stored, 16 * N_STORED)
            dve.wait_ge(kvc_stored, 32)
            dve.wait_ge(xin_loaded, 80)
            for n in range(2):
                cols = slice(512 * n, 512 * n + 512)
                for t in range(5):
                    key, i, P = ("wo", n, t), 5 * n + t, TM[t]
                    want_filled(dve, key)
                    for s in range(2):
                        want_emptied(dve, ("gate", 0, n, s))
                    frees(dve.tensor_tensor(x1t[0:P, i % 2, :], ps(key)[0:P, :], gbc[0:P, t // 4, cols], ALU.mult), key)
                    want_emptied(dve, key)
                    dve.tensor_tensor(xs[0:P, t, cols], x1t[0:P, i % 2, :], xin[0:P, t, cols], ALU.add).then_inc(x1_ready, 1)
            dve.wait_ge(x1_ready, 10)
            for t in range(6):
                if t < 5:
                    P = TM[t]
                    dve.wait_ge(x1_root, t + 1)
                    if t >= 2:
                        want_filled(dve, ("hT", t - 2, 1))
                    link(dve.reciprocal(small[0:P, 24 + t:25 + t], small[0:P, 24 + t:25 + t]))
                    dve.tensor_scalar(xnb[0:P, t % 2, :], xs[0:P, t, :], small[0:P, 24 + t:25 + t], None, ALU.mult
                                      ).then_inc(x1n_ready, 1)
                if t and t < 5:
                    key = ("hT", t - 1, 0)
                    want_filled(dve, key)
                    for k in range(4):
                        ins = dve.tensor_scalar(hT[:, k, 128 * (t - 1):128 * t], ps(key)[:, 128 * k:128 * k + 128],
                                                mod[:, 1, 0, k, 0:1], mod[:, 1, 1, k, 0:1], ALU.mult, ALU.add)
                    frees(ins, key)
            for h in range(2):
                key = ("hT", 4, h)
                want_filled(dve, key)
                dst = hT[:, 4 * h:4 * h + 4, SEQ:TOK].rearrange("p k (b q) -> p k b q", b=8)
                A, B = (mod[:, 1, x, 4 * h:4 * h + 4, 1:9].unsqueeze(3).to_broadcast([128, 4, 8, 8]) for x in range(2))
                link(dve.tensor_tensor(dst, ps(key)[:, 0:256].rearrange("p (k b q) -> p k b q", k=4, b=8), A, ALU.mult))
                frees(dve.tensor_tensor(dst, dst, B, ALU.add), key)
            for i in range(NFT):
                for h in range(2):
                    key = ("gu", i, 1, h)
                    want_filled(dve, key)
                    want_emptied(dve, ("gu", i, 0, h))
                    frees(dve.tensor_tensor(actT[:, i, HALF * h:HALF * h + HALF], ps(key)[:, 0:HALF],
                                            sgb[:, i % 2, HALF * h:HALF * h + HALF], ALU.mult), key)
            for n in range(2):
                cols = slice(512 * n, 512 * n + 512)
                for t in range(5):
                    key, i, P = ("dn", n, t), 5 * n + t, TM[t]
                    want_filled(dve, key)
                    for s in range(2):
                        want_emptied(dve, ("gate", 1, n, s))
                    frees(dve.tensor_tensor(yt[0:P, i % 2, :], ps(key)[0:P, :], gbc[0:P, t // 4, cols], ALU.mult), key)
                    want_emptied(dve, key)
                    dve.tensor_tensor(xs[0:P, t, cols], yt[0:P, i % 2, :], xs[0:P, t, cols], ALU.add).then_inc(out_ready, 1)

        @block.tensor
        def _(pe):
            def turn(dst, src):
                P = src.shape[0]
                return pe.transpose(dst, src, ident[0:P, 0:P])

            pe.wait_ge(consts_loaded, 16)
            pe.wait_ge(gains_loaded, 160)
            fills(turn(ps(("rows",))[:, 0:52], rowb[:, :]), ("rows",))
            pe.wait_ge(scrow_ready, 1)
            for k in range(8):
                ins = turn(ps(("cT",))[:, 9 * k:9 * k + 9], scrow[:, 128 * k:128 * k + 128])
            fills(ins, ("cT",))
            pe.wait_ge(conv_state_loaded, 16)
            for m in range(4):
                ins = turn(ps(("sconv",))[:, 16 * m:16 * m + 16], stc[:, 128 * m:128 * m + 128])
            fills(ins, ("sconv",))
            for t in range(5):
                pe.wait_ge(xn_ready, t + 1)
                for h in range(2):
                    key = ("xT", t, h)
                    want_free(pe, key)
                    for k in range(4):
                        f = 128 * (4 * h + k)
                        ins = turn(ps(key)[:, TM[t] * k:TM[t] * k + TM[t]], xs[0:TM[t], t, f:f + 128])
                    fills(ins, key)
            pe.wait_ge(comp_w_loaded, 96)
            want_emptied(pe, ("rows",))
            for x in range(2):
                key = ("peb", x)
                want_free(pe, key)
                for i in range(16):
                    ins = pe.matmul(ps(key)[0:64, 0:1], w1v[:, x, i % 8, i // 8, :], colT[:, 36 + i:37 + i],
                                    start=i == 0, stop=i == 15)
                fills(ins, key)

            def mod_turn(l):
                key = ("mod", l)
                want_free(pe, key)
                for n in range(4):
                    want_emptied(pe, ("ada", n + 6 * l))
                for i in range(16):
                    c0 = 2048 * l + 128 * i
                    ins = turn(ps(key)[:, 9 * i:9 * i + 9], modss[:, c0:c0 + 128])
                fills(ins, key)

            want_emptied(pe, ("cT",))
            for n in range(12):
                key = ("ada", n)
                want_free(pe, key)
                for kh in range(2):
                    w = weights(pe, ("ada", n, kh))
                    for k in range(4):
                        kk = 4 * kh + k
                        ins = pe.matmul(ps(key)[0:9, :], cT[:, 9 * kk:9 * kk + 9], w[:, k, :], start=kk == 0, stop=kk == 7)
                fills(ins, key)
                if n == 3:
                    mod_turn(0)
            mod_turn(1)

            for n in range(3):
                w = min(512, TEND - 512 * n)
                for t in range(5):
                    key = ("in", n, t)
                    want_free(pe, key)
                    for kh in range(2):
                        wt = weights(pe, ("in", n, kh))
                        for k in range(4):
                            kk = 4 * kh + k
                            if n == 0 and t == 0:
                                pe.wait_ge(hT_ready, kk + 1)
                            ins = pe.matmul(ps(key)[0:TM[t], 0:w], hT[:, kk, 128 * t:128 * t + TM[t]], wt[:, k, 0:w],
                                            start=kk == 0, stop=kk == 7)
                    fills(ins, key)
            for n in range(3):
                for m in range(4):
                    for h in range(2):
                        key = ("cv", n, m, h)
                        want_free(pe, key)
                        for kk in range(8):
                            wt = weights(pe, ("cv", n, kk // 4))
                            ins = pe.matmul(ps(key)[:, 0:HALF], wt[:, kk % 4, 128 * m:128 * m + 128],
                                            hT[:, kk, HALF * h:HALF * h + HALF], start=kk == 0, stop=kk == 7)
                        fills(ins, key)
            pe.wait_ge(u_end_ready, 4)
            want_free(pe, ("ulast",))
            for m in range(4):
                ins = turn(ps(("ulast",))[0:18, 128 * m:128 * m + 128], ulast[:, 18 * m:18 * m + 18])
            fills(ins, ("ulast",))
            pe.wait_ge(y_square, 4)
            for h in range(2):
                key = ("yss", h)
                want_free(pe, key)
                for m in range(4):
                    ins = pe.matmul(ps(key)[:, 0:HALF], cst[:, C_ONE:C_ONE + 128], hcT[:, m, HALF * h:HALF * h + HALF],
                                    start=m == 0, stop=m == 3)
                fills(ins, key)

            for u in range(19):
                if u < 18:
                    n = CH if u < 16 else PCH
                    xc = cache(pe, u)
                    for i in range(4):
                        key = ("xt", u, i)
                        want_free(pe, key)
                        for jj in range(4):
                            ins = turn(ps(key)[:, 128 * jj:128 * jj + n], xc[0:n, 2 * (4 * (i // 2) + jj) + i % 2, :])
                        fills(ins, key)
                if u:
                    key, m = ("cmp", u - 1), (NC if u <= 16 else PNC)
                    x = (u - 1) % 2
                    want_free(pe, key)
                    pe.wait_ge(silu_ready, u)
                    for k in range(2):
                        ins = pe.matmul(ps(key)[0:m, 64 * k:64 * k + 64], slu[:, k, 0:m], w2[:, 64 * x:64 * x + 64],
                                        start=True, stop=True)
                    fills(ins, key)
                if u < 18:
                    key = ("pre", u)
                    want_free(pe, key)
                    for i in range(4):
                        want_emptied(pe, ("xt", u, i))
                    for j in range(8):
                        ins = pe.matmul(ps(key)[:, 0:2 * n], w1v[:, u % 2, j].rearrange("p r h -> p (r h)"),
                                        xcmp[:, u % 2, j, :, 0:n], start=j == 0, stop=j == 7)
                    fills(ins, key)
            pe.wait_ge(nrm_done, 8)
            for i in range(3):
                key = ("kct", i)
                want_free(pe, key)
                for b in range(4 * i, min(4 * i + 4, 9)):
                    m = NC if b < 8 else PNC
                    c0 = 128 * (b - 4 * i)
                    ins = turn(ps(key)[:, c0:c0 + m], kcm[0:m, b, :])
                fills(ins, key)
            for g in range(G):
                for s in range(2):
                    key = ("qT", g, s)
                    want_free(pe, key)
                    for t in (range(4), (4,))[s]:
                        c0 = 128 * (t % 4)
                        ins = turn(ps(key)[:, c0:c0 + TM[t]],
                                   pj[0:TM[t], t, 128 * g:128 * g + 128])
                    fills(ins, key)
            for x, c in enumerate((TKS, TKW)):
                key = ("kT", x)
                want_free(pe, key)
                for t in range(4):
                    ins = turn(ps(key)[:, 128 * t:128 * t + 128], pj[:, t, c:c + 128])
                fills(ins, key)
            want_free(pe, ("kTn",))
            for x, c in enumerate((TKS, TKW)):
                ins = turn(ps(("kTn",))[:, 64 * x:64 * x + 64], pj[0:TS, 4, c:c + 128])
            fills(ins, ("kTn",))

            for g in range(G):
                want_emptied(pe, ("qT", g, 1))
            for i in range(3):
                want_emptied(pe, ("kct", i))
            for gp in range(4):
                key = ("cS", gp)
                want_free(pe, key)
                for b in range(2):
                    bb = 2 * gp + b
                    ins = pe.matmul(ps(key)[64 * b:64 * b + 64, 0:NC], qblk[:, 64 * bb:64 * bb + 64], kcT[:, bb, 0:NC],
                                    start=True, stop=True)
                fills(ins, key)
                key = ("cPT", gp)
                want_free(pe, key)
                pe.wait_ge(c_prob, gp + 1)
                fills(turn(ps(key)[0:NC, 0:128], csb), key)
                key = ("imp", gp)
                want_free(pe, key)
                pe.wait_ge(c_group, gp + 1)
                fills(pe.matmul(ps(key)[:, 0:32], cpx, cst[0:NC, C_OVL:C_OVL + 32],
                                start=True, stop=True), key)
                key = ("cO", gp)
                want_free(pe, key)
                want_emptied(pe, ("cPT", gp))
                for b in range(2):
                    ins = pe.matmul(ps(key)[64 * b:64 * b + 64, 0:128], ctb[:, 64 * b:64 * b + 64], vcm[0:NC, 2 * gp + b, :],
                                    start=True, stop=True)
                fills(ins, key)

            want_emptied(pe, ("kTn",))
            for gp in range(4):
                i0 = 18 + 4 * gp

                def score(c):
                    key = ("S", gp, c)
                    want_free(pe, key)
                    for b in range(2):
                        want_emptied(pe, ("T", gp, c, b))
                    for b in range(2):
                        bb = 2 * gp + b
                        ins = pe.matmul(ps(key)[64 * b:64 * b + 64, :], qblk[:, 64 * bb:64 * bb + 64], kTc[:, b, c % 2, :],
                                        start=True, stop=True)
                    fills(ins, key)

                for c in range(5):
                    for b in range(2):
                        key = ("T", gp, c, b)
                        want_free(pe, key)
                        if c < 4:
                            kk = cache(pe, i0 + b)[:, 4 * c:4 * c + 4, :]
                        else:
                            pe.wait_ge(win_loaded, 64 * (gp + 1))
                            kk = wnd[:, 0, b, :].rearrange("p (s n) -> p s n", s=4)
                        for i in range(4):
                            ins = turn(ps(key)[:, 128 * i:128 * i + 128], kk[:, i, :])
                        fills(ins, key)
                    if c:
                        score(c - 1)
                score(4)
                key = ("Sn", gp)
                want_free(pe, key)
                for b in range(2):
                    bb = 2 * gp + b
                    ins = pe.matmul(ps(key)[64 * b:64 * b + 64, 0:128], qblk[:, 64 * bb:64 * bb + 64],
                                    kTn.rearrange("p x n -> p (x n)"), start=True, stop=True)
                fills(ins, key)
                for i in range(6):
                    key = ("PT", gp, i)
                    want_free(pe, key)
                    pe.wait_ge(s_exp, 2 * gp + (1 if i < 4 else 2))
                    if i < 5:
                        src = wsb[:, 0:512] if i == 4 else ssb[:, 512 * i:512 * i + 512]
                        for s in range(4):
                            ins = turn(ps(key)[:, 128 * s:128 * s + 128], src[:, 128 * s:128 * s + 128])
                    else:
                        turn(ps(key)[0:TS, 0:128], ssb[:, 2048:2112])
                        ins = turn(ps(key)[0:TS, 128:256], wsb[:, 512:576])
                    fills(ins, key)
                for i in range(6):
                    want_emptied(pe, ("PT", gp, i))
                for x in range(2):
                    key = ("O", gp, x)
                    want_free(pe, key)
                    for b in range(2):
                        r = slice(64 * b, 64 * b + 64)
                        if x:
                            vv, pp, ns, vc = wnd[:, 1, b, :].rearrange("p (s n) -> p s n", s=4), pTw, 4, TVW
                        else:
                            vv, pp, ns, vc = cache(pe, i0 + 2 + b), pT, 16, TVS
                        for s in range(ns):
                            pe.matmul(ps(key)[r, 0:128], pp[:, s, r], vv[:, s, :], start=s == 0, stop=False)
                        ins = pe.matmul(ps(key)[r, 0:128], pTn[:, x, r], pj[0:TS, 4, vc:vc + 128], start=False, stop=True)
                    fills(ins, key)

            for g in range(G):
                want_emptied(pe, ("qT", g, 0))
            for x in range(2):
                want_emptied(pe, ("kT", x))
            for t in range(4):
                def rows(h):
                    return slice(64 * (h // G), 64 * (h // G) + 64)

                def q_of(h):
                    return qTp[rows(h), h % G, 128 * t:128 * t + 128]

                for k in range(NKV):
                    key = ("pcS", t, k)
                    want_free(pe, key)
                    for g in range(G):
                        ins = pe.matmul(ps(key)[:, PNC * g:PNC * g + PNC], q_of(G * k + g), kcT[rows(G * k), 8, 0:PNC],
                                        start=True, stop=True)
                    fills(ins, key)
                pe.wait_ge(p_prob, t + 1)
                for hh in range(2):
                    key = ("pcPT", t, hh)
                    want_free(pe, key)
                    for i in range(4):
                        h = 4 * hh + i
                        ins = turn(ps(key)[0:PNC, 128 * i:128 * i + 128], pcp[:, h, :])
                    fills(ins, key)
                key = ("pO", t, 0)
                want_free(pe, key)
                for hh in range(2):
                    want_emptied(pe, ("pcPT", t, hh))
                for h in range(NH):
                    ins = pe.matmul(ps(key)[:, 64 * h:64 * h + 64], ppTc[:, h, :], vcm[0:PNC, 8, rows(h)], start=True, stop=True)
                fills(ins, key)
                for br in range(2):
                    okey = ("pO", t, 1 + br)
                    want_free(pe, okey)
                    for i in range(NH + 2):
                        if i < NH:
                            key = ("pS", t, br, i)
                            want_free(pe, key)
                            fills(pe.matmul(ps(key)[:, 0:128 * (t + 1)], q_of(i), kTp[rows(i), br, 0:128 * (t + 1)],
                                            start=True, stop=True), key)
                        if 1 <= i <= NH:
                            h = i - 1
                            key = ("pPT", t, br, h)
                            want_free(pe, key)
                            pe.wait_ge(p_soft, 8 * (2 * t + br) + h + 1)
                            for k in range(t + 1):
                                ins = turn(ps(key)[:, 128 * k:128 * k + 128], psb[:, h % 2, 128 * k:128 * k + 128])
                            fills(ins, key)
                        if i >= 2:
                            h = i - 2
                            want_emptied(pe, ("pPT", t, br, h))
                            c0 = (TVS, TVW)[br] + 64 * (h // G)
                            for k in range(t + 1):
                                ins = pe.matmul(ps(okey)[:, 64 * h:64 * h + 64], ppT[:, h % 2, k, :], pj[:, k, c0:c0 + 64],
                                                start=k == 0, stop=k == t)
                    fills(ins, okey)
            for t in range(5):
                key = ("oT", t)
                want_free(pe, key)
                pe.wait_ge(a_ready, t + 1)
                for k in range(4):
                    ins = turn(ps(key)[:, TM[t] * k:TM[t] * k + TM[t]], pj[0:TM[t], t, 128 * k:128 * k + 128])
                fills(ins, key)

            def gate_rows(l):
                for n in range(2):
                    want_emptied(pe, ("ada", (4, 10)[l] + n))
                    for s in range(2):
                        key, P = ("gate", l, n, s), (128, TS)[s]
                        want_free(pe, key)
                        c0 = 1024 * l + 512 * n
                        fills(pe.matmul(ps(key)[0:P, :], cst[0:9, C_SEL + 128 * s:C_SEL + 128 * s + P], grow[:, c0:c0 + 512],
                                        start=True, stop=True), key)

            gate_rows(0)
            pe.wait_ge(vT_ready, 4)
            for n in range(2):
                for t in range(5):
                    key = ("wo", n, t)
                    want_free(pe, key)
                    want_emptied(pe, ("oT", t))
                    for kk in range(8):
                        wt = weights(pe, ("wo", n, kk // 4))
                        src = oT if kk < 4 else vT
                        ins = pe.matmul(ps(key)[0:TM[t], :], src[:, kk % 4, 128 * t:128 * t + TM[t]], wt[:, kk % 4, :],
                                        start=kk == 0, stop=kk == 7)
                    fills(ins, key)
            for t in range(5):
                pe.wait_ge(x1n_ready, t + 1)
                for h in range(2):
                    key = ("hT", t, h)
                    want_free(pe, key)
                    for k in range(4):
                        f = 128 * (4 * h + k)
                        ins = turn(ps(key)[:, TM[t] * k:TM[t] * k + TM[t]], xnb[0:TM[t], t % 2, f:f + 128])
                    fills(ins, key)
            pe.wait_ge(x1_ready, 10)
            gate_rows(1)
            for t in range(5):
                for h in range(2):
                    want_emptied(pe, ("hT", t, h))
            for i in range(NFT):
                for x in range(2):
                    for h in range(2):
                        key = ("gu", i, x, h)
                        want_free(pe, key)
                        for kk in range(8):
                            wt = weights(pe, ("gu", i // 2, kk // 4))
                            c0 = 256 * x + 128 * (i % 2)
                            ins = pe.matmul(ps(key)[:, 0:HALF], wt[:, kk % 4, c0:c0 + 128], hT[:, kk, HALF * h:HALF * h + HALF],
                                            start=kk == 0, stop=kk == 7)
                        fills(ins, key)
            for n in range(2):
                for kc in range(6):
                    wt = weights(pe, ("dn", n, kc))
                    nk = 4 if kc < 5 else NFT - 20
                    if n == 0:
                        for k in range(nk):
                            for h in range(2):
                                want_emptied(pe, ("gu", 4 * kc + k, 1, h))
                    for t in range(5):
                        key = ("dn", n, t)
                        if kc == 0:
                            want_free(pe, key)
                        for k in range(nk):
                            kk = 4 * kc + k
                            ins = pe.matmul(ps(key)[0:TM[t], :], actT[:, kk, 128 * t:128 * t + TM[t]], wt[:, k, :],
                                            start=kk == 0, stop=kk == NFT - 1)
                        if kc == 5:
                            fills(ins, key)
                    if kc < 5:
                        ins.then_inc(dn_read, 1)


NORMS = [("q", 128, 32, 0, 4, 8, 0), ("q", TS, 8, 4, 1, 8, 0), ("ks", 128, 8, 0, 4, 2, 2), ("ks", TS, 2, 4, 1, 2, 2),
         ("kw", 128, 8, 0, 4, 2, 3), ("kw", TS, 2, 4, 1, 2, 3), ("kcm", NC, 16, 0, 8, 2, 1), ("kcm", PNC, 2, 8, 1, 2, 1)]
NORM_AT = [0, 1, 2, 3, 4, 5]
N_STORED = 3 + 1 + 1 + 2 + 8 + 2 + 1 + 8 + 2

_INS = ["x_prompt", "x_sample", "cache_k_cmp", "cache_v_cmp", "cache_k_slc", "cache_v_slc", "state_k_win", "state_v_win",
        "state_conv", "page_table", "c_prompt", "c_sample", "w_ada", "b_ada", "ln1_g", "w_in", "q_norm_g", "k_norm_g",
        "pe_cmp", "w_ck1", "w_ck2", "w_cv1", "w_cv2", "w_conv", "attn_out_g", "conv_out_g", "w_o", "ln2_g", "w_gu", "w_down"]
_OUTS = [("y_prompt", (1, SEQ, D)), ("y_sample", (NB, NQ, D))]
_OUTS += [(f"p_{n}", (1, 1, SEQ, NKV, HD)) for n in ("k_cmp", "v_cmp", "k_slc", "v_slc", "k_win", "v_win")]
_OUTS += [("p_conv", (1, 1, 2, 512))]
_OUTS += [(f"s_{n}", (1, NB, NQ, NKV, HD)) for n in ("k_cmp", "v_cmp", "k_slc", "v_slc")]
_OUTS += [(f"s_{n}", (1, NB, SEQ, NKV, HD)) for n in ("k_win", "v_win")]
_OUTS += [("s_conv", (1, NB, 2, 512))]


def kernel(**inputs):
    import numpy as _np
    import concourse.bacc as _bacc
    from concourse import mybir as _mybir
    from concourse.bass_utils import run_bass_kernel_spmd as _run

    nc = _bacc.Bacc("TRN2", target_bir_lowering=False, num_devices=1)
    arrays, ins, outs = {}, {}, {}
    given = {name: _np.ascontiguousarray(inputs[name]) for name in _INS}
    given["consts"] = constants()
    for name, x in given.items():
        arrays[f"in_{name}"] = x
        ins[name] = nc.dram_tensor(f"in_{name}", x.shape, _mybir.dt.from_np(x.dtype), kind="ExternalInput").ap()
    for name, shape in _OUTS:
        outs[name] = nc.dram_tensor(f"out_{name}", shape, F32, kind="ExternalOutput").ap()
    decoder_kernel(nc, ins, outs)
    r = _run(nc, [arrays], core_ids=[0])
    return tuple(r.results[0][f"out_{name}"] for name, _ in _OUTS)
```

```python
from contextlib import ExitStack

import concourse.bass as bass
import numpy as np
from concourse import mybir

ALU = mybir.AluOpType
ACT = mybir.ActivationFunctionType
AX = mybir.AxisListType.X
F32 = mybir.dt.float32
F32R = mybir.dt.float32r
I32 = mybir.dt.int32
U32 = mybir.dt.uint32

D = 1024
SEQ, NB, NQ = 512, 8, 8
TS = NB * NQ
TOK = SEQ + TS
HALF = TOK // 2
HD, NH, NKV, G = 64, 8, 2, 4
KV = NKV * HD
PAST = 2048
CH = PAST // 16
NC = CH - 1
PCH = SEQ // 16
PNC = PCH - 1
NF = 2816
NFT = NF // 128
NC1 = 30
NSEL_FREE = 13
EPS = 1e-6
NEG = -1e30
QS = HD ** -0.5
WR = 4
CR = 4
TM = [128, 128, 128, 128, TS]
TQ, TKC, TVC, TKS, TVS, TKW, TVW, TG, TEND = 0, 512, 640, 768, 896, 1024, 1152, 1280, 1304

C_ID, C_ROPE, C_ROPEC, C_CAUS, C_CMB, C_CM01, C_NEW, C_WIN, C_OVL, C_TRI, C_SEL, C_ONE, C_P8, C_END = np.cumsum(
    [0, 128, 80, 16, 512, 124, 124, 256, 512, 32, 900, 192, 128, 1]).tolist()

GU_ORDER = [(0, 0), (1, 0), (0, 1), (1, 1)] + [(i, h) for i in range(2, NFT) for h in range(2)]
GATE_AT = (3, 1)
ADA_FIRST = 6
ADA_STEPS = 10


def constants():
    c = np.zeros((128, C_END), np.float32)
    p = np.arange(128)
    c[:, C_ID:C_ID + 128] = np.eye(128)
    inv = np.float32(500000.0) ** (-np.arange(8, dtype=np.float32) * np.float32(2.0) / np.float32(16))

    def cs(pos):
        ang = pos.astype(np.float32)[:, None] * inv[None, :]
        return np.concatenate([np.cos(ang), np.sin(ang)], 1)

    for t in range(5):
        c[:, C_ROPE + 16 * t:C_ROPE + 16 * t + 16] = cs(t * 128 + p if t < 4 else PAST + p % NQ)
    c[:, C_ROPEC:C_ROPEC + 16] = cs(p * 16 + 31)
    c[:, C_CAUS + 384:C_CAUS + 512] = np.where(p[None, :] <= p[:, None], 0, NEG)
    n = np.arange(PNC)
    for t in range(4):
        ok = n[None, :] * 16 + 31 <= (t * 128 + p)[:, None]
        c[:, C_CMB + PNC * t:C_CMB + PNC * (t + 1)] = np.where(ok, 0, NEG)
        c[:, C_CM01 + PNC * t:C_CM01 + PNC * (t + 1)] = ok
    b2, q = p // 64, p % 8
    k = np.arange(TS)
    for gp in range(4):
        ok = (k[None, :] // 8 == (2 * gp + b2)[:, None]) & (k[None, :] % 8 <= q[:, None])
        c[:, C_NEW + 64 * gp:C_NEW + 64 * gp + 64] = np.where(ok, 0, NEG)
    i = np.arange(512)
    c[:, C_WIN:C_WIN + 512] = np.where((4 * (i % 128) + i // 128)[None, :] > q[:, None], 0, NEG)
    j = np.arange(32)
    c[:, C_OVL:C_OVL + 32] = (p[:, None] * 16 < (j[None, :] + 1) * 64) & (p[:, None] * 16 + 32 > j[None, :] * 64)
    t30 = np.arange(NC1)
    c[:, C_TRI:C_TRI + 900] = (t30[None, :] < t30[:, None]).reshape(1, 900)
    c[0, C_SEL:C_SEL + 128] = 1
    c[1 + np.arange(TS) // 8, C_SEL + 128 + np.arange(TS)] = 1
    c[:, C_ONE:C_ONE + 128] = 1
    c[:, C_P8] = p % 8
    return c


def plan_banks():
    ring, wide, low_ring, extra = [], [], [], []
    ring += [("rows",), ("cT",), ("sconv",)]
    ring += [("xT", t, h) for t in range(5) for h in range(2)]
    ring += [("peb", x) for x in range(2)]
    for n in range(ADA_FIRST):
        ring.append(("ada", n))
        if n == 3:
            ring.append(("mod", 0))
    ring += [("in", n, t) for n in range(3) for t in range(5)]
    ring += [("cv", n, m, h) for n in range(3) for m in range(4) for h in range(2)]
    ring += [("ulast",), ("yss", 0), ("yss", 1)]
    ring += [("xt", 0, i) for i in range(4)]
    for u in range(19):
        if u < 17:
            ring += [("xt", u + 1, i) for i in range(4)]
        if u < 18:
            ring.append(("pre", u))
        if u:
            ring.append(("cmp", u - 1))
    ring += [("qT", g, s) for g in range(4) for s in range(2)]
    ring += [("kT", x) for x in range(2)] + [("kTn",)]
    ring += [("kct", i) for i in range(3)]

    def turned(gp, c):
        return [("T", gp, c, b) for b in range(2)]

    ring += [("cS", 0)] + turned(0, 0) + [("cPT", 0)] + turned(0, 1) + [("imp", 0)]
    wide.append(("cO", 0))
    for gp in range(4):
        more = gp < 3
        ring += [("S", gp, 0)] + turned(gp, 2) + [("S", gp, 1)]
        ring += [("cS", gp + 1)] * more
        ring += turned(gp, 3) + [("S", gp, 2)] + turned(gp, 4) + [("S", gp, 3)]
        ring += [("cPT", gp + 1)] * more
        ring += [("S", gp, 4), ("Sn", gp)]
        if more:
            ring += turned(gp + 1, 0) + turned(gp + 1, 1) + [("imp", gp + 1)]
            wide.append(("cO", gp + 1))
        ring += [("PT", gp, i) for i in range(6)]
        wide += [("O", gp, 0), ("O", gp, 1)]
    for t in range(4):
        low_ring += [("pcS", t, 0), ("pcS", t, 1), ("pcPT", t, 0), ("pcPT", t, 1)]
        wide.append(("pO", t, 0))
        for br in range(2):
            wide.append(("pO", t, 1 + br))
            for i in range(NH + 1):
                if i < NH:
                    low_ring.append(("pS", t, br, i))
                if i:
                    low_ring.append(("pPT", t, br, i - 1))
    extra += [("ada", n) for n in range(ADA_FIRST, 12)]
    before = len(ring)
    ring.append(("mod", 1))
    ring += [("oT", t) for t in range(5)]
    ring += [("gate", 0, n, s) for n in range(2) for s in range(2)]
    ring += [("wo", 0, t) for t in range(5)]
    for t in range(6):
        if t < 5:
            ring.append(("wo", 1, t))
        if t:
            ring += [("hT", t - 1, h) for h in range(2)]
    for i, h in GU_ORDER:
        ring += [("gu", i, x, h) for x in range(2)]
        if (i, h) == GATE_AT:
            ring += [("gate", 1, n, s) for n in range(2) for s in range(2)]
    ring += [("dn", n, t) for n in range(2) for t in range(5)]
    at, used = {}, [0] * 8
    for keys, banks in ((ring[:before], (0, 1, 2, 3, 4, 5)), (low_ring, (0, 1, 2, 3, 4)), (extra, (5,)),
                        (ring[before:], (0, 1, 2, 3, 4, 5)), (wide, (6, 7))):
        for i, k in enumerate(keys):
            b = banks[i % len(banks)]
            at[k] = (b, used[b])
            used[b] += 1
    return at


def plan_weights():
    c = [(("ada", n, kh), ("ada", n)) for n in range(ADA_FIRST) for kh in range(2)]
    c += [(("in", n, kh), ("in", n, 4)) for n in range(3) for kh in range(2)]
    c += [(("cv", n, kh), ("cv", n, 3, 1)) for n in range(3) for kh in range(2)]
    c += [(("ada", n, kh), ("ada", n)) for n in range(ADA_FIRST, 12) for kh in range(2)]
    c += [(("wo", n, kh), ("wo", n, 4)) for n in range(2) for kh in range(2)]
    c += [(("gu", n, kh), None) for n in range(NFT // 2) for kh in range(2)]
    c += [(("dn", n, kc), None) for n in range(2) for kc in range(6)]
    return c


def decoder_kernel(nc, a, o):
    at = plan_banks()
    chunks = plan_weights()
    chunk_of = {k: i for i, (k, _) in enumerate(chunks)}

    with ExitStack() as ctx:
        place = {}

        def sb(name, cols, dt=F32, parts=128):
            place[name] = -(-nc.sbuf_base // 32) * 32
            return ctx.enter_context(nc.sbuf_tensor(name, [parts, cols], dt))

        def pairs_at(name, tensor, c0, cols):
            z = nc.alloc_sbuf_tensor_at(name, [128, cols], F32R, offset=place[tensor.name] + 4 * c0)
            return z

        def sem(name):
            return ctx.enter_context(nc.semaphore(name))

        bank = [ctx.enter_context(nc.psum_tensor(f"bank{i}", [128, 512], F32)) for i in range(8)]
        bank_filled = [sem(f"bank_filled{i}") for i in range(8)]
        bank_free = [sem(f"bank_free{i}") for i in range(8)]

        cst = sb("cst", C_END)
        hbuf = sb("hbuf", 8 * TOK)
        hT = hbuf[:, :].rearrange("p (k n) -> p k n", k=8)
        xcmp = hbuf[:, 0:4096].rearrange("p (u j k c) -> p u j k c", u=2, j=8, k=2)
        kTc = hbuf[:, 0:2048].rearrange("p (b s n) -> p b s n", b=2, s=2)
        pT = hbuf[:, 2048:4096].rearrange("p (s n) -> p s n", s=16)
        pTn = hbuf[0:TS, 4096:4352].rearrange("p (x n) -> p x n", x=2)
        ppT = hbuf[:, 0:1024].rearrange("p (s k n) -> p s k n", s=2, k=4)
        ppTc = hbuf[0:PNC, 1024:2048].rearrange("p (h n) -> p h n", h=8)
        proj = sb("proj", 5 * TEND)
        pj = proj[:, :].rearrange("p (t n) -> p t n", t=5)
        xs = proj[:, 0:5 * D].rearrange("p (t n) -> p t n", t=5)
        wring = sb("wring", WR * 2048)
        wch = wring[:, :].rearrange("p (r k n) -> p r k n", r=WR, k=4)
        arena = sb("arena", NFT * TOK)
        actT = arena[:, :].rearrange("p (i n) -> p i n", i=NFT)
        cring = arena[:, 0:CR * 2048].rearrange("p (r n) -> p r n", r=CR)
        xin = arena[:, 0:5 * D].rearrange("p (t n) -> p t n", t=5)
        xnb = arena[:, 5 * D:7 * D].rearrange("p (s n) -> p s n", s=2)
        late = arena[:, CR * 2048:NFT * TOK]
        hcT = late[:, 0:4 * TOK].rearrange("p (f n) -> p f n", f=4)
        yrs = late[:, 4 * TOK:5 * TOK]
        modss = late[0:9, 0:2048]
        sqb = late[:, 0:2048]
        ropb = late[:, 2048:3072]
        ssb, wsb = late[:, 0:2112], late[:, 2112:2688]
        pTw = late[:, 2688:3200].rearrange("p (s n) -> p s n", s=4)
        psb = late[:, 2688:3712].rearrange("p (s n) -> p s n", s=2)
        x1t = late[:, 2688:3712].rearrange("p (s n) -> p s n", s=2)
        osm = late[0:TS, 0:1536].rearrange("p (h c n) -> p h c n", h=8, c=3)
        otmp = late[:, 1536:2048]
        ulr = late[0:18, 3800:4312]
        uvT = sb("uvT", 4 * TOK)
        uT = uvT[:, :].rearrange("p (f n) -> p f n", f=4)
        oT = uT
        rk1, rk2 = uvT[:, 768:1668], late[:, 3200:4100]
        csb, ctb, cpx = uvT[:, 1668:1668 + NC], uvT[0:NC, 1800:1928], uvT[0:NC, 1928:2056]
        cpg = uvT[0:NC, 2056:2088].rearrange("p (a q) -> p a q", a=4)
        crow, scrow = uvT[0:9, 0:D], uvT[0:9, D:2 * D]
        sgb = uvT[:, 0:2 * TOK].rearrange("p (s n) -> p s n", s=2)
        yt = uvT[:, 2 * TOK:2 * TOK + 1024].rearrange("p (s n) -> p s n", s=2)
        mem = sb("mem", 4 * TOK + 2048 + 7168)
        vTt = mem[:, 0:4 * TOK]
        vT = vTt.rearrange("p (f n) -> p f n", f=4)
        stc = vTt[0:16, 0:512]
        att = mem[:, 4 * TOK + 2048:]
        w1v = att[:, 0:2048].rearrange("p (x j r h) -> p x j r h", x=2, j=8, r=2)
        qTp = att[:, 0:2048].rearrange("p (g n) -> p g n", g=4)
        gbc = att[:, 5120:7168].rearrange("p (s n) -> p s n", s=2)
        qblk = att[:, 2048:2560]
        kTp = att[:, 2560:3584].rearrange("p (x n) -> p x n", x=2)
        kTn = att[:, 3584:3712].rearrange("p (x n) -> p x n", x=2)
        kcm = att[:, 3712:4864].rearrange("p (b n) -> p b n", b=9)
        vcm = att[:, 4864:6016].rearrange("p (b n) -> p b n", b=9)
        kcT = att[:, 6016:7168].rearrange("p (b n) -> p b n", b=9)
        rows2 = sb("rows2", 2048, parts=41)
        grow, modss2 = rows2[0:9, :], rows2[32:41, :]
        rowb = sb("rowb", 128, parts=52)
        winb = mem[:, 4 * TOK:4 * TOK + 2048]
        wnd = winb.rearrange("p (x b n) -> p x b n", x=2, b=2)
        w2 = sb("w2", 128, parts=64)
        colT = sb("colT", 52)
        cT = sb("cT", 72)
        stT = sb("stT", 64)
        modt = sb("modt", 288)
        mod = modt[:, :].rearrange("p (l x k b) -> p l x k b", l=2, x=2, k=8)
        gains = sb("gains", 256)
        ulast = sb("ulast", 72)
        gat = sb("gat", 120)
        gate = gat[:, :].rearrange("p (t h c) -> p t h c", t=5, h=8)
        small = sb("small", 256)
        selb = sb("selb", 512)
        sel32 = sb("sel32", 32)
        imps = sb("imps", NC1)
        slv = late[0:64, 3072:3584]
        half = slv[:, 0:2 * NC].rearrange("p (k n) -> p k n", k=2)
        slu = slv[:, 256:256 + 2 * NC].rearrange("p (k n) -> p k n", k=2)
        orows = uvT[:, 0:4 * 192]
        orow = orows[:, :].rearrange("p (g c n) -> p g c n", g=4, c=3)
        pti = sb("pti", 8, I32)
        idx = sb("idx", 8, U32)
        pebt = sb("pebt", 2, parts=64)
        pct = sb("pct", 8 * PNC)
        pcp = pct[:, :].rearrange("p (h n) -> p h n", h=8)
        epst = sb("epst", 1)
        ident = cst[:, C_ID:C_ID + 128]
        ws = pairs_at("ws", mem, 0, 8192)[:, :].rearrange("p (s x n) -> p s x n", s=2, x=2)
        hhi = pairs_at("hhi", hbuf, 0, 8 * TOK)[:, :].rearrange("p (k n) -> p k n", k=8)
        hlo_at = [(k0, n, z[:, c0:c0 + n * TOK].rearrange("p (k n) -> p k n", k=n),
                   pairs_at(f"hlo{k0}", z, c0, n * TOK)[:, :].rearrange("p (k n) -> p k n", k=n))
                  for k0, n, z, c0 in ((0, 4, cst, C_ROPE), (4, 2, mem, 8192), (6, 2, proj, 5 * D))]
        hraw = [z[2][:, k] for z in hlo_at for k in range(z[1])]
        hlo = [z[3][:, k] for z in hlo_at for k in range(z[1])]
        o_rows = nc.dram_tensor("o_rows", [NB, NH, NQ, 192], F32).ap()

        consts_loaded, gains_loaded, c_loaded, comp_w_loaded, bias_loaded, conv_state_loaded, pages_loaded = (
            sem(n) for n in ("consts_loaded", "gains_loaded", "c_loaded", "comp_w_loaded", "bias_loaded",
                             "conv_state_loaded", "pages_loaded"))
        x_loaded = [sem(f"x_loaded{t}") for t in range(5)]
        w_loaded = [sem(f"w_loaded{i}") for i in range(WR)]
        cache_loaded = [sem(f"cache_loaded{i}") for i in range(CR)]
        win_loaded = [sem(f"win_loaded{i}") for i in range(2)]
        xin_loaded, rows_back, rows_out, stored, kvc_stored = (
            sem(n) for n in ("xin_loaded", "rows_back", "rows_out", "stored", "kvc_stored"))
        dve_step, act_step = sem("dve_step"), sem("act_step")
        (cleared, scrow_ready, x_square, x_root, xn_ready, idx_ready, hT_ready, u_end_ready, y_ready, y_square, y_inv,
         vT_ready, v_scaled, half_ready, pre_ready, silu_ready, nrm_square, nrm_root, nrm_done, gate_exp, gates_ready,
         c_exp, c_prob, c_group, sel_ready, s_min, s_exp, o_row, p_in, p_exp, p_prob, p_soft, attn_ready, a_square,
         a_root, a_ready, x1_ready, x1_square, x1_root, x1n_ready, dn_read, out_ready, hi_ready, lo_ready,
         h_low, h_high, h_low2) = (sem(n) for n in (
            "cleared scrow_ready x_square x_root xn_ready idx_ready hT_ready u_end_ready y_ready y_square y_inv "
            "vT_ready v_scaled half_ready pre_ready silu_ready nrm_square nrm_root nrm_done gate_exp gates_ready "
            "c_exp c_prob c_group sel_ready s_min s_exp o_row p_in p_exp p_prob p_soft attn_ready a_square "
            "a_root a_ready x1_ready x1_square x1_root x1n_ready dn_read out_ready hi_ready lo_ready h_low h_high h_low2").split())

        def ps(key):
            return bank[at[key][0]]

        def want_free(eng, key):
            b, n = at[key]
            if n:
                eng.wait_ge(bank_free[b], n)

        def want_filled(eng, key):
            b, n = at[key]
            eng.wait_ge(bank_filled[b], n + 1)

        def want_emptied(eng, key):
            b, n = at[key]
            eng.wait_ge(bank_free[b], n + 1)

        def fills(ins, key):
            ins.then_inc(bank_filled[at[key][0]], 1)

        def frees(ins, key):
            ins.then_inc(bank_free[at[key][0]], 1)

        def loads_of(i):
            return 32 if chunks[i][0][0] == "gu" else 16

        def weights(pe, key):
            i = chunk_of[key]
            pe.wait_ge(w_loaded[i % WR], sum(loads_of(j) for j in range(i % WR, i + 1, WR)))
            return wch[:, i % WR]

        caches = [(("cache_k_cmp", "cache_v_cmp")[u % 2], u // 2, ("xt", u, 3)) for u in range(16)]
        caches += [("p_k_cmp", None, ("xt", 16, 3)), ("p_v_cmp", None, ("xt", 17, 3))]
        for gp in range(4):
            caches += [("cache_k_slc", 2 * gp + b, ("T", gp, 3, b)) for b in range(2)]
            caches += [("cache_v_slc", 2 * gp + b, ("O", gp, 0)) for b in range(2)]

        def cache(eng, i):
            eng.wait_ge(cache_loaded[i % CR], 16 * (i // CR + 1))
            return cring[:, i % CR, :].rearrange("p (s n) -> p s n", s=16)

        def tok_rows(name_p, name_s, t):
            return a[name_p][0, 128 * t:128 * t + 128, :] if t < 4 else a[name_s].rearrange("b q d -> (b q) d")

        def out_rows(name):
            return o[name].rearrange("l b (t p) k d -> p (l b t) (k d)", p=128)

        def high(copy, dst, src):
            return copy(dst, src)

        def low(eng, dst, src, hi):
            return eng.tensor_tensor(dst, src, hi.bitcast(F32), ALU.subtract)

        def reads_job(j):
            if j < NFT:
                return lambda eng: want_filled(eng, ("gu", j, 1, 1))
            n, kc = divmod(j - NFT, 6)
            return (lambda eng: eng.wait_ge(dn_read, 5 * n + kc + 1)) if kc < 5 else (
                lambda eng: want_filled(eng, ("dn", n, 4)))

        def job_parts(j):
            hi, lo = ws[:, j % 2, 0], ws[:, j % 2, 1]
            if j < NFT:
                parts = []
                for kh in range(2):
                    raw = wch[:, chunk_of["gu", j // 2, kh] % WR].rearrange("p k (x m c) -> p k x m c", x=2, m=2)[:, :, :, j % 2]
                    parts.append([raw] + [z[:, 1024 * kh:1024 * kh + 1024].rearrange("p (k x c) -> p k x c", k=4, x=2)
                                          for z in (hi, lo)])
                return parts
            n, kc = divmod(j - NFT, 6)
            nk = 4 if kc < 5 else NFT - 20
            return [[wch[:, chunk_of["dn", n, kc] % WR, 0:nk]] +
                    [z[:, 0:512 * nk].rearrange("p (k c) -> p k c", k=nk) for z in (hi, lo)]]

        def job_acts(j):
            kc = (j - NFT) % 6
            nk = 4 if kc < 5 else NFT - 20
            raw = actT[:, 4 * kc:4 * kc + nk]
            if j % 2 == 0:
                return [[raw, hhi[:, 0:nk], hhi[:, 4:4 + nk]]]
            z = hlo_at[0][3]
            parts = [[raw[:, 0:2], z[:, 0:2], hlo_at[1][3]]]
            return parts + ([[raw[:, 2:4], z[:, 2:4], hlo_at[2][3]]] if nk == 4 else [])

        def act_pairs(j):
            return [(p[1][:, k], p[2][:, k]) for p in job_acts(j) for k in range(p[0].shape[1])]

        block = ctx.enter_context(nc.Block())

        @block.sync
        def _(sp):
            for t in range(5):
                sp.dma_start(xs[0:TM[t], t, :], tok_rows("x_prompt", "x_sample", t)).then_inc(x_loaded[t], 16)
            for dst, c0, w in ((modss[:, 0:2048], 0, 2048), (modss2, 3 * D, 2048),
                               (grow[:, 0:D], 2 * D, D), (grow[:, D:2 * D], 5 * D, D)):
                sp.dma_start(dst, a["b_ada"][0:1, c0:c0 + w].to_broadcast([9, w])).then_inc(bias_loaded, 16)

            def load(i):
                if i >= WR:
                    (kind, n, kh), last = chunks[i - WR]
                    if kind == "gu":
                        sp.wait_ge(lo_ready, 2 * n + 2)
                    elif kind == "dn":
                        sp.wait_ge(lo_ready, NFT + 6 * n + kh + 1)
                    else:
                        want_filled(sp, last)
                (kind, n, kh), _ = chunks[i]
                dst, k0, nk, w = wch[:, i % WR], 512 * kh, 4, 512
                if kind == "gu":
                    for x in range(2):
                        c0 = x * NF + 256 * n
                        sp.dma_start(dst[:, :, 256 * x:256 * x + 256],
                                     a["w_gu"][0, k0:k0 + 512, c0:c0 + 256].rearrange("(k p) n -> p k n", p=128)
                                     ).then_inc(w_loaded[i % WR], 16)
                    return
                src, c0 = a[{"ada": "w_ada", "in": "w_in", "cv": "w_in", "wo": "w_o", "dn": "w_down"}[kind]], 512 * n
                if kind == "in":
                    w = min(512, TEND - c0)
                if kind == "cv":
                    c0 = TEND + 512 * (0, 2, 1)[n]
                if kind == "dn" and kh == 5:
                    nk = NFT - 20
                sp.dma_start(dst[:, 0:nk, 0:w],
                             src[0, k0:k0 + 128 * nk, c0:c0 + w].rearrange("(k p) n -> p k n", p=128)
                             ).then_inc(w_loaded[i % WR], 16)

            done = chunk_of["ada", ADA_FIRST, 0]
            for i in range(done):
                load(i)
            count = 0

            def store(dst, src):
                sp.dma_start(dst, src).then_inc(stored, 16)
                return 1

            for t in range(5):
                want_emptied(sp, ("in", 1, t))
            for c0, name in ((TKC, "p_k_cmp"), (TVC, "p_v_cmp")):
                sp.dma_start(out_rows(name), pj[:, 0:4, c0:c0 + 128]).then_inc(kvc_stored, 16)
            for c0, name in ((TKC, "s_k_cmp"), (TVC, "s_v_cmp"), (TVS, "s_v_slc")):
                count += store(o[name].rearrange("l b q k d -> (l b q) (k d)"), pj[0:TS, 4, c0:c0 + 128])
            count += store(out_rows("p_v_slc"), pj[:, 0:4, TVS:TVS + 128])
            for t in range(5):
                want_emptied(sp, ("in", 2, t))
            count += store(out_rows("p_v_win"), pj[:, 0:4, TVW:TVW + 128])
            for w in ("k", "v"):
                count += store(o[f"s_{w}_win"][0, :, 0:SEQ - NQ].rearrange("b t k d -> b (t k d)"),
                               a[f"state_{w}_win"][0, :, NQ:SEQ].rearrange("b t k d -> b (t k d)"))
            for b in range(NB):
                count += store(o["s_v_win"][0, b, SEQ - NQ:SEQ].rearrange("q k d -> q (k d)"),
                               pj[NQ * b:NQ * b + NQ, 4, TVW:TVW + 128])
            sp.wait_ge(nrm_done, 6)
            for c0, name in ((TKS, "p_k_slc"), (TKW, "p_k_win")):
                count += store(out_rows(name), pj[:, 0:4, c0:c0 + 128])
            count += store(o["s_k_slc"].rearrange("l b q k d -> (l b q) (k d)"), pj[0:TS, 4, TKS:TKS + 128])
            for b in range(NB):
                count += store(o["s_k_win"][0, b, SEQ - NQ:SEQ].rearrange("q k d -> q (k d)"),
                               pj[NQ * b:NQ * b + NQ, 4, TKW:TKW + 128])
            want_emptied(sp, ("ulast",))
            count += store(o["p_conv"].rearrange("l b r f -> (l b r) f"), ulr[0:2, :])
            count += store(o["s_conv"].rearrange("l b r f -> (l b r) f"), ulr[2:18, :])
            assert count == N_STORED
            for i in range(done, done + WR):
                load(i)
            for gp in range(4):
                sp.wait_ge(o_row, gp + 1)
                sp.dma_start(o_rows[2 * gp:2 * gp + 2].rearrange("b h q n -> (b h q) n"),
                             orows[:, 192 * gp:192 * gp + 192]).then_inc(rows_out, 16)
            sp.wait_ge(rows_out, 64)
            for b in range(NB):
                sp.dma_start(late[NQ * b:NQ * b + NQ, 0:1536].rearrange("q (h n) -> q h n", h=8),
                             o_rows[b].rearrange("h q n -> q h n")).then_inc(rows_back, 16)
            want_filled(sp, ("O", 3, 1))
            for t in range(5):
                sp.dma_start(xin[0:TM[t], t, :], tok_rows("x_prompt", "x_sample", t)).then_inc(xin_loaded, 16)
            for i in range(done + WR, len(chunks)):
                load(i)
            for n in range(2):
                for t in range(5):
                    sp.wait_ge(out_ready, 5 * n + t + 1)
                    dst = o["y_prompt"][0, 128 * t:128 * t + 128, :] if t < 4 else o["y_sample"].rearrange("b q d -> (b q) d")
                    count += store(dst[:, 512 * n:512 * n + 512], xs[0:TM[t], t, 512 * n:512 * n + 512])
            sp.wait_ge(kvc_stored, 32)
            sp.wait_ge(stored, 16 * count)

        @block.gpsimd
        def _(pool):
            for b in range(NB):
                pt = a["page_table"]
                pool.dma_start(pti[:, b:b + 1], bass.AP(pt.tensor, 16 * b, [[1, 16], [0, 8], [1, 1]])).then_inc(pages_loaded, 16)
            pool.wait_ge(idx_ready, 1)
            loaded = 0

            def window(gp, x):
                if gp:
                    want_filled(pool, (("T", gp - 1, 4, 1), ("O", gp - 1, 1))[x])
                for b in range(2):
                    pool.dma_start(wnd[:, x, b, :],
                                   a[f"state_{'kv'[x]}_win"][0, 2 * gp + b].rearrange("(c s) k d -> c (s k d)", s=4)
                                   ).then_inc(win_loaded[x], 16)

            for i, (name, b, last) in enumerate(caches):
                if i >= CR:
                    want_filled(pool, caches[i - CR][2])
                slot = cring[:, i % CR, :]
                if b is None:
                    pool.wait_ge(kvc_stored, 32)
                    pool.dma_start(slot[0:PCH, :], o[name].rearrange("l b (c s) k d -> (l b c) (s k d)", s=16)
                                   ).then_inc(cache_loaded[i % CR], 16)
                else:
                    pool.indirect_dma_start(slot, None, a[name].rearrange("l n (c s) k d -> (l n c) (s k d)", s=16),
                                            bass.IndirectOffsetOnAxis(idx[:, b:b + 1], 0)).then_inc(cache_loaded[i % CR], 16)
                if i >= 18 and i % 2 == 1:
                    window((i - 18) // 4, (i - 18) % 4 // 2)
            for t in range(4):
                pool.wait_ge(h_high, t + 1)
                cols = slice(128 * t, 128 * t + 128)
                for k0, n, z, zl in hlo_at[1:]:
                    ins = low(pool, zl[:, :, cols], z[:, :, cols], hhi[:, k0:k0 + n, cols])
                ins.then_inc(h_low2, 1)

        def spread_chunks(copy, u, i, n):
            key = ("xt", u, i)
            for k in range(2):
                ins = copy(xcmp[64 * (i % 2):64 * (i % 2) + 64, u % 2, 4 * (i // 2):4 * (i // 2) + 4, k, 0:n],
                           ps(key)[64 * k:64 * k + 64, :].rearrange("p (j c) -> p j c", j=4)[:, :, 0:n])
            frees(ins, key)


        @block.scalar
        def _(act):
            steps = [0]

            def link(ins):
                steps[0] += 1
                ins.then_inc(act_step, 1)
                act.wait_ge(act_step, steps[0])

            act.dma_start(cst[:, :], a["consts"]).then_inc(consts_loaded, 16)
            act.dma_start(crow[0:1, :], a["c_prompt"]).then_inc(c_loaded, 16)
            act.dma_start(crow[1:9, :], a["c_sample"]).then_inc(c_loaded, 16)
            r0 = 0
            for name, n in (("ln1_g", 8), ("ln2_g", 8), ("attn_out_g", 4), ("conv_out_g", 4)):
                act.dma_start(rowb[r0:r0 + n, :], a[name].rearrange("l (k p) -> (l k) p", p=128)).then_inc(gains_loaded, 16)
                r0 += n
            act.dma_start(rowb[24:36, :], a["w_conv"].rearrange("l w (k p) -> (l w k) p", p=128)).then_inc(gains_loaded, 16)
            act.dma_start(rowb[36:52, :], a["pe_cmp"].rearrange("l (k s) d -> (l k) (s d)", s=2)).then_inc(gains_loaded, 16)
            act.dma_start(gains[:, 0:64], a["q_norm_g"].to_broadcast([128, 64])).then_inc(gains_loaded, 16)
            for i in range(3):
                act.dma_start(gains[:, 64 + 64 * i:128 + 64 * i], a["k_norm_g"][0, i:i + 1, :].to_broadcast([128, 64])
                              ).then_inc(gains_loaded, 16)
            act.dma_start(stc, a["state_conv"].rearrange("l b r f -> (l b r) f")).then_inc(conv_state_loaded, 16)
            for x, w in enumerate(("w_ck1", "w_cv1")):
                for r in range(2):
                    act.dma_start(w1v[:, x, :, r, :], a[w][0, 1024 * r:1024 * r + 1024, :].rearrange("(j p) h -> p j h", p=128)
                                  ).then_inc(comp_w_loaded, 16)
            for x, w in enumerate(("w_ck2", "w_cv2")):
                act.dma_start(w2[:, 64 * x:64 * x + 64], a[w][0]).then_inc(comp_w_loaded, 16)

            act.wait_ge(c_loaded, 32)
            act.activation(scrow, crow, ACT.Silu).then_inc(scrow_ready, 1)
            act.wait_ge(cleared, 1)
            for t in range(5):
                act.wait_ge(x_loaded[t], 16)
                if t:
                    act.wait_ge(x_square, t)
                act.activation(hbuf[0:TM[t], 0:D], xs[0:TM[t], t, :], ACT.Square, accum_out=small[0:TM[t], t:t + 1]
                               ).then_inc(x_square, 1)
            act.wait_ge(x_square, 5)
            act.activation(small[:, 8:13], small[:, 0:5], ACT.Sqrt, bias=epst[:, 0:1], scale=1.0 / D).then_inc(x_root, 1)
            for t in range(5):
                want_filled(act, ("xT", t, 1))
                frees(act.copy(hT[:, 4:8, 128 * t:128 * t + TM[t]],
                               ps(("xT", t, 1))[:, 0:4 * TM[t]].rearrange("p (k n) -> p k n", k=4)), ("xT", t, 1))
            for n in range(3):
                if n == 1:
                    continue
                w = min(512, TEND - 512 * n)
                for t in range(5):
                    want_filled(act, ("in", n, t))
                    dst, src = pj[0:TM[t], t, 512 * n:512 * n + w], ps(("in", n, t))[0:TM[t], 0:w]
                    if n == 0:
                        dst = dst.rearrange("p (g k d) -> p g k d", g=4, k=2)
                        src = src.rearrange("p (k g d) -> p g k d", k=2, g=4)
                    frees(act.copy(dst, src), ("in", n, t))
            for m in range(4):
                for h in range(2):
                    want_filled(act, ("cv", 0, m, h))
                    frees(act.copy(hcT[:, m, HALF * h:HALF * h + HALF], ps(("cv", 0, m, h))[:, 0:HALF]), ("cv", 0, m, h))
            for m in range(4):
                act.wait_ge(y_ready, m + 1)
                act.activation(hcT[:, m, :], vT[:, m, :], ACT.Square).then_inc(y_square, 1)
            want_filled(act, ("ulast",))
            frees(act.copy(ulr, ps(("ulast",))[0:18, :]), ("ulast",))
            for h in range(2):
                want_filled(act, ("yss", h))
                frees(act.activation(yrs[:, HALF * h:HALF * h + HALF], ps(("yss", h))[:, 0:HALF], ACT.Sqrt,
                                     bias=epst[:, 0:1], scale=1.0 / 512), ("yss", h))

            def nrm(i):
                act.wait_ge(nrm_square, i + 1)
                P, n = NORMS[i][1], NORMS[i][2]
                act.activation(small[0:P, 64:64 + n], small[0:P, 32:32 + n], ACT.Sqrt, bias=epst[0:P, 0:1], scale=1.0 / HD
                               ).then_inc(nrm_root, 1)

            def spread(u):
                for i in (0, 2):
                    if u >= 2:
                        want_filled(act, ("pre", u - 2))
                    want_filled(act, ("xt", u, i))
                    spread_chunks(act.copy, u, i, CH if u < 16 else PCH)

            spread(0)
            for u in range(18):
                n, m = (CH, NC) if u < 16 else (PCH, PNC)
                if u < 17:
                    spread(u + 1)
                if u in NORM_AT:
                    nrm(NORM_AT.index(u))
                want_filled(act, ("pre", u))
                if u:
                    act.wait_ge(silu_ready, u)
                act.copy(half[:, :, 0:m], ps(("pre", u))[64:128, 0:2 * n].rearrange("p (k c) -> p k c", k=2)[:, :, 1:n]
                         ).then_inc(half_ready, 1)
                want_emptied(act, ("pre", u))
                if u:
                    want_filled(act, ("cmp", u - 1))
                x = u % 2
                act.activation(slu[:, :, 0:m], half[:, :, 0:m], ACT.Silu, bias=pebt[:, x:x + 1]).then_inc(silu_ready, 1)
            for g in range(G):
                want_filled(act, ("qT", g, 0))
                frees(act.copy(qTp[:, g, :], ps(("qT", g, 0))[:, :]), ("qT", g, 0))
            for x in range(2):
                want_filled(act, ("kT", x))
                frees(act.copy(kTp[:, x, :], ps(("kT", x))[:, :]), ("kT", x))
            nrm(8)
            act.activation(gat[:, 0:96].rearrange("p (t n) -> p t n", t=4), pj[:, 0:4, TG:TEND], ACT.Exp, scale=-1.0).then_inc(gate_exp, 1)
            act.activation(gat[0:TS, 96:120], pj[0:TS, 4, TG:TEND], ACT.Exp, scale=-1.0).then_inc(gate_exp, 1)
            for i in range(3):
                want_filled(act, ("kct", i))
                nb, m = (4, NC) if i < 2 else (1, PNC)
                frees(act.copy(kcT[:, 4 * i:4 * i + nb, 0:m],
                               ps(("kct", i))[:, :].rearrange("p (b n) -> p b n", b=4)[:, 0:nb, 0:m]), ("kct", i))

            def cmp_exp(gp):
                want_emptied(act, ("cS", gp))
                act.activation(csb, csb, ACT.Exp, bias=small[:, 100:101], scale=-1.0, accum_out=small[:, 101:102]).then_inc(c_exp, 1)

            def cmp_turned(gp):
                want_filled(act, ("cPT", gp))
                if gp:
                    want_filled(act, ("cO", gp - 1))
                frees(act.copy(ctb, ps(("cPT", gp))[0:NC, 0:128]), ("cPT", gp))

            def cmp_rows(gp):
                want_filled(act, ("cO", gp))
                for i in range(4):
                    r = slice(32 * i, 32 * i + 32)
                    ins = act.copy(orow[r, gp, 0, :], ps(("cO", gp))[r, 64 * (i % 2):64 * (i % 2) + 64])
                frees(ins, ("cO", gp))

            def key_part(gp, c):
                want_filled(act, ("T", gp, c, 0))
                if c >= 2:
                    want_filled(act, ("S", gp, c - 2))
                elif gp:
                    want_filled(act, ("S", gp - 1, c + 3))
                frees(act.copy(kTc[:, 0, c % 2, :], ps(("T", gp, c, 0))[:, :]), ("T", gp, c, 0))

            cmp_exp(0)
            key_part(0, 0)
            cmp_turned(0)
            key_part(0, 1)
            cmp_rows(0)
            for gp in range(4):
                more = gp < 3
                key_part(gp, 2)
                if more:
                    cmp_exp(gp + 1)
                key_part(gp, 3)
                key_part(gp, 4)
                if more:
                    cmp_turned(gp + 1)
                act.wait_ge(s_min, gp + 1)
                act.activation(ssb, ssb, ACT.Exp, bias=small[:, 112:113], scale=-1.0, accum_out=small[:, 114:115]).then_inc(s_exp, 1)
                act.activation(wsb, wsb, ACT.Exp, bias=small[:, 113:114], scale=-1.0, accum_out=small[:, 115:116]).then_inc(s_exp, 1)
                if more:
                    key_part(gp + 1, 0)
                    key_part(gp + 1, 1)
                for i in (0, 2, 4):
                    want_filled(act, ("PT", gp, i))
                    dst = pTw if i == 4 else pT[:, 4 * i:4 * i + 4, :]
                    frees(act.copy(dst, ps(("PT", gp, i))[:, :].rearrange("p (s n) -> p s n", s=4)), ("PT", gp, i))
                if more:
                    cmp_rows(gp + 1)
            for t in range(4):
                act.wait_ge(p_in, t + 1)
                act.activation(pct[:, :], pct[:, :], ACT.Exp, scale=QS).then_inc(p_exp, 1)
                for hh in range(2):
                    want_filled(act, ("pcPT", t, hh))
                    frees(act.copy(ppTc[:, 4 * hh:4 * hh + 4, :],
                                   ps(("pcPT", t, hh))[0:PNC, :].rearrange("p (h n) -> p h n", h=4)), ("pcPT", t, hh))
                for br in range(2):
                    for i in range(NH + 1):
                        if i < NH:
                            want_emptied(act, ("pS", t, br, i))
                            w = 128 * (t + 1)
                            c0 = 128 + 8 * br + i
                            act.activation(psb[:, i % 2, 0:w], psb[:, i % 2, 0:w], ACT.Exp, bias=small[:, 144 + i:145 + i],
                                           scale=-1.0, accum_out=small[:, c0:c0 + 1]).then_inc(p_soft, 1)
                        if i:
                            want_filled(act, ("pPT", t, br, i - 1))
                            frees(act.copy(ppT[:, (i - 1) % 2, 0:t + 1, :],
                                           ps(("pPT", t, br, i - 1))[:, 0:128 * (t + 1)].rearrange("p (k n) -> p k n", n=128)),
                                  ("pPT", t, br, i - 1))
            for t in range(5):
                act.wait_ge(attn_ready, t + 1)
                if t:
                    act.wait_ge(a_square, t)
                act.activation(psb[0:TM[t], 0, :], pj[0:TM[t], t, 0:512], ACT.Square, accum_out=small[0:TM[t], t:t + 1]
                               ).then_inc(a_square, 1)
            act.wait_ge(a_square, 5)
            act.activation(small[:, 8:13], small[:, 0:5], ACT.Sqrt, bias=epst[:, 0:1], scale=1.0 / 512).then_inc(a_root, 1)

            def gates_rows(l):
                for n in range(2):
                    for s in range(2):
                        P = 128 if s == 0 else TS
                        want_filled(act, ("gate", l, n, s))
                        frees(act.copy(gbc[0:P, s, 512 * n:512 * n + 512], ps(("gate", l, n, s))[0:P, :]), ("gate", l, n, s))

            gates_rows(0)
            def second_half(t):
                want_filled(act, ("hT", t, 1))
                cols = slice(128 * t, 128 * t + 128)
                for k in range(4, 8):
                    ins = act.activation(hraw[k][:, cols], ps(("hT", t, 1))[:, 128 * (k - 4):128 * (k - 3)],
                                         ACT.Identity, bias=mod[:, 1, 1, k, 0:1], scale=mod[:, 1, 0, k, 0:1])
                frees(ins, ("hT", t, 1))
                want_emptied(act, ("hT", t, 1))
                for k0, n, z, _ in hlo_at[1:]:
                    ins = high(act.copy, hhi[:, k0:k0 + n, cols], z[:, :, cols])
                ins.then_inc(h_high, 1)

            def high_job(j):
                if j >= 2:
                    reads_job(j - 2)(act)
                keys = [("gu", j // 2, kh) for kh in range(2)] if j < NFT else [("dn",) + divmod(j - NFT, 6)]
                for key, (raw, hi, lo) in zip(keys, job_parts(j)):
                    weights(act, key)
                    ins = high(act.copy, hi, raw)
                if j >= NFT:
                    kc = (j - NFT) % 6
                    if j < NFT + 2:
                        want_filled(act, ("gu", NFT - 1, 1, 1))
                    for k in range(4 * kc, min(4 * kc + 4, NFT)):
                        for h in range(2):
                            want_emptied(act, ("gu", k, 1, h))
                    for raw, hi, lo in job_acts(j):
                        ins = high(act.copy, hi, raw)
                ins.then_inc(hi_ready, 1)

            for t in range(6):
                if t < 5:
                    act.wait_ge(x1_ready, 5 + t + 1)
                    if t:
                        act.wait_ge(x1_square, t)
                    act.activation(late[0:TM[t], 0:D], xs[0:TM[t], t, :], ACT.Square, accum_out=small[0:TM[t], 16 + t:17 + t]
                                   ).then_inc(x1_square, 1)
                    act.wait_ge(x1_square, t + 1)
                    act.activation(small[0:TM[t], 24 + t:25 + t], small[0:TM[t], 16 + t:17 + t], ACT.Sqrt,
                                   bias=epst[0:TM[t], 0:1], scale=1.0 / D).then_inc(x1_root, 1)
                if 1 <= t < 5:
                    second_half(t - 1)
            want_filled(act, ("wo", 1, 4))
            high_job(0)
            high_job(1)
            for i, h in GU_ORDER:
                want_filled(act, ("gu", i, 0, h))
                if i >= 2:
                    want_emptied(act, ("gu", i - 2, 1, h))
                frees(act.activation(sgb[:, i % 2, HALF * h:HALF * h + HALF], ps(("gu", i, 0, h))[:, 0:HALF], ACT.Silu),
                      ("gu", i, 0, h))
                if (i, h) == GATE_AT:
                    gates_rows(1)
                if (i, h) == (1, 1) or i > 1 and h == 0:
                    high_job(i + 1)
            for j in range(NFT + 1, NFT + 12):
                high_job(j)

        @block.vector
        def _(dve):
            steps = [0]

            def link(ins):
                steps[0] += 1
                ins.then_inc(dve_step, 1)
                dve.wait_ge(dve_step, steps[0])

            link(dve.memset(epst[:, :], EPS))
            link(dve.memset(small[:, :], 1.0))
            link(dve.memset(sel32[:, :], 0.0))
            dve.memset(qblk, 0.0).then_inc(cleared, 1)
            dve.wait_ge(cleared, 1)
            dve.wait_ge(consts_loaded, 16)
            dve.wait_ge(pages_loaded, 128)
            dve.scalar_tensor_tensor(idx[:, :], pti[:, :], 8.0, cst[:, C_P8:C_P8 + 1].to_broadcast([128, 8]), ALU.mult, ALU.add
                                     ).then_inc(idx_ready, 1)

            def evac(key, dst, src):
                want_filled(dve, key)
                frees(dve.tensor_copy(dst, src), key)

            evac(("rows",), colT[:, :], ps(("rows",))[:, 0:52])
            evac(("cT",), cT[:, :], ps(("cT",))[:, 0:72])
            evac(("sconv",), stT[:, :], ps(("sconv",))[:, 0:64])
            dve.wait_ge(x_root, 1)
            link(dve.reciprocal(small[:, 16:21], small[:, 8:13]))
            for t in range(5):
                dve.tensor_scalar(xs[0:TM[t], t, :], xs[0:TM[t], t, :], small[0:TM[t], 16 + t:17 + t], None, ALU.mult
                                  ).then_inc(xn_ready, 1)
            for t in range(5):
                evac(("xT", t, 0), hT[:, 0:4, 128 * t:128 * t + TM[t]],
                     ps(("xT", t, 0))[:, 0:4 * TM[t]].rearrange("p (k n) -> p k n", k=4))
            for x in range(2):
                evac(("peb", x), pebt[:, x:x + 1], ps(("peb", x))[0:64, 0:1])

            dve.wait_ge(bias_loaded, 64)

            def mod_cols(l):
                key = ("mod", l)
                want_filled(dve, key)
                v = ps(key)[:, 0:144].rearrange("p (x k b) -> p x k b", x=2, k=8)
                link(dve.tensor_copy(mod[:, l, 1], v[:, 0]))
                frees(dve.scalar_tensor_tensor(mod[:, l, 0], v[:, 1], 1.0,
                                               colT[:, 8 * l:8 * l + 8].unsqueeze(2).to_broadcast([128, 8, 9]),
                                               ALU.add, ALU.mult), key)

            def ada_rows(n):
                tensor, c0 = (modss, modss, grow, modss2, modss2, grow)[n // 2], 512 * n - (0, 0, 2048, 3072, 3072, 4096)[n // 2]
                dst = tensor[:, c0:c0 + 512]
                want_filled(dve, ("ada", n))
                frees(dve.tensor_tensor(dst, ps(("ada", n))[0:9, :], dst, ALU.add), ("ada", n))

            for n in range(ADA_FIRST):
                ada_rows(n)
                if n == 3:
                    mod_cols(0)
                    for t in range(5):
                        want_emptied(dve, ("xT", t, 0))
                        want_emptied(dve, ("xT", t, 1))
                    want_emptied(dve, ("mod", 0))
                    sv = hT[:, :, SEQ:TOK].rearrange("p k (b q) -> p k b q", b=8)
                    link(dve.tensor_tensor(sv, sv, mod[:, 0, 0, :, 1:9].unsqueeze(3).to_broadcast([128, 8, 8, 8]), ALU.mult))
                    link(dve.tensor_tensor(sv, sv, mod[:, 0, 1, :, 1:9].unsqueeze(3).to_broadcast([128, 8, 8, 8]), ALU.add))
                    for k in range(8):
                        dve.tensor_scalar(hT[:, k, 0:SEQ], hT[:, k, 0:SEQ], mod[:, 0, 0, k, 0:1], mod[:, 0, 1, k, 0:1],
                                          ALU.mult, ALU.add).then_inc(hT_ready, 1)
            for t in range(5):
                evac(("in", 1, t), pj[0:TM[t], t, 512:1024], ps(("in", 1, t))[0:TM[t], :])

            def conv(m):
                w = [colT[:, 24 + 4 * k + m:25 + 4 * k + m] for k in range(3)]
                y, u = vT[:, m, :], uT[:, m, :]
                ys, us = (z[:, SEQ:TOK].rearrange("p (b q) -> p b q", b=8) for z in (y, u))
                st = stT[:, 16 * m:16 * m + 16].rearrange("p (b r) -> p b r", b=8)

                def tap(dst, src, k):
                    link(dve.scalar_tensor_tensor(dst, src, w[k], dst, ALU.mult, ALU.add))

                link(dve.tensor_scalar(y, u, w[2], None, ALU.mult))
                tap(y[:, 1:SEQ], u[:, 0:SEQ - 1], 1)
                tap(y[:, 2:SEQ], u[:, 0:SEQ - 2], 0)
                tap(ys[:, :, 1:8], us[:, :, 0:7], 1)
                tap(ys[:, :, 2:8], us[:, :, 0:6], 0)
                tap(ys[:, :, 0:1], st[:, :, 1:2], 1)
                tap(ys[:, :, 0:2], st, 0)

            for m in range(4):
                for h in range(2):
                    key = ("cv", 1, m, h)
                    want_filled(dve, key)
                    want_emptied(dve, ("cv", 0, m, h))
                    frees(dve.tensor_tensor(uT[:, m, HALF * h:HALF * h + HALF], ps(key)[:, 0:HALF],
                                            hcT[:, m, HALF * h:HALF * h + HALF], ALU.mult), key)
                want_emptied(dve, ("cv", 1, m, 0))
                want_emptied(dve, ("cv", 1, m, 1))
                conv(m)
            ul = ulast[:, :].rearrange("p (m c) -> p m c", m=4)
            link(dve.tensor_copy(ul[:, :, 0:2], uT[:, :, SEQ - 2:SEQ]))
            for m in range(4):
                dve.tensor_copy(ul[:, m, 2:18].rearrange("p (b r) -> p b r", b=8),
                                uT[:, m, SEQ:TOK].rearrange("p (b q) -> p b q", b=8)[:, :, 6:8]).then_inc(u_end_ready, 1)
            for m in range(4):
                for h in range(2):
                    key = ("cv", 2, m, h)
                    want_filled(dve, key)
                    y = vT[:, m, HALF * h:HALF * h + HALF]
                    frees(dve.tensor_tensor(y, ps(key)[:, 0:HALF], y, ALU.mult), key)
                want_emptied(dve, ("cv", 2, m, 1))
                dve.tensor_copy(small[:, 250:251], vT[:, m, 0:1]).then_inc(y_ready, 1)
                dve.wait_ge(y_ready, m + 1)
            want_emptied(dve, ("yss", 0))
            want_emptied(dve, ("yss", 1))
            link(dve.reciprocal(yrs, yrs))
            for m in range(4):
                dve.scalar_tensor_tensor(vT[:, m, :], vT[:, m, :], colT[:, 20 + m:21 + m], yrs, ALU.mult, ALU.mult
                                         ).then_inc(vT_ready, 1)
            dve.wait_ge(vT_ready, 4)

            def norm_rope(i):
                name, P, n, t0, nt, nh, gain = NORMS[i]
                if name == "kcm":
                    for b in range(t0, t0 + nt):
                        want_emptied(dve, ("cmp", 2 * b))
                    v = kcm[0:P, t0:t0 + nt, :]
                else:
                    for t in range(t0, t0 + nt):
                        want_emptied(dve, ("in", {"q": 0, "ks": 1, "kw": 2}[name], t))
                    c0 = {"q": TQ, "ks": TKS, "kw": TKW}[name]
                    v = pj[0:P, t0:t0 + nt, c0:c0 + 64 * nh]
                v = v.rearrange("p t (h d) -> p t h d", h=nh)
                q = sqb[0:P, 0:64 * n].rearrange("p (t h d) -> p t h d", t=nt, h=nh)
                link(dve.tensor_tensor(q, v, v, ALU.mult))
                dve.tensor_reduce(small[0:P, 32:32 + n], q, AX, ALU.add).then_inc(nrm_square, 1)
                dve.wait_ge(nrm_root, i + 1)
                link(dve.reciprocal(small[0:P, 32:32 + n], small[0:P, 64:64 + n]))
                rs = small[0:P, 32:32 + n].rearrange("p (t h) -> p t h", t=nt).unsqueeze(3).to_broadcast([P, nt, nh, 64])
                link(dve.tensor_tensor(v, v, rs, ALU.mult))
                gn = gains[0:P, 64 * gain:64 * gain + 64].unsqueeze(1).unsqueeze(1).to_broadcast([P, nt, nh, 64])
                link(dve.tensor_tensor(v, v, gn, ALU.mult))
                if name == "kcm":
                    cs = cst[0:P, C_ROPEC:C_ROPEC + 16].unsqueeze(1).to_broadcast([P, nt, 16])
                else:
                    cs = cst[0:P, C_ROPE + 16 * t0:C_ROPE + 16 * (t0 + nt)].rearrange("p (t c) -> p t c", t=nt)
                cos, sin = (cs[:, :, x:x + 8].unsqueeze(2).to_broadcast([P, nt, nh, 8]) for x in (0, 8))
                x1, x2 = v[:, :, :, 0:8], v[:, :, :, 8:16]
                r = [ropb[0:P, 256 * j:256 * j + 8 * n].rearrange("p (t h d) -> p t h d", t=nt, h=nh) for j in range(4)]
                dve.tensor_tensor(r[0], x1, cos, ALU.mult)
                dve.tensor_tensor(r[1], x2, sin, ALU.mult)
                dve.tensor_tensor(r[2], x2, cos, ALU.mult)
                link(dve.tensor_tensor(r[3], x1, sin, ALU.mult))
                dve.tensor_tensor(x1, r[0], r[1], ALU.subtract)
                dve.tensor_tensor(x2, r[2], r[3], ALU.add).then_inc(nrm_done, 1)
                dve.wait_ge(nrm_done, i + 1)

            def cmp_evac(u):
                b, x, m = u // 2, u % 2, (NC if u < 16 else PNC)
                evac(("cmp", u), (vcm if x else kcm)[0:m, b, :], ps(("cmp", u))[0:m, 0:128])

            def spread(u):
                for i in (1, 3):
                    if u >= 2:
                        want_filled(dve, ("pre", u - 2))
                    want_filled(dve, ("xt", u, i))
                    spread_chunks(dve.tensor_copy, u, i, CH if u < 16 else PCH)

            spread(0)
            for u in range(18):
                n, m = (CH, NC) if u < 16 else (PCH, PNC)
                if u < 17:
                    spread(u + 1)
                if u >= 2:
                    cmp_evac(u - 2)
                if u in NORM_AT:
                    norm_rope(NORM_AT.index(u))
                want_filled(dve, ("pre", u))
                dve.wait_ge(half_ready, u + 1)
                frees(dve.tensor_tensor(half[:, :, 0:m], half[:, :, 0:m],
                                        ps(("pre", u))[0:64, 0:2 * n].rearrange("p (k c) -> p k c", k=2)[:, :, 0:m], ALU.add),
                      ("pre", u))
            cmp_evac(16)
            cmp_evac(17)
            qv = qblk.rearrange("p (b k g q) -> p b k g q", b=8, k=2, g=4)
            for g in range(G):
                key = ("qT", g, 1)
                want_filled(dve, key)
                for k in range(2):
                    r = slice(64 * k, 64 * k + 64)
                    ins = dve.tensor_copy(qv[r, :, k, g, :], ps(key)[r, 0:TS].rearrange("p (b q) -> p b q", b=8))
                frees(ins, key)
            evac(("kTn",), kTn, ps(("kTn",))[:, 0:128].rearrange("p (x n) -> p x n", x=2))
            norm_rope(8)
            dve.wait_ge(gate_exp, 2)
            for z in (gat[:, 0:96], gat[0:TS, 96:120]):
                link(dve.tensor_scalar(z, z, 1.0, None, ALU.add))
                link(dve.reciprocal(z, z))
            def cmp_scores(gp):
                key = ("cS", gp)
                want_filled(dve, key)
                if gp:
                    want_filled(dve, ("cPT", gp - 1))
                frees(dve.tensor_tensor_reduce(csb, ps(key)[:, 0:NC], cst[:, C_CAUS:C_CAUS + NC], -QS, 3e38, ALU.add, ALU.min,
                                               small[:, 100:101]), key)

            def cmp_probs(gp):
                dve.wait_ge(c_exp, gp + 1)
                link(dve.reciprocal(small[:, 102:103], small[:, 101:102]))
                dve.tensor_scalar(csb, csb, small[:, 102:103], None, ALU.mult).then_inc(c_prob, 1)

            def cmp_groups(gp):
                want_emptied(dve, ("cPT", gp))
                link(dve.tensor_reduce(cpg, ctb.rearrange("p (a g q) -> p a q g", a=4, g=4), AX, ALU.add))
                dve.tensor_copy(cpx.rearrange("p (a g q) -> p a g q", a=4, g=4), cpg.unsqueeze(2).to_broadcast([NC, 4, 4, 8])
                                ).then_inc(c_group, 1)

            def cmp_importance(gp):
                evac(("imp", gp), imps[:, :], ps(("imp", gp))[:, 1:31])

            def cmp_select(gp):
                want_emptied(dve, ("imp", gp))
                vi = imps[:, :].unsqueeze(1).to_broadcast([128, NC1, NC1])
                vj = imps[:, :].unsqueeze(2).to_broadcast([128, NC1, NC1])
                r1, r2 = (z.rearrange("p (j i) -> p j i", j=NC1) for z in (rk1, rk2))
                dve.tensor_tensor(r1, vi, vj, ALU.is_gt)
                link(dve.tensor_tensor(r2, vi, vj, ALU.is_equal))
                link(dve.tensor_tensor(rk2, rk2, cst[:, C_TRI:C_TRI + 900], ALU.mult))
                link(dve.tensor_tensor(rk1, rk1, rk2, ALU.add))
                link(dve.tensor_reduce(sel32[:, 1:31], r1, AX, ALU.add))
                link(dve.tensor_scalar(sel32[:, 1:31], sel32[:, 1:31], NSEL_FREE - 0.5, NEG, ALU.is_gt, ALU.mult))
                link(dve.tensor_copy(selb[:, 128 * gp:128 * gp + 128].rearrange("p (j c) -> p j c", j=32),
                                     sel32[:, :].unsqueeze(2).to_broadcast([128, 32, 4])))

            def key_part(gp, c):
                if c >= 2:
                    want_filled(dve, ("S", gp, c - 2))
                elif gp:
                    want_filled(dve, ("S", gp - 1, c + 3))
                evac(("T", gp, c, 1), kTc[:, 1, c % 2, :], ps(("T", gp, c, 1))[:, :])

            def masked(key, dst, src, mask, col):
                want_filled(dve, key)
                return dve.tensor_tensor_reduce(dst, src, mask, -QS, 3e38, ALU.add, ALU.min, small[:, 104 + col:105 + col])

            def scores(gp, c):
                key = ("S", gp, c)
                if c < 4:
                    m = selb[:, 128 * gp:128 * gp + 128].unsqueeze(1).to_broadcast([128, 4, 128])
                    ins = masked(key, ssb[:, 512 * c:512 * c + 512].rearrange("p (s n) -> p s n", s=4),
                                 ps(key)[:, :].rearrange("p (s n) -> p s n", s=4), m, c)
                else:
                    ins = masked(key, wsb[:, 0:512], ps(key)[:, :], cst[:, C_WIN:C_WIN + 512], 5)
                frees(ins, key)

            dve.wait_ge(stored, 16 * N_STORED)
            cmp_scores(0)
            key_part(0, 0)
            cmp_probs(0)
            key_part(0, 1)
            cmp_groups(0)
            cmp_importance(0)
            cmp_select(0)
            for gp in range(4):
                more = gp < 3
                if gp:
                    want_filled(dve, ("PT", gp - 1, 5))
                scores(gp, 0)
                key_part(gp, 2)
                scores(gp, 1)
                if more:
                    cmp_scores(gp + 1)
                key_part(gp, 3)
                scores(gp, 2)
                key_part(gp, 4)
                if more:
                    cmp_probs(gp + 1)
                scores(gp, 3)
                scores(gp, 4)
                nm = cst[:, C_NEW + 64 * gp:C_NEW + 64 * gp + 64]
                masked(("Sn", gp), ssb[:, 2048:2112], ps(("Sn", gp))[:, 0:64], nm, 4)
                frees(masked(("Sn", gp), wsb[:, 512:576], ps(("Sn", gp))[:, 64:128], nm, 6), ("Sn", gp))
                want_emptied(dve, ("Sn", gp))
                dve.tensor_reduce(small[:, 112:113], small[:, 104:109], AX, ALU.min)
                dve.tensor_reduce(small[:, 113:114], small[:, 109:111], AX, ALU.min).then_inc(s_min, 1)
                if more:
                    cmp_groups(gp + 1)
                    key_part(gp + 1, 0)
                    key_part(gp + 1, 1)
                    cmp_importance(gp + 1)
                for i in (1, 3, 5):
                    key = ("PT", gp, i)
                    if i == 5:
                        evac(key, pTn, ps(key)[0:TS, 0:256].rearrange("p (x n) -> p x n", x=2))
                    else:
                        evac(key, pT[:, 4 * i:4 * i + 4, :], ps(key)[:, :].rearrange("p (s n) -> p s n", s=4))
                if more:
                    cmp_select(gp + 1)
                dve.wait_ge(s_exp, 2 * gp + 2)
                link(dve.reciprocal(small[:, 116:118], small[:, 114:116]))
                for x in range(2):
                    key = ("O", gp, x)
                    want_filled(dve, key)
                    for i in range(4):
                        r = slice(32 * i, 32 * i + 32)
                        ins = dve.tensor_scalar(orow[r, gp, 1 + x, :], ps(key)[r, 64 * (i % 2):64 * (i % 2) + 64],
                                                small[r, 116 + x:117 + x], None, ALU.mult)
                    frees(ins, key)
                want_emptied(dve, ("cO", gp))
                want_emptied(dve, ("O", gp, 1))
                dve.tensor_copy(small[:, 251:252], orow[:, gp, 2, 0:1]).then_inc(o_row, 1)

            for t in range(4):
                w = 128 * (t + 1)
                if t:
                    want_filled(dve, ("pcPT", t - 1, 1))
                mb = cst[:, C_CMB + PNC * t:C_CMB + PNC * (t + 1)].unsqueeze(1).to_broadcast([128, 4, PNC])
                for k in range(NKV):
                    key = ("pcS", t, k)
                    want_filled(dve, key)
                    frees(dve.tensor_tensor(pcp[:, 4 * k:4 * k + 4, :], ps(key)[:, 0:4 * PNC].rearrange("p (h n) -> p h n", h=4),
                                            mb, ALU.add), key)
                    want_emptied(dve, key)
                link(dve.tensor_reduce(small[:, 160:168], pcp, AX, ALU.max))
                dve.tensor_tensor(pcp, pcp, small[:, 160:168].unsqueeze(2).to_broadcast([128, 8, PNC]), ALU.subtract
                                  ).then_inc(p_in, 1)
                dve.wait_ge(p_exp, t + 1)
                m01 = cst[:, C_CM01 + PNC * t:C_CM01 + PNC * (t + 1)].unsqueeze(1).to_broadcast([128, 8, PNC])
                link(dve.tensor_tensor(pcp, pcp, m01, ALU.mult))
                link(dve.tensor_reduce(small[:, 160:168], pcp, AX, ALU.add))
                link(dve.tensor_scalar(small[:, 160:168], small[:, 160:168], 1e-30, None, ALU.max))
                link(dve.reciprocal(small[:, 160:168], small[:, 160:168]))
                dve.tensor_tensor(pcp, pcp, small[:, 160:168].unsqueeze(2).to_broadcast([128, 8, PNC]), ALU.mult
                                  ).then_inc(p_prob, 1)
                ov = pj[:, t, 0:512].rearrange("p (h d) -> p h d", h=8)
                ot = otmp.rearrange("p (h d) -> p h d", h=8)

                def add_branch(x):
                    key = ("pO", t, x)
                    cf = small[:, 168 + 8 * x:176 + 8 * x]
                    if x:
                        dve.wait_ge(p_soft, 8 * (2 * t + x))
                        link(dve.reciprocal(cf, small[:, 120 + 8 * x:128 + 8 * x]))
                        link(dve.tensor_tensor(cf, cf, gate[:, t, :, x], ALU.mult))
                        cf = cf.unsqueeze(2).to_broadcast([128, 8, 64])
                    else:
                        cf = gate[:, t, :, 0:1].to_broadcast([128, 8, 64])
                    want_filled(dve, key)
                    frees(dve.tensor_tensor(ot if x else ov, ps(key)[:, :].rearrange("p (h d) -> p h d", h=8), cf, ALU.mult), key)
                    want_emptied(dve, key)
                    if x == 1:
                        link(dve.tensor_tensor(ov, ov, ot, ALU.add))
                    if x == 2:
                        dve.tensor_tensor(ov, ov, ot, ALU.add).then_inc(attn_ready, 1)

                add_branch(0)
                for br in range(2):
                    for i in range(NH):
                        key = ("pS", t, br, i)
                        want_filled(dve, key)
                        if i >= 2:
                            want_filled(dve, ("pPT", t, br, i - 2))
                        elif br or t:
                            want_filled(dve, ("pPT", t - (1 - br), 1 - br, 6 + i))
                        frees(dve.tensor_tensor_reduce(psb[:, i % 2, 0:w], ps(key)[:, 0:w],
                                                       cst[:, C_CAUS + 512 - w:C_CAUS + 512], -QS, 3e38, ALU.add, ALU.min,
                                                       small[:, 144 + i:145 + i]), key)
                        n, step = divmod(8 * (2 * t + br) + i, ADA_STEPS)
                        if step == 8 and ADA_FIRST + n < 12:
                            ada_rows(ADA_FIRST + n)
                    add_branch(1 + br)
            mod_cols(1)
            dve.wait_ge(rows_back, 128)
            ov = pj[0:TS, 4, 0:512].rearrange("p (h d) -> p h d", h=8)
            ot = otmp[0:TS, :].rearrange("p (h d) -> p h d", h=8)
            for x in range(3):
                cf = gate[0:TS, 4, :, x:x + 1].to_broadcast([TS, 8, 64])
                link(dve.tensor_tensor(ot if x else ov, osm[:, :, x, :], cf, ALU.mult))
                if x == 1:
                    link(dve.tensor_tensor(ov, ov, ot, ALU.add))
                if x == 2:
                    dve.tensor_tensor(ov, ov, ot, ALU.add).then_inc(attn_ready, 1)
            dve.wait_ge(a_root, 1)
            link(dve.reciprocal(small[:, 16:21], small[:, 8:13]))
            for t in range(5):
                dve.tensor_scalar(pj[0:TM[t], t, 0:512], pj[0:TM[t], t, 0:512], small[0:TM[t], 16 + t:17 + t], None, ALU.mult
                                  ).then_inc(a_ready, 1)
            for t in range(5):
                key = ("oT", t)
                want_filled(dve, key)
                frees(dve.tensor_tensor(oT[:, :, 128 * t:128 * t + TM[t]],
                                        ps(key)[:, 0:4 * TM[t]].rearrange("p (k n) -> p k n", k=4),
                                        colT[:, 16:20].unsqueeze(2).to_broadcast([128, 4, TM[t]]), ALU.mult), key)
            def second_norm(t):
                P = TM[t]
                dve.wait_ge(x1_root, t + 1)
                if t >= 2:
                    want_filled(dve, ("hT", t - 2, 1))
                link(dve.reciprocal(small[0:P, 24 + t:25 + t], small[0:P, 24 + t:25 + t]))
                dve.tensor_scalar(xnb[0:P, t % 2, :], xs[0:P, t, :], small[0:P, 24 + t:25 + t], None, ALU.mult
                                  ).then_inc(x1n_ready, 1)

            def first_half(t):
                key, cols, (_, _, z, zl) = ("hT", t, 0), slice(128 * t, 128 * t + 128), hlo_at[0]
                want_filled(dve, key)
                for k in range(4):
                    ins = dve.tensor_scalar(hraw[k][:, cols], ps(key)[:, 128 * k:128 * k + 128],
                                            mod[:, 1, 0, k, 0:1], mod[:, 1, 1, k, 0:1], ALU.mult, ALU.add)
                frees(ins, key)
                want_emptied(dve, key)
                link(high(dve.tensor_copy, hhi[:, 0:4, cols], z[:, :, cols]))
                low(dve, zl[:, :, cols], z[:, :, cols], hhi[:, 0:4, cols]).then_inc(h_low, 1)

            dve.wait_ge(stored, 16 * N_STORED)
            dve.wait_ge(kvc_stored, 32)
            dve.wait_ge(xin_loaded, 80)
            for n in range(2):
                cols = slice(512 * n, 512 * n + 512)
                for t in range(6):
                    if n and t:
                        second_norm(t - 1)
                    if t < 5:
                        key, i, P = ("wo", n, t), 5 * n + t, TM[t]
                        want_filled(dve, key)
                        for s in range(2):
                            want_emptied(dve, ("gate", 0, n, s))
                        frees(dve.tensor_tensor(x1t[0:P, i % 2, :], ps(key)[0:P, :], gbc[0:P, t // 4, cols], ALU.mult), key)
                        want_emptied(dve, key)
                        dve.tensor_tensor(xs[0:P, t, cols], x1t[0:P, i % 2, :], xin[0:P, t, cols], ALU.add).then_inc(x1_ready, 1)
                    if n and 1 <= t < 5:
                        first_half(t - 1)
            for h in range(2):
                key = ("hT", 4, h)
                want_filled(dve, key)
                dst = [hlo_at[0:1], hlo_at[1:]][h]
                for k0, n, z, zl in dst:
                    v = z[:, :, SEQ:TOK].rearrange("p k (b q) -> p k b q", b=8)
                    A, B = (mod[:, 1, x, k0:k0 + n, 1:9].unsqueeze(3).to_broadcast([128, n, 8, 8]) for x in range(2))
                    src = ps(key)[:, 64 * (k0 % 4):64 * (k0 % 4) + 64 * n].rearrange("p (k b q) -> p k b q", k=n, b=8)
                    ins = dve.tensor_tensor(v, src, A, ALU.mult)
                    if k0 + n in (4, 8):
                        frees(ins, key)
                        want_emptied(dve, key)
                    else:
                        link(ins)
                    link(dve.tensor_tensor(v, v, B, ALU.add))
                    w = z[:, :, SEQ:TOK]
                    link(high(dve.tensor_copy, hhi[:, k0:k0 + n, SEQ:TOK], w))
                    ins = low(dve, zl[:, :, SEQ:TOK], w, hhi[:, k0:k0 + n, SEQ:TOK])
                ins.then_inc(h_low, 1)

            def low_job(j):
                dve.wait_ge(hi_ready, j + 1)
                for raw, hi, lo in job_parts(j):
                    ins = low(dve, lo, raw, hi)
                if j >= NFT:
                    for raw, hi, lo in job_acts(j):
                        ins = low(dve, lo, raw, hi)
                ins.then_inc(lo_ready, 1)

            low_job(0)
            low_job(1)
            for i, h in GU_ORDER:
                key = ("gu", i, 1, h)
                want_filled(dve, key)
                want_emptied(dve, ("gu", i, 0, h))
                frees(dve.tensor_tensor(actT[:, i, HALF * h:HALF * h + HALF], ps(key)[:, 0:HALF],
                                        sgb[:, i % 2, HALF * h:HALF * h + HALF], ALU.mult), key)
                if (i, h) == (1, 1) or i > 1 and h == 0:
                    low_job(i + 1)
            for j in range(NFT + 1, NFT + 7):
                low_job(j)
            for n in range(2):
                cols = slice(512 * n, 512 * n + 512)
                for t in range(5):
                    key, i, P = ("dn", n, t), 5 * n + t, TM[t]
                    want_filled(dve, key)
                    for s in range(2):
                        want_emptied(dve, ("gate", 1, n, s))
                    frees(dve.tensor_tensor(yt[0:P, i % 2, :], ps(key)[0:P, :], gbc[0:P, t // 4, cols], ALU.mult), key)
                    want_emptied(dve, key)
                    dve.tensor_tensor(xs[0:P, t, cols], yt[0:P, i % 2, :], xs[0:P, t, cols], ALU.add).then_inc(out_ready, 1)
                if n == 0:
                    for j in range(NFT + 7, NFT + 12):
                        low_job(j)

        @block.tensor
        def _(pe):
            def turn(dst, src):
                P = src.shape[0]
                return pe.transpose(dst, src, ident[0:P, 0:P])

            pe.wait_ge(consts_loaded, 16)
            pe.wait_ge(gains_loaded, 160)
            fills(turn(ps(("rows",))[:, 0:52], rowb[:, :]), ("rows",))
            pe.wait_ge(scrow_ready, 1)
            for k in range(8):
                ins = turn(ps(("cT",))[:, 9 * k:9 * k + 9], scrow[:, 128 * k:128 * k + 128])
            fills(ins, ("cT",))
            pe.wait_ge(conv_state_loaded, 16)
            for m in range(4):
                ins = turn(ps(("sconv",))[:, 16 * m:16 * m + 16], stc[:, 128 * m:128 * m + 128])
            fills(ins, ("sconv",))
            for t in range(5):
                pe.wait_ge(xn_ready, t + 1)
                for h in range(2):
                    key = ("xT", t, h)
                    want_free(pe, key)
                    for k in range(4):
                        f = 128 * (4 * h + k)
                        ins = turn(ps(key)[:, TM[t] * k:TM[t] * k + TM[t]], xs[0:TM[t], t, f:f + 128])
                    fills(ins, key)
            pe.wait_ge(comp_w_loaded, 96)
            want_emptied(pe, ("rows",))
            for x in range(2):
                key = ("peb", x)
                want_free(pe, key)
                for i in range(16):
                    ins = pe.matmul(ps(key)[0:64, 0:1], w1v[:, x, i % 8, i // 8, :], colT[:, 36 + i:37 + i],
                                    start=i == 0, stop=i == 15)
                fills(ins, key)

            def mod_turn(l):
                key = ("mod", l)
                want_free(pe, key)
                for n in range(4):
                    want_emptied(pe, ("ada", n + 6 * l))
                src, eye = (modss, ident[0:9, 0:9]) if l == 0 else (modss2, ident[32:41, 32:41])
                for i in range(16):
                    ins = pe.transpose(ps(key)[:, 9 * i:9 * i + 9], src[:, 128 * i:128 * i + 128], eye)
                fills(ins, key)

            def ada_product(n, kk):
                key = ("ada", n)
                if kk == 0:
                    want_free(pe, key)
                w = weights(pe, ("ada", n, kk // 4))
                ins = pe.matmul(ps(key)[0:9, :], cT[:, 9 * kk:9 * kk + 9], w[:, kk % 4, :], start=kk == 0, stop=kk == 7)
                if kk == 7:
                    fills(ins, key)

            want_emptied(pe, ("cT",))
            for n in range(ADA_FIRST):
                for kk in range(8):
                    ada_product(n, kk)
                if n == 3:
                    mod_turn(0)

            for n in range(3):
                w = min(512, TEND - 512 * n)
                for t in range(5):
                    key = ("in", n, t)
                    want_free(pe, key)
                    for kh in range(2):
                        wt = weights(pe, ("in", n, kh))
                        for k in range(4):
                            kk = 4 * kh + k
                            if n == 0 and t == 0:
                                pe.wait_ge(hT_ready, kk + 1)
                            ins = pe.matmul(ps(key)[0:TM[t], 0:w], hT[:, kk, 128 * t:128 * t + TM[t]], wt[:, k, 0:w],
                                            start=kk == 0, stop=kk == 7)
                    fills(ins, key)
            for n in range(3):
                for m in range(4):
                    for h in range(2):
                        key = ("cv", n, m, h)
                        want_free(pe, key)
                        for kk in range(8):
                            wt = weights(pe, ("cv", n, kk // 4))
                            ins = pe.matmul(ps(key)[:, 0:HALF], wt[:, kk % 4, 128 * m:128 * m + 128],
                                            hT[:, kk, HALF * h:HALF * h + HALF], start=kk == 0, stop=kk == 7)
                        fills(ins, key)
            pe.wait_ge(u_end_ready, 4)
            want_free(pe, ("ulast",))
            for m in range(4):
                ins = turn(ps(("ulast",))[0:18, 128 * m:128 * m + 128], ulast[:, 18 * m:18 * m + 18])
            fills(ins, ("ulast",))
            pe.wait_ge(y_square, 4)
            for h in range(2):
                key = ("yss", h)
                want_free(pe, key)
                for m in range(4):
                    ins = pe.matmul(ps(key)[:, 0:HALF], cst[:, C_ONE:C_ONE + 128], hcT[:, m, HALF * h:HALF * h + HALF],
                                    start=m == 0, stop=m == 3)
                fills(ins, key)

            def turn_chunks(u):
                n = CH if u < 16 else PCH
                xc = cache(pe, u)
                for i in range(4):
                    key = ("xt", u, i)
                    want_free(pe, key)
                    for jj in range(4):
                        ins = turn(ps(key)[:, 128 * jj:128 * jj + n], xc[0:n, 2 * (4 * (i // 2) + jj) + i % 2, :])
                    fills(ins, key)

            turn_chunks(0)
            for u in range(19):
                if u < 17:
                    turn_chunks(u + 1)
                if u < 18:
                    n, key = (CH if u < 16 else PCH), ("pre", u)
                    want_free(pe, key)
                    for i in range(4):
                        want_emptied(pe, ("xt", u, i))
                    for j in range(8):
                        ins = pe.matmul(ps(key)[:, 0:2 * n], w1v[:, u % 2, j].rearrange("p r h -> p (r h)"),
                                        xcmp[:, u % 2, j, :, 0:n], start=j == 0, stop=j == 7)
                    fills(ins, key)
                if u:
                    key, m, x = ("cmp", u - 1), (NC if u <= 16 else PNC), (u - 1) % 2
                    want_free(pe, key)
                    pe.wait_ge(silu_ready, u)
                    for k in range(2):
                        ins = pe.matmul(ps(key)[0:m, 64 * k:64 * k + 64], slu[:, k, 0:m], w2[:, 64 * x:64 * x + 64],
                                        start=True, stop=True)
                    fills(ins, key)
            pe.wait_ge(nrm_done, 6)
            for g in range(G):
                for s in range(2):
                    key = ("qT", g, s)
                    want_free(pe, key)
                    for t in (range(4), (4,))[s]:
                        c0 = 128 * (t % 4)
                        ins = turn(ps(key)[:, c0:c0 + TM[t]],
                                   pj[0:TM[t], t, 128 * g:128 * g + 128])
                    fills(ins, key)
            for x, c in enumerate((TKS, TKW)):
                key = ("kT", x)
                want_free(pe, key)
                for t in range(4):
                    ins = turn(ps(key)[:, 128 * t:128 * t + 128], pj[:, t, c:c + 128])
                fills(ins, key)
            want_free(pe, ("kTn",))
            for x, c in enumerate((TKS, TKW)):
                ins = turn(ps(("kTn",))[:, 64 * x:64 * x + 64], pj[0:TS, 4, c:c + 128])
            fills(ins, ("kTn",))

            pe.wait_ge(nrm_done, 9)
            for i in range(3):
                key = ("kct", i)
                want_free(pe, key)
                for b in range(4 * i, min(4 * i + 4, 9)):
                    m = NC if b < 8 else PNC
                    c0 = 128 * (b - 4 * i)
                    ins = turn(ps(key)[:, c0:c0 + m], kcm[0:m, b, :])
                fills(ins, key)
            for g in range(G):
                want_emptied(pe, ("qT", g, 1))
            for i in range(3):
                want_emptied(pe, ("kct", i))

            def cmp_scores(gp):
                key = ("cS", gp)
                want_free(pe, key)
                for b in range(2):
                    bb = 2 * gp + b
                    ins = pe.matmul(ps(key)[64 * b:64 * b + 64, 0:NC], qblk[:, 64 * bb:64 * bb + 64], kcT[:, bb, 0:NC],
                                    start=True, stop=True)
                fills(ins, key)

            def cmp_turn(gp):
                key = ("cPT", gp)
                want_free(pe, key)
                pe.wait_ge(c_prob, gp + 1)
                fills(turn(ps(key)[0:NC, 0:128], csb), key)

            def cmp_values(gp):
                key = ("imp", gp)
                want_free(pe, key)
                pe.wait_ge(c_group, gp + 1)
                fills(pe.matmul(ps(key)[:, 0:32], cpx, cst[0:NC, C_OVL:C_OVL + 32],
                                start=True, stop=True), key)
                key = ("cO", gp)
                want_free(pe, key)
                want_emptied(pe, ("cPT", gp))
                for b in range(2):
                    ins = pe.matmul(ps(key)[64 * b:64 * b + 64, 0:128], ctb[:, 64 * b:64 * b + 64], vcm[0:NC, 2 * gp + b, :],
                                    start=True, stop=True)
                fills(ins, key)

            def turn_keys(gp, c):
                for b in range(2):
                    key = ("T", gp, c, b)
                    want_free(pe, key)
                    if c < 4:
                        kk = cache(pe, 18 + 4 * gp + b)[:, 4 * c:4 * c + 4, :]
                    else:
                        pe.wait_ge(win_loaded[0], 32 * (gp + 1))
                        kk = wnd[:, 0, b, :].rearrange("p (s n) -> p s n", s=4)
                    for i in range(4):
                        ins = turn(ps(key)[:, 128 * i:128 * i + 128], kk[:, i, :])
                    fills(ins, key)

            def score(gp, c):
                key = ("S", gp, c)
                want_free(pe, key)
                for b in range(2):
                    want_emptied(pe, ("T", gp, c, b))
                for b in range(2):
                    bb = 2 * gp + b
                    ins = pe.matmul(ps(key)[64 * b:64 * b + 64, :], qblk[:, 64 * bb:64 * bb + 64], kTc[:, b, c % 2, :],
                                    start=True, stop=True)
                fills(ins, key)

            def score_new(gp):
                key = ("Sn", gp)
                want_free(pe, key)
                for b in range(2):
                    bb = 2 * gp + b
                    ins = pe.matmul(ps(key)[64 * b:64 * b + 64, 0:128], qblk[:, 64 * bb:64 * bb + 64],
                                    kTn.rearrange("p x n -> p (x n)"), start=True, stop=True)
                fills(ins, key)

            def turn_probs(gp):
                for i in range(6):
                    key = ("PT", gp, i)
                    want_free(pe, key)
                    pe.wait_ge(s_exp, 2 * gp + (1 if i < 4 else 2))
                    if i < 5:
                        src = wsb[:, 0:512] if i == 4 else ssb[:, 512 * i:512 * i + 512]
                        for s in range(4):
                            ins = turn(ps(key)[:, 128 * s:128 * s + 128], src[:, 128 * s:128 * s + 128])
                    else:
                        turn(ps(key)[0:TS, 0:128], ssb[:, 2048:2112])
                        ins = turn(ps(key)[0:TS, 128:256], wsb[:, 512:576])
                    fills(ins, key)

            def values(gp):
                for i in range(6):
                    want_emptied(pe, ("PT", gp, i))
                for x in range(2):
                    key = ("O", gp, x)
                    want_free(pe, key)
                    if x:
                        pe.wait_ge(win_loaded[1], 32 * (gp + 1))
                    for b in range(2):
                        r = slice(64 * b, 64 * b + 64)
                        if x:
                            vv, pp, ns, vc = wnd[:, 1, b, :].rearrange("p (s n) -> p s n", s=4), pTw, 4, TVW
                        else:
                            vv, pp, ns, vc = cache(pe, 20 + 4 * gp + b), pT, 16, TVS
                        for s in range(ns):
                            pe.matmul(ps(key)[r, 0:128], pp[:, s, r], vv[:, s, :], start=s == 0, stop=False)
                        ins = pe.matmul(ps(key)[r, 0:128], pTn[:, x, r], pj[0:TS, 4, vc:vc + 128], start=False, stop=True)
                    fills(ins, key)

            want_emptied(pe, ("kTn",))
            cmp_scores(0)
            turn_keys(0, 0)
            cmp_turn(0)
            turn_keys(0, 1)
            cmp_values(0)
            for gp in range(4):
                more = gp < 3
                score(gp, 0)
                turn_keys(gp, 2)
                score(gp, 1)
                if more:
                    cmp_scores(gp + 1)
                turn_keys(gp, 3)
                score(gp, 2)
                turn_keys(gp, 4)
                score(gp, 3)
                if more:
                    cmp_turn(gp + 1)
                score(gp, 4)
                score_new(gp)
                if more:
                    turn_keys(gp + 1, 0)
                    turn_keys(gp + 1, 1)
                    cmp_values(gp + 1)
                turn_probs(gp)
                values(gp)

            for g in range(G):
                want_emptied(pe, ("qT", g, 0))
            for x in range(2):
                want_emptied(pe, ("kT", x))
            for t in range(4):
                def rows(h):
                    return slice(64 * (h // G), 64 * (h // G) + 64)

                def q_of(h):
                    return qTp[rows(h), h % G, 128 * t:128 * t + 128]

                for k in range(NKV):
                    key = ("pcS", t, k)
                    want_free(pe, key)
                    for g in range(G):
                        ins = pe.matmul(ps(key)[:, PNC * g:PNC * g + PNC], q_of(G * k + g), kcT[rows(G * k), 8, 0:PNC],
                                        start=True, stop=True)
                    fills(ins, key)
                pe.wait_ge(p_prob, t + 1)
                for hh in range(2):
                    key = ("pcPT", t, hh)
                    want_free(pe, key)
                    for i in range(4):
                        h = 4 * hh + i
                        ins = turn(ps(key)[0:PNC, 128 * i:128 * i + 128], pcp[:, h, :])
                    fills(ins, key)
                key = ("pO", t, 0)
                want_free(pe, key)
                for hh in range(2):
                    want_emptied(pe, ("pcPT", t, hh))
                for h in range(NH):
                    ins = pe.matmul(ps(key)[:, 64 * h:64 * h + 64], ppTc[:, h, :], vcm[0:PNC, 8, rows(h)], start=True, stop=True)
                fills(ins, key)
                for br in range(2):
                    okey = ("pO", t, 1 + br)
                    want_free(pe, okey)
                    for i in range(NH + 2):
                        if i < NH:
                            key = ("pS", t, br, i)
                            want_free(pe, key)
                            fills(pe.matmul(ps(key)[:, 0:128 * (t + 1)], q_of(i), kTp[rows(i), br, 0:128 * (t + 1)],
                                            start=True, stop=True), key)
                            n, kk = divmod(8 * (2 * t + br) + i, ADA_STEPS)
                            if kk < 8 and ADA_FIRST + n < 12:
                                ada_product(ADA_FIRST + n, kk)
                        if 1 <= i <= NH:
                            h = i - 1
                            key = ("pPT", t, br, h)
                            want_free(pe, key)
                            pe.wait_ge(p_soft, 8 * (2 * t + br) + h + 1)
                            for k in range(t + 1):
                                ins = turn(ps(key)[:, 128 * k:128 * k + 128], psb[:, h % 2, 128 * k:128 * k + 128])
                            fills(ins, key)
                        if i >= 2:
                            h = i - 2
                            want_emptied(pe, ("pPT", t, br, h))
                            c0 = (TVS, TVW)[br] + 64 * (h // G)
                            for k in range(t + 1):
                                ins = pe.matmul(ps(okey)[:, 64 * h:64 * h + 64], ppT[:, h % 2, k, :], pj[:, k, c0:c0 + 64],
                                                start=k == 0, stop=k == t)
                    fills(ins, okey)
            mod_turn(1)
            for t in range(5):
                key = ("oT", t)
                want_free(pe, key)
                pe.wait_ge(a_ready, t + 1)
                for k in range(4):
                    ins = turn(ps(key)[:, TM[t] * k:TM[t] * k + TM[t]], pj[0:TM[t], t, 128 * k:128 * k + 128])
                fills(ins, key)

            def gate_rows(l):
                for n in range(2):
                    want_emptied(pe, ("ada", (4, 10)[l] + n))
                    for s in range(2):
                        key, P = ("gate", l, n, s), (128, TS)[s]
                        want_free(pe, key)
                        c0 = 1024 * l + 512 * n
                        fills(pe.matmul(ps(key)[0:P, :], cst[0:9, C_SEL + 128 * s:C_SEL + 128 * s + P], grow[:, c0:c0 + 512],
                                        start=True, stop=True), key)

            gate_rows(0)
            pe.wait_ge(vT_ready, 4)
            def project_out(n, t):
                key = ("wo", n, t)
                want_free(pe, key)
                want_emptied(pe, ("oT", t))
                for kk in range(8):
                    wt = weights(pe, ("wo", n, kk // 4))
                    src = oT if kk < 4 else vT
                    ins = pe.matmul(ps(key)[0:TM[t], :], src[:, kk % 4, 128 * t:128 * t + TM[t]], wt[:, kk % 4, :],
                                    start=kk == 0, stop=kk == 7)
                fills(ins, key)

            def turn_normed(t):
                pe.wait_ge(x1n_ready, t + 1)
                for h in range(2):
                    key = ("hT", t, h)
                    want_free(pe, key)
                    for k in range(4):
                        f = 128 * (4 * h + k)
                        ins = turn(ps(key)[:, TM[t] * k:TM[t] * k + TM[t]], xnb[0:TM[t], t % 2, f:f + 128])
                    fills(ins, key)
            for t in range(5):
                project_out(0, t)
            for t in range(6):
                if t < 5:
                    project_out(1, t)
                if t:
                    turn_normed(t - 1)

            def products(dst, pairs, first, last):
                for k, ((sh, sl), (mh, ml)) in enumerate(pairs):
                    pe.matmul(dst, sh, ml, start=first and k == 0, stop=False)
                    pe.matmul(dst, sl, mh, start=False, stop=False)
                    ins = pe.matmul(dst, sh, mh, start=False, stop=last and k == len(pairs) - 1)
                return ins

            for i, h in GU_ORDER:
                pe.wait_ge(h_low, 6 if h else 3)
                pe.wait_ge(h_low2, 4 if h else 3)
                pe.wait_ge(lo_ready, i + 1)
                wv = ws[:, i % 2].rearrange("p y (k x c) -> p y k x c", k=8, x=2)
                for x in range(2):
                    key = ("gu", i, x, h)
                    want_free(pe, key)
                    cols = slice(HALF * h, HALF * h + HALF)
                    fills(products(ps(key)[:, 0:HALF], [((wv[:, 0, k, x], wv[:, 1, k, x]), (hhi[:, k, cols], hlo[k][:, cols]))
                                                        for k in range(8)], True, True), key)
                if (i, h) == GATE_AT:
                    pe.wait_ge(x1_ready, 10)
                    gate_rows(1)
            for n in range(2):
                for kc in range(6):
                    j = NFT + 6 * n + kc
                    pe.wait_ge(lo_ready, j + 1)
                    acts, wv = act_pairs(j), ws[:, j % 2]
                    for t in range(5):
                        key, cols = ("dn", n, t), slice(128 * t, 128 * t + TM[t])
                        if kc == 0:
                            want_free(pe, key)
                        ins = products(ps(key)[0:TM[t], :],
                                       [((hi[:, cols], lo[:, cols]), (wv[:, 0, 512 * k:512 * k + 512], wv[:, 1, 512 * k:512 * k + 512]))
                                        for k, (hi, lo) in enumerate(acts)], kc == 0, kc == 5)
                        if kc == 5:
                            fills(ins, key)
                    if kc < 5:
                        ins.then_inc(dn_read, 1)


NORMS = [("q", 128, 32, 0, 4, 8, 0), ("q", TS, 8, 4, 1, 8, 0), ("ks", 128, 8, 0, 4, 2, 2), ("ks", TS, 2, 4, 1, 2, 2),
         ("kw", 128, 8, 0, 4, 2, 3), ("kw", TS, 2, 4, 1, 2, 3), ("kcm", NC, 8, 0, 4, 2, 1),
         ("kcm", NC, 8, 4, 4, 2, 1), ("kcm", PNC, 2, 8, 1, 2, 1)]
NORM_AT = [0, 1, 2, 3, 4, 5, 10, 17]
N_STORED = 3 + 1 + 1 + 2 + 8 + 2 + 1 + 8 + 2

_INS = ["x_prompt", "x_sample", "cache_k_cmp", "cache_v_cmp", "cache_k_slc", "cache_v_slc", "state_k_win", "state_v_win",
        "state_conv", "page_table", "c_prompt", "c_sample", "w_ada", "b_ada", "ln1_g", "w_in", "q_norm_g", "k_norm_g",
        "pe_cmp", "w_ck1", "w_ck2", "w_cv1", "w_cv2", "w_conv", "attn_out_g", "conv_out_g", "w_o", "ln2_g", "w_gu", "w_down"]
_OUTS = [("y_prompt", (1, SEQ, D)), ("y_sample", (NB, NQ, D))]
_OUTS += [(f"p_{n}", (1, 1, SEQ, NKV, HD)) for n in ("k_cmp", "v_cmp", "k_slc", "v_slc", "k_win", "v_win")]
_OUTS += [("p_conv", (1, 1, 2, 512))]
_OUTS += [(f"s_{n}", (1, NB, NQ, NKV, HD)) for n in ("k_cmp", "v_cmp", "k_slc", "v_slc")]
_OUTS += [(f"s_{n}", (1, NB, SEQ, NKV, HD)) for n in ("k_win", "v_win")]
_OUTS += [("s_conv", (1, NB, 2, 512))]


def kernel(**inputs):
    import numpy as _np
    import concourse.bacc as _bacc
    from concourse import mybir as _mybir
    from concourse.bass_utils import run_bass_kernel_spmd as _run

    nc = _bacc.Bacc("TRN2", target_bir_lowering=False, num_devices=1)
    arrays, ins, outs = {}, {}, {}
    given = {name: _np.ascontiguousarray(inputs[name]) for name in _INS}
    given["consts"] = constants()
    for name, x in given.items():
        arrays[f"in_{name}"] = x
        ins[name] = nc.dram_tensor(f"in_{name}", x.shape, _mybir.dt.from_np(x.dtype), kind="ExternalInput").ap()
    for name, shape in _OUTS:
        outs[name] = nc.dram_tensor(f"out_{name}", shape, F32, kind="ExternalOutput").ap()
    decoder_kernel(nc, ins, outs)
    r = _run(nc, [arrays], core_ids=[0])
    return tuple(r.results[0][f"out_{name}"] for name, _ in _OUTS)
```

```python
from contextlib import ExitStack

import concourse.bass as bass
import numpy as np
from concourse import mybir

ALU = mybir.AluOpType
ACT = mybir.ActivationFunctionType
AX = mybir.AxisListType.X
F32 = mybir.dt.float32
F32R = mybir.dt.float32r
I32 = mybir.dt.int32
U32 = mybir.dt.uint32

D = 1024
SEQ, NB, NQ = 512, 8, 8
TS = NB * NQ
TOK = SEQ + TS
HALF = TOK // 2
HD, NH, NKV, G = 64, 8, 2, 4
PAST = 2048
CH = PAST // 16
NC = CH - 1
PCH = SEQ // 16
PNC = PCH - 1
NF = 2816
NFT = NF // 128
NC1 = 30
NSEL_FREE = 13
EPS = 1e-6
NEG = -1e30
QS = HD ** -0.5
WR = 4
CR = 4
TM = [128, 128, 128, 128, TS]
TQ, TKC, TVC, TKS, TVS, TKW, TVW, TG, TEND = 0, 512, 640, 768, 896, 1024, 1152, 1280, 1304

C_ID, C_P8, C_ROPE, C_ROPEC, C_CAUS, C_CMB, C_CM01, C_NEW, C_WIN, C_OVL, C_TRI, C_ONE, C_END = np.cumsum(
    [0, 128, 8, 80, 16, 512, 124, 124, 256, 512, 32, 900, 128]).tolist()

GU_ORDER = [(0, 0), (1, 0), (0, 1), (1, 1)] + [(i, h) for i in range(2, NFT) for h in range(2)]
ADA_FIRST, ADA_PROMPT = 5, 6
ADA_STEPS = 11
SQUARE = {(1, 0): 0, (1, 1): 4, (2, 0): 1, (3, 0): 2}
FINISH = {(3, 0, 7): 0, (3, 1, 0): 4, (3, 1, 1): 1, (3, 1, 2): 2}
OUT_ORDER = [0, 4, 1, 2, 3]

NG = 4 * 2 * NH
LAG = 3


def head(g):
    return g // 16, g // 8 % 2, g % 8


def constants():
    c = np.zeros((128, C_END), np.float32)
    p = np.arange(128)
    c[:, C_ID:C_ID + 128] = np.eye(128)
    inv = np.float32(500000.0) ** (-np.arange(8, dtype=np.float32) * np.float32(2.0) / np.float32(16))

    def cs(pos):
        ang = pos.astype(np.float32)[:, None] * inv[None, :]
        return np.concatenate([np.cos(ang), np.sin(ang)], 1)

    for t in range(5):
        c[:, C_ROPE + 16 * t:C_ROPE + 16 * t + 16] = cs(t * 128 + p if t < 4 else PAST + p % NQ)
    c[:, C_ROPEC:C_ROPEC + 16] = cs(p * 16 + 31)
    c[:, C_CAUS + 384:C_CAUS + 512] = np.where(p[None, :] <= p[:, None], 0, NEG)
    n = np.arange(PNC)
    for t in range(4):
        ok = n[None, :] * 16 + 31 <= (t * 128 + p)[:, None]
        c[:, C_CMB + PNC * t:C_CMB + PNC * (t + 1)] = np.where(ok, 0, NEG)
        c[:, C_CM01 + PNC * t:C_CM01 + PNC * (t + 1)] = ok
    b2, q = p // 64, p % 8
    k = np.arange(TS)
    for gp in range(4):
        ok = (k[None, :] // 8 == (2 * gp + b2)[:, None]) & (k[None, :] % 8 <= q[:, None])
        c[:, C_NEW + 64 * gp:C_NEW + 64 * gp + 64] = np.where(ok, 0, NEG)
    i = np.arange(512)
    c[:, C_WIN:C_WIN + 512] = np.where((4 * (i % 128) + i // 128)[None, :] > q[:, None], 0, NEG)
    j = np.arange(32)
    c[:, C_OVL:C_OVL + 32] = (p[:, None] * 16 < (j[None, :] + 1) * 64) & (p[:, None] * 16 + 32 > j[None, :] * 64)
    t30 = np.arange(NC1)
    c[:, C_TRI:C_TRI + 900] = (t30[None, :] < t30[:, None]).reshape(1, 900)
    c[:, C_ONE:C_ONE + 128] = 1
    c[:, C_P8:C_ROPE] = (p % 8)[:, None]
    return c


def plan_banks():
    ring, wide, low_ring, extra = [], [], [], []
    ring += [("cT",), ("ada", 0), ("ada", 1), ("rows",)]
    ring += [("xT", t, h) for t in range(5) for h in range(2)]
    ring += [("ada", 2), ("ada", 3), ("mod", 0), ("sconv",)]
    ring += [("ada", n) for n in range(4, ADA_FIRST)] + [("peb", 0), ("peb", 1)]
    first = len(ring)
    ring += [("cv", n, m, h) for n in range(3) for m in range(4) for h in range(2)]
    ring += [("ulast",)] + [("xt", 0, i) for i in range(4)] + [("yss", 0), ("yss", 1)]
    for u in range(19):
        if u < 17:
            ring += [("xt", u + 1, i) for i in range(4)]
        if u < 18:
            ring.append(("pre", u))
        if u == 18:
            ring += [("qT", g, s) for g in range(4) for s in range(2)]
            ring += [("kT", x) for x in range(2)] + [("kTn",)]
        if u:
            ring.append(("cmp", u - 1))
    pairs = len(ring)
    ring += [("T", 0, c, b) for c in range(2) for b in range(2)]
    ring += [("kct", i) for i in range(3)]

    def turned(gp, c):
        return [("T", gp, c, b) for b in range(2)]

    ring += [("cS", 0), ("cPT", 0), ("imp", 0)]
    wide.append(("cO", 0))
    for gp in range(4):
        more = gp < 3
        ring += [("S", gp, 0)] + turned(gp, 2) + [("S", gp, 1)]
        ring += [("cS", gp + 1)] * more
        ring += turned(gp, 3) + [("S", gp, 2)] + turned(gp, 4) + [("S", gp, 3)]
        ring += [("cPT", gp + 1)] * more
        ring += [("S", gp, 4), ("Sn", gp)]
        if more:
            ring.append(("imp", gp + 1))
            wide.append(("cO", gp + 1))
        ring += [("PT", gp, i) for i in range(6)]
        if more:
            ring += turned(gp + 1, 0) + turned(gp + 1, 1)
        wide += [("O", gp, 0), ("O", gp, 1)]
    low_ring += [("pcS", 0, k) for k in range(2)]
    for g in range(NG + LAG + 1):
        t, br, i = head(g)
        if g < NG:
            low_ring.append(("pS", g))
            if br == 0 and i == 0:
                low_ring += [("pcPT", t, hh) for hh in range(2)]
            if br == 0 and i == 1:
                low_ring.append(("pO", t, 0))
        if LAG <= g < NG + LAG:
            low_ring.append(("pPT", g - LAG))
        if g < NG:
            if (t, br, i) in FINISH:
                low_ring.append(("oT", FINISH[t, br, i]))
            if t < 3 and br == 0 and i == 7:
                low_ring += [("pcS", t + 1, k) for k in range(2)]
    wide += [("pO", t, br) for t in range(4) for br in (1, 2)]
    extra += [("ada", n) for n in range(ADA_FIRST, 12)]
    before = len(ring)
    ring.append(("mod", 1))
    ring += [("wo", 0, 0), ("wo", 0, 1), ("oT", 3)]
    ring += [("wo", 0, t) for t in range(2, 5)]
    for t in range(6):
        if t < 5:
            ring.append(("wo", 1, t))
        if t == 5:
            ring += [("gu", 0, x, 0) for x in range(2)]
        if t:
            ring += [("hT", t - 1, h) for h in range(2)]
    for i, h in GU_ORDER[1:]:
        ring += [("gu", i, x, h) for x in range(2)]
    ring += [("dn", n, t) for n in range(2) for t in range(5)]
    at, used = {}, [0] * 8
    for keys, banks in ((ring[:first], (0, 1, 2, 3, 4, 5)), ([("in", n, t) for n in range(3) for t in range(5)], range(8)),
                        (ring[first:pairs], (0, 1, 2, 3, 4, 5)), (ring[pairs:before], (0, 1, 2, 3, 4)),
                        (low_ring, (0, 1, 2, 3, 4)), (extra, (5,)),
                        (ring[before:], (0, 1, 2, 3, 4, 5)), (wide, (6, 7))):
        for i, k in enumerate(keys):
            b = banks[i % len(banks)]
            at[k] = (b, used[b])
            used[b] += 1
    return at


def plan_weights():
    c = [(("ada", n, kh), ("ada", n)) for n in range(ADA_FIRST) for kh in range(2)]
    c += [((kind, n, kh), None) for kind in ("in", "cv") for n in range(3) for kh in range(2)]
    c += [(("ada", n, kh), ("ada", n)) for n in range(ADA_FIRST, 12) for kh in range(2)]
    c += [(("wo", n, kh), ("wo", n, 4)) for n in range(2) for kh in range(2)]
    c += [(("gu", n, kh), None) for n in range(NFT // 2) for kh in range(2)]
    c += [(("dn", n, kc), None) for n in range(2) for kc in range(6)]
    return c


def decoder_kernel(nc, a, o):
    at = plan_banks()
    chunks = plan_weights()
    chunk_of = {k: i for i, (k, _) in enumerate(chunks)}

    with ExitStack() as ctx:
        place = {}

        def sb(name, cols, dt=F32, parts=128):
            place[name] = -(-nc.sbuf_base // 32) * 32
            return ctx.enter_context(nc.sbuf_tensor(name, [parts, cols], dt))

        def pairs_at(name, tensor, c0, cols):
            z = nc.alloc_sbuf_tensor_at(name, [128, cols], F32R, offset=place[tensor.name] + 4 * c0)
            return z

        def sem(name):
            return ctx.enter_context(nc.semaphore(name))

        bank = [ctx.enter_context(nc.psum_tensor(f"bank{i}", [128, 512], F32)) for i in range(8)]
        bank_filled = [sem(f"bank_filled{i}") for i in range(8)]
        bank_free = [sem(f"bank_free{i}") for i in range(8)]

        cst = sb("cst", C_END)
        hbuf = sb("hbuf", 8 * TOK)
        hT = hbuf[:, :].rearrange("p (k n) -> p k n", k=8)
        xcmp = hbuf[:, 0:4096].rearrange("p (u j k c) -> p u j k c", u=2, j=8, k=2)
        kTc = hbuf[:, 0:2048].rearrange("p (b s n) -> p b s n", b=2, s=2)
        pT = hbuf[:, 2048:4096].rearrange("p (s n) -> p s n", s=16)
        pTn = hbuf[0:TS, 4096:4352].rearrange("p (x n) -> p x n", x=2)
        ppT = [hbuf[:, c:c + 512].rearrange("p (k n) -> p k n", k=4) for c in (0, 512, 3072, 3584)]
        ppTc = hbuf[0:PNC, 1024:2048].rearrange("p (h n) -> p h n", h=8)
        proj = sb("proj", 5 * TEND)
        pj = proj[:, :].rearrange("p (t n) -> p t n", t=5)
        xs = proj[:, 0:5 * D].rearrange("p (t n) -> p t n", t=5)
        wring = sb("wring", WR * 2048)
        wch = wring[:, :].rearrange("p (r k n) -> p r k n", r=WR, k=4)
        arena = sb("arena", NFT * TOK)
        actT = arena[:, :].rearrange("p (i n) -> p i n", i=NFT)
        cring = arena[:, 0:CR * 2048].rearrange("p (r n) -> p r n", r=CR)
        xin = arena[:, 0:5 * D].rearrange("p (t n) -> p t n", t=5)
        xnb = arena[:, 5 * D:7 * D].rearrange("p (s n) -> p s n", s=2)
        late = arena[:, CR * 2048:NFT * TOK]
        hcT = late[:, 0:4 * TOK].rearrange("p (f n) -> p f n", f=4)
        yrs = late[:, 4 * TOK:5 * TOK]
        modss = late[0:9, 0:2048]
        sqb = late[:, 0:2048]
        ropb = late[:, 2048:3072]
        ssb, wsb = late[:, 0:2112], late[:, 2112:2688]
        pTw = late[:, 2688:3200].rearrange("p (s n) -> p s n", s=4)
        psb = [late[:, 2688:3200], late[:, 3200:3712], hbuf[:, 2048:2560], hbuf[:, 2560:3072], hbuf[:, 4096:4608]]
        x1t = late[:, 2688:3712].rearrange("p (s n) -> p s n", s=2)
        osm = late[0:TS, 0:1536].rearrange("p (h c n) -> p h c n", h=8, c=3)
        otmp, sqo = late[:, 1536:2048], late[:, 2048:2560]
        ulr = late[0:18, 3800:4312]
        uvT = sb("uvT", 4 * TOK)
        uT = uvT[:, :].rearrange("p (f n) -> p f n", f=4)
        oT = uT
        rk1, rk2 = uvT[:, 768:1668], late[:, 3200:4100]
        csb, ctb, cpx = uvT[:, 1668:1668 + NC], uvT[0:NC, 1800:1928], uvT[0:NC, 1928:2056]
        cpg = uvT[0:NC, 2056:2088].rearrange("p (a q) -> p a q", a=4)
        crow, scrow = uvT[0:9, 0:D], uvT[0:9, D:2 * D]
        sgb = uvT[:, 0:2 * TOK].rearrange("p (s n) -> p s n", s=2)
        yt = uvT[:, 2 * TOK:2 * TOK + 1024].rearrange("p (s n) -> p s n", s=2)
        mem = sb("mem", 4 * TOK + 2048 + 7168)
        vTt = mem[:, 0:4 * TOK]
        vT = vTt.rearrange("p (f n) -> p f n", f=4)
        stc = vTt[0:16, 0:512]
        att = mem[:, 4 * TOK + 2048:]
        w1v = att[:, 0:2048].rearrange("p (x j r h) -> p x j r h", x=2, j=8, r=2)
        qTp = att[:, 0:2048].rearrange("p (g n) -> p g n", g=4)
        gbc = att[:, 5120:7168].rearrange("p (s n) -> p s n", s=2)
        qblk = att[:, 2048:2560]
        kTp = att[:, 2560:3584].rearrange("p (x n) -> p x n", x=2)
        kTn = att[:, 3584:3712].rearrange("p (x n) -> p x n", x=2)
        kcm = att[:, 3712:4864].rearrange("p (b n) -> p b n", b=9)
        vcm = att[:, 4864:6016].rearrange("p (b n) -> p b n", b=9)
        kcT = att[:, 6016:7168].rearrange("p (b n) -> p b n", b=9)
        rows2 = sb("rows2", 2048, parts=41)
        grow, modss2 = rows2[0:9, :], rows2[32:41, :]
        rowb = sb("rowb", 128, parts=52)
        winb = mem[:, 4 * TOK:4 * TOK + 2048]
        wnd = winb.rearrange("p (x b n) -> p x b n", x=2, b=2)
        w2 = sb("w2", 128, parts=64)
        colT = sb("colT", 52)
        cT = sb("cT", 72)
        stT = sb("stT", 64)
        modt = sb("modt", 288)
        mod = modt[:, :].rearrange("p (l x k b) -> p l x k b", l=2, x=2, k=8)
        gains = sb("gains", 256)
        ulast = sb("ulast", 72)
        gat = sb("gat", 120)
        gate = gat[:, :].rearrange("p (t h c) -> p t h c", t=5, h=8)
        small = sb("small", 256)
        hss, hrt = sb("hss", NORM_COL[-1]), sb("hrt", NORM_COL[-1])
        selb = sb("selb", 512)
        sel32 = sb("sel32", 32)
        imps = sb("imps", NC1)
        slv = late[0:64, 3072:3584]
        half = slv[:, 0:2 * NC].rearrange("p (k n) -> p k n", k=2)
        slu = slv[:, 256:256 + 2 * NC].rearrange("p (k n) -> p k n", k=2)
        orows = uvT[:, 0:4 * 192]
        orow = orows[:, :].rearrange("p (g c n) -> p g c n", g=4, c=3)
        pti = sb("pti", 8, I32)
        idx = sb("idx", 8, U32)
        pebt = sb("pebt", 2, parts=64)
        pct = sb("pct", 8 * PNC)
        pcp = pct[:, :].rearrange("p (h n) -> p h n", h=8)
        epst = sb("epst", 1)
        ident = cst[:, C_ID:C_ID + 128]
        ws = pairs_at("ws", mem, 0, 8192)[:, :].rearrange("p (s x n) -> p s x n", s=2, x=2)
        hhi = pairs_at("hhi", hbuf, 0, 8 * TOK)[:, :].rearrange("p (k n) -> p k n", k=8)
        ws1 = [pairs_at(f"ws1_{i}", z, c0, 4096)[:, :].rearrange("p (x n) -> p x n", x=2)
               for i, (z, c0) in enumerate(((arena, 4096), (mem, 4 * TOK + 4096)))]
        h1hi = [z[:, TOK * k:TOK * k + TOK] for n, z in
                [(n, pairs_at(f"h1hi_{i}", z, c0, n * TOK)) for i, (n, z, c0) in enumerate(
                    ((3, arena, 2048), (3, mem, 4 * TOK), (2, arena, CR * 2048 + 5 * TOK)))] for k in range(n)]
        h1lo = [hhi[:, k] for k in range(8)]
        hlo_at = [(k0, n, z[:, c0:c0 + n * TOK].rearrange("p (k n) -> p k n", k=n),
                   pairs_at(f"hlo{k0}", z, c0, n * TOK)[:, :].rearrange("p (k n) -> p k n", k=n))
                  for k0, n, z, c0 in ((0, 4, cst, C_ROPE), (4, 2, mem, 8192), (6, 2, proj, 5 * D))]
        hraw = [z[2][:, k] for z in hlo_at for k in range(z[1])]
        hlo = [z[3][:, k] for z in hlo_at for k in range(z[1])]
        g_rows = nc.dram_tensor("g_rows", [9, 2048], F32).ap()
        o_rows = nc.dram_tensor("o_rows", [NB, NH, NQ, 192], F32).ap()

        ident_loaded, consts_loaded, gains_loaded, c_loaded, comp_w_loaded, bias_loaded, conv_state_loaded, pages_loaded = (
            sem(n) for n in ("ident_loaded", "consts_loaded", "gains_loaded", "c_loaded", "comp_w_loaded", "bias_loaded",
                             "conv_state_loaded", "pages_loaded"))
        x_loaded = [sem(f"x_loaded{t}") for t in range(5)]
        w_loaded = [sem(f"w_loaded{i}") for i in range(WR)]
        cache_loaded = [sem(f"cache_loaded{i}") for i in range(CR)]
        win_loaded = [sem(f"win_loaded{i}") for i in range(2)]
        gates_out, gates_in = sem("gates_out"), sem("gates_in")
        xin_loaded, rows_back, rows_out, stored, kvc_stored = (
            sem(n) for n in ("xin_loaded", "rows_back", "rows_out", "stored", "kvc_stored"))
        dve_step, act_step = sem("dve_step"), sem("act_step")
        (cleared, scrow_ready, x_square, x_root, xn_ready, idx_ready, hT_ready, u_end_ready, y_ready, y_square, y_inv,
         vT_ready, v_scaled, half_ready, pre_ready, silu_ready, nrm_square, nrm_root, nrm_done, gate_exp, gates_ready,
         c_exp, c_prob, c_group, sel_ready, s_min, s_exp, o_row, p_in, p_exp, p_prob, p_soft, attn_ready, a_square,
         a_root, a_ready, x1_ready, x1_square, x1_root, x1n_ready, dn_read, out_ready, hi_ready, lo_ready,
         h_low, h_high, h_low2, hi1_ready, lo1_ready, in_read, h1_sample, h1_mod,
         h1_hi, first_high, first_low) = (sem(n) for n in (
            "cleared scrow_ready x_square x_root xn_ready idx_ready hT_ready u_end_ready y_ready y_square y_inv "
            "vT_ready v_scaled half_ready pre_ready silu_ready nrm_square nrm_root nrm_done gate_exp gates_ready "
            "c_exp c_prob c_group sel_ready s_min s_exp o_row p_in p_exp p_prob p_soft attn_ready a_square "
            "a_root a_ready x1_ready x1_square x1_root x1n_ready dn_read out_ready hi_ready lo_ready h_low h_high h_low2 hi1_ready lo1_ready in_read h1_sample h1_mod "
            "h1_hi first_high first_low").split())

        def ps(key):
            return bank[at[key][0]]

        def want_free(eng, key):
            b, n = at[key]
            if n:
                eng.wait_ge(bank_free[b], n)

        def want_filled(eng, key):
            b, n = at[key]
            eng.wait_ge(bank_filled[b], n + 1)

        def want_emptied(eng, key):
            b, n = at[key]
            eng.wait_ge(bank_free[b], n + 1)

        def fills(ins, key):
            ins.then_inc(bank_filled[at[key][0]], 1)

        def frees(ins, key):
            ins.then_inc(bank_free[at[key][0]], 1)

        def loads_of(i):
            return 32 if chunks[i][0][0] == "gu" else 16

        def weights(pe, key):
            i = chunk_of[key]
            pe.wait_ge(w_loaded[i % WR], sum(loads_of(j) for j in range(i % WR, i + 1, WR)))
            return wch[:, i % WR]

        caches = [(("cache_k_cmp", "cache_v_cmp")[u % 2], u // 2, ("xt", u, 3)) for u in range(16)]
        caches += [("p_k_cmp", None, ("xt", 16, 3)), ("p_v_cmp", None, ("xt", 17, 3))]
        for gp in range(4):
            caches += [("cache_k_slc", 2 * gp + b, ("T", gp, 3, b)) for b in range(2)]
            caches += [("cache_v_slc", 2 * gp + b, ("O", gp, 0)) for b in range(2)]

        def cache(eng, i):
            eng.wait_ge(cache_loaded[i % CR], 16 * (i // CR + 1))
            return cring[:, i % CR, :].rearrange("p (s n) -> p s n", s=16)

        def tok_rows(name_p, name_s, t):
            return a[name_p][0, 128 * t:128 * t + 128, :] if t < 4 else a[name_s].rearrange("b q d -> (b q) d")

        def out_rows(name):
            return o[name].rearrange("l b (t p) k d -> p (l b t) (k d)", p=128)

        def high(copy, dst, src):
            return copy(dst, src)

        def low(eng, dst, src, hi):
            return eng.tensor_tensor(dst, src, hi.bitcast(F32), ALU.subtract)

        def job1_read(eng, j):
            n, x = divmod(j % 6, 2)
            if j >= 6:
                want_filled(eng, ("cv", n, 2 * x + 1, 1))
            elif x:
                want_filled(eng, ("in", n, 4))
            else:
                eng.wait_ge(in_read, n + 1)

        def job1_parts(j):
            (n, x), hi, lo = divmod(j % 6, 2), ws1[j % 2][:, 0], ws1[j % 2][:, 1]
            if j < 6:
                w = min(512, TEND - 512 * n)
                return [(("in", n, x), wch[:, chunk_of["in", n, x] % WR, :, 0:w]) +
                        tuple(z.rearrange("p (k c) -> p k c", k=4)[:, :, 0:w] for z in (hi, lo))]
            return [(("cv", n, kh), wch[:, chunk_of["cv", n, kh] % WR, :, 256 * x:256 * x + 256]) +
                    tuple(z[:, 1024 * kh:1024 * kh + 1024].rearrange("p (k c) -> p k c", k=4) for z in (hi, lo))
                    for kh in range(2)]

        def reads_job(j):
            if j < NFT:
                return lambda eng: want_filled(eng, ("gu", j, 1, 1))
            n, kc = divmod(j - NFT, 6)
            return (lambda eng: eng.wait_ge(dn_read, 5 * n + kc + 1)) if kc < 5 else (
                lambda eng: want_filled(eng, ("dn", n, 4)))

        def job_parts(j):
            hi, lo = ws[:, (j + 1) % 2, 0], ws[:, (j + 1) % 2, 1]
            if j < NFT:
                parts = []
                for kh in range(2):
                    raw = wch[:, chunk_of["gu", j // 2, kh] % WR].rearrange("p k (x m c) -> p k x m c", x=2, m=2)[:, :, :, j % 2]
                    parts.append([raw] + [z[:, 1024 * kh:1024 * kh + 1024].rearrange("p (k x c) -> p k x c", k=4, x=2)
                                          for z in (hi, lo)])
                return parts
            n, kc = divmod(j - NFT, 6)
            nk = 4 if kc < 5 else NFT - 20
            return [[wch[:, chunk_of["dn", n, kc] % WR, 0:nk]] +
                    [z[:, 0:512 * nk].rearrange("p (k c) -> p k c", k=nk) for z in (hi, lo)]]

        def job_acts(j):
            kc = (j - NFT) % 6
            nk = 4 if kc < 5 else NFT - 20
            raw = actT[:, 4 * kc:4 * kc + nk]
            if j % 2 == 0:
                return [[raw, hhi[:, 0:nk], hhi[:, 4:4 + nk]]]
            z = hlo_at[0][3]
            parts = [[raw[:, 0:2], z[:, 0:2], hlo_at[1][3]]]
            return parts + ([[raw[:, 2:4], z[:, 2:4], hlo_at[2][3]]] if nk == 4 else [])

        def act_pairs(j):
            return [(p[1][:, k], p[2][:, k]) for p in job_acts(j) for k in range(p[0].shape[1])]

        block = ctx.enter_context(nc.Block())

        @block.sync
        def _(sp):
            sp.dma_start(crow[0:1, :], a["c_prompt"]).then_inc(c_loaded, 16)
            sp.dma_start(crow[1:9, :], a["c_sample"]).then_inc(c_loaded, 16)
            def load(i):
                if i >= WR:
                    (kind, n, kh), last = chunks[i - WR]
                    if kind == "in":
                        sp.wait_ge(lo1_ready, 2 * n + kh + 1)
                    elif kind == "cv":
                        sp.wait_ge(lo1_ready, 6 + 2 * n + 2)
                    elif kind == "gu":
                        sp.wait_ge(lo_ready, 2 * n + 2)
                    elif kind == "dn":
                        sp.wait_ge(lo_ready, NFT + 6 * n + kh + 1)
                    else:
                        want_filled(sp, last)
                (kind, n, kh), _ = chunks[i]
                dst, k0, nk, w = wch[:, i % WR], 512 * kh, 4, 512
                if kind == "gu":
                    for x in range(2):
                        c0 = x * NF + 256 * n
                        sp.dma_start(dst[:, :, 256 * x:256 * x + 256],
                                     a["w_gu"][0, k0:k0 + 512, c0:c0 + 256].rearrange("(k p) n -> p k n", p=128)
                                     ).then_inc(w_loaded[i % WR], 16)
                    return
                src, c0 = a[{"ada": "w_ada", "in": "w_in", "cv": "w_in", "wo": "w_o", "dn": "w_down"}[kind]], 512 * n
                if kind == "in":
                    w = min(512, TEND - c0)
                if kind == "cv":
                    c0 = TEND + 512 * (0, 2, 1)[n]
                if kind == "dn" and kh == 5:
                    nk = NFT - 20
                sp.dma_start(dst[:, 0:nk, 0:w],
                             src[0, k0:k0 + 128 * nk, c0:c0 + w].rearrange("(k p) n -> p k n", p=128)
                             ).then_inc(w_loaded[i % WR], 16)

            done = chunk_of["ada", ADA_FIRST, 0]
            for i in range(2):
                load(i)
            for t in range(5):
                sp.dma_start(xs[0:TM[t], t, :], tok_rows("x_prompt", "x_sample", t)).then_inc(x_loaded[t], 16)
            for dst, c0, w in ((modss[:, 0:2048], 0, 2048), (modss2, 3 * D, 2048),
                               (grow[:, 0:D], 2 * D, D), (grow[:, D:2 * D], 5 * D, D)):
                sp.dma_start(dst, a["b_ada"][0:1, c0:c0 + w].to_broadcast([9, w])).then_inc(bias_loaded, 16)
            for i in range(2, done):
                load(i)
            count = 0

            def store(dst, src):
                sp.dma_start(dst, src).then_inc(stored, 16)
                return 1

            for t in range(5):
                want_emptied(sp, ("in", 1, t))
            for c0, name in ((TKC, "p_k_cmp"), (TVC, "p_v_cmp")):
                sp.dma_start(out_rows(name), pj[:, 0:4, c0:c0 + 128]).then_inc(kvc_stored, 16)
            for c0, name in ((TKC, "s_k_cmp"), (TVC, "s_v_cmp"), (TVS, "s_v_slc")):
                count += store(o[name].rearrange("l b q k d -> (l b q) (k d)"), pj[0:TS, 4, c0:c0 + 128])
            count += store(out_rows("p_v_slc"), pj[:, 0:4, TVS:TVS + 128])
            for t in range(5):
                want_emptied(sp, ("in", 2, t))
            count += store(out_rows("p_v_win"), pj[:, 0:4, TVW:TVW + 128])
            for w in ("k", "v"):
                count += store(o[f"s_{w}_win"][0, :, 0:SEQ - NQ].rearrange("b t k d -> b (t k d)"),
                               a[f"state_{w}_win"][0, :, NQ:SEQ].rearrange("b t k d -> b (t k d)"))
            for b in range(NB):
                count += store(o["s_v_win"][0, b, SEQ - NQ:SEQ].rearrange("q k d -> q (k d)"),
                               pj[NQ * b:NQ * b + NQ, 4, TVW:TVW + 128])
            sp.wait_ge(nrm_done, 9)
            for c0, name in ((TKS, "p_k_slc"), (TKW, "p_k_win")):
                count += store(out_rows(name), pj[:, 0:4, c0:c0 + 128])
            count += store(o["s_k_slc"].rearrange("l b q k d -> (l b q) (k d)"), pj[0:TS, 4, TKS:TKS + 128])
            for b in range(NB):
                count += store(o["s_k_win"][0, b, SEQ - NQ:SEQ].rearrange("q k d -> q (k d)"),
                               pj[NQ * b:NQ * b + NQ, 4, TKW:TKW + 128])
            want_emptied(sp, ("ulast",))
            count += store(o["p_conv"].rearrange("l b r f -> (l b r) f"), ulr[0:2, :])
            count += store(o["s_conv"].rearrange("l b r f -> (l b r) f"), ulr[2:18, :])
            assert count == N_STORED
            for i in range(done, done + WR):
                load(i)
            for gp in range(4):
                sp.wait_ge(o_row, gp + 1)
                sp.dma_start(o_rows[2 * gp:2 * gp + 2].rearrange("b h q n -> (b h q) n"),
                             orows[:, 192 * gp:192 * gp + 192]).then_inc(rows_out, 16)
                if gp == 2:
                    for i in range(done + WR, done + WR + 2):
                        load(i)
            sp.wait_ge(rows_out, 64)
            for b in range(NB):
                sp.dma_start(late[NQ * b:NQ * b + NQ, 0:1536].rearrange("q (h n) -> q h n", h=8),
                             o_rows[b].rearrange("h q n -> q h n")).then_inc(rows_back, 16)
            for i in range(done + WR + 2, done + WR + 8):
                load(i)
            want_filled(sp, ("O", 3, 1))
            for t in range(5):
                sp.dma_start(xin[0:TM[t], t, :], tok_rows("x_prompt", "x_sample", t)).then_inc(xin_loaded, 16)
            for i in range(done + WR + 8, len(chunks)):
                load(i)
            for n in range(2):
                for t in range(5):
                    sp.wait_ge(out_ready, 5 * n + t + 1)
                    dst = o["y_prompt"][0, 128 * t:128 * t + 128, :] if t < 4 else o["y_sample"].rearrange("b q d -> (b q) d")
                    count += store(dst[:, 512 * n:512 * n + 512], xs[0:TM[t], t, 512 * n:512 * n + 512])
            sp.wait_ge(kvc_stored, 32)
            sp.wait_ge(stored, 16 * count)

        @block.gpsimd
        def _(pool):
            for b in range(NB):
                pt = a["page_table"]
                pool.dma_start(pti[:, b:b + 1], bass.AP(pt.tensor, 16 * b, [[1, 16], [0, 8], [1, 1]])).then_inc(pages_loaded, 16)
            pool.wait_ge(idx_ready, 1)
            want_filled(pool, ("ada", 1))
            loaded = 0

            def window(gp, x):
                if gp:
                    want_filled(pool, (("T", gp - 1, 4, 1), ("O", gp - 1, 1))[x])
                for b in range(2):
                    pool.dma_start(wnd[:, x, b, :],
                                   a[f"state_{'kv'[x]}_win"][0, 2 * gp + b].rearrange("(c s) k d -> c (s k d)", s=4)
                                   ).then_inc(win_loaded[x], 16)

            for i, (name, b, last) in enumerate(caches):
                if i >= CR:
                    want_filled(pool, caches[i - CR][2])
                elif i:
                    want_filled(pool, ("cv", 2, 3, 1))
                slot = cring[:, i % CR, :]
                if b is None:
                    pool.wait_ge(kvc_stored, 32)
                    pool.dma_start(slot[0:PCH, :], o[name].rearrange("l b (c s) k d -> (l b c) (s k d)", s=16)
                                   ).then_inc(cache_loaded[i % CR], 16)
                else:
                    pool.indirect_dma_start(slot, None, a[name].rearrange("l n (c s) k d -> (l n c) (s k d)", s=16),
                                            bass.IndirectOffsetOnAxis(idx[:, b:b + 1], 0)).then_inc(cache_loaded[i % CR], 16)
                if i >= 18 and i % 2 == 1:
                    window((i - 18) // 4, (i - 18) % 4 // 2)
            def gates_store(l):
                want_emptied(pool, ("ada", (4, 10)[l]))
                want_emptied(pool, ("ada", (5, 11)[l]))
                pool.dma_start(g_rows[:, 1024 * l:1024 * l + 1024], grow[:, 1024 * l:1024 * l + 1024]).then_inc(gates_out, 16)

            def gates_load(l):
                pool.wait_ge(gates_out, 16 * (l + 1))
                pool.dma_start(gbc[:, 0, :], g_rows[0:1, 1024 * l:1024 * l + 1024].to_broadcast([128, 1024])).then_inc(gates_in, 16)
                pool.dma_start(gbc[0:TS, 1, :], bass.AP(g_rows.tensor, 2048 + 1024 * l, [[2048, NB], [0, NQ], [1, 1024]])
                               ).then_inc(gates_in, 16)

            gates_store(0)
            want_filled(pool, ("pO", 3, 0))
            gates_load(0)
            gates_store(1)
            for t in range(4):
                pool.wait_ge(h_high, t + 1)
                cols = slice(128 * t, 128 * t + 128)
                for k0, n, z, zl in hlo_at[1:]:
                    ins = low(pool, zl[:, :, cols], z[:, :, cols], hhi[:, k0:k0 + n, cols])
                ins.then_inc(h_low2, 1)
                if t == 1:
                    pool.wait_ge(hi_ready, 1)
                    for raw, hi, lo in job_parts(0):
                        ins = low(pool, lo, raw, hi)
                    ins.then_inc(lo_ready, 1)
            pool.wait_ge(x1_ready, 10)
            gates_load(1)

        def spread_chunks(copy, u, i, n):
            key = ("xt", u, i)
            for k in range(2):
                ins = copy(xcmp[64 * (i % 2):64 * (i % 2) + 64, u % 2, 4 * (i // 2):4 * (i // 2) + 4, k, 0:n],
                           ps(key)[64 * k:64 * k + 64, :].rearrange("p (j c) -> p j c", j=4)[:, :, 0:n])
            frees(ins, key)


        @block.scalar
        def _(act):
            steps = [0]

            def link(ins):
                steps[0] += 1
                ins.then_inc(act_step, 1)
                act.wait_ge(act_step, steps[0])

            act.dma_start(cst[:, 0:C_ROPE], a["consts"][:, 0:C_ROPE]).then_inc(ident_loaded, 16)
            act.wait_ge(c_loaded, 32)
            act.activation(scrow, crow, ACT.Silu).then_inc(scrow_ready, 1)
            r0 = 0
            for name, n in (("ln1_g", 8), ("ln2_g", 8), ("attn_out_g", 4), ("conv_out_g", 4)):
                act.dma_start(rowb[r0:r0 + n, :], a[name].rearrange("l (k p) -> (l k) p", p=128)).then_inc(gains_loaded, 16)
                r0 += n
            act.dma_start(rowb[24:36, :], a["w_conv"].rearrange("l w (k p) -> (l w k) p", p=128)).then_inc(gains_loaded, 16)
            act.dma_start(rowb[36:52, :], a["pe_cmp"].rearrange("l (k s) d -> (l k) (s d)", s=2)).then_inc(gains_loaded, 16)
            act.dma_start(gains[:, 0:64], a["q_norm_g"].to_broadcast([128, 64])).then_inc(gains_loaded, 16)
            for i in range(3):
                act.dma_start(gains[:, 64 + 64 * i:128 + 64 * i], a["k_norm_g"][0, i:i + 1, :].to_broadcast([128, 64])
                              ).then_inc(gains_loaded, 16)
            act.dma_start(stc, a["state_conv"].rearrange("l b r f -> (l b r) f")).then_inc(conv_state_loaded, 16)
            for x, w in enumerate(("w_ck1", "w_cv1")):
                for r in range(2):
                    act.dma_start(w1v[:, x, :, r, :], a[w][0, 1024 * r:1024 * r + 1024, :].rearrange("(j p) h -> p j h", p=128)
                                  ).then_inc(comp_w_loaded, 16)
            for x, w in enumerate(("w_ck2", "w_cv2")):
                act.dma_start(w2[:, 64 * x:64 * x + 64], a[w][0]).then_inc(comp_w_loaded, 16)
            act.dma_start(cst[:, C_ROPE:C_END], a["consts"][:, C_ROPE:C_END]).then_inc(consts_loaded, 16)
            act.wait_ge(cleared, 1)
            for t in range(5):
                act.wait_ge(x_loaded[t], 16)
                if t:
                    act.wait_ge(x_square, t)
                act.activation(hbuf[0:TM[t], 0:D], xs[0:TM[t], t, :], ACT.Square, accum_out=small[0:TM[t], t:t + 1]
                               ).then_inc(x_square, 1)
            act.wait_ge(x_square, 5)
            act.activation(small[:, 8:13], small[:, 0:5], ACT.Sqrt, bias=epst[:, 0:1], scale=1.0 / D).then_inc(x_root, 1)
            for t in range(5):
                want_filled(act, ("xT", t, 1))
                frees(act.copy(hT[:, 4:8, 128 * t:128 * t + TM[t]],
                               ps(("xT", t, 1))[:, 0:4 * TM[t]].rearrange("p (k n) -> p k n", k=4)), ("xT", t, 1))
            want_emptied(act, ("mod", 0))
            for t in range(5):
                want_emptied(act, ("xT", t, 1))
            for k in range(4, 8):
                link(act.activation(hT[:, k, 0:SEQ], hT[:, k, 0:SEQ], ACT.Identity, bias=mod[:, 0, 1, k, 0:1],
                                    scale=mod[:, 0, 0, k, 0:1]))
            act.wait_ge(h1_sample, 1)
            for k in range(8):
                act.wait_ge(h1_mod, min(k + 1, 4))
                high(act.copy, h1hi[k], hT[:, k]).then_inc(h1_hi, 1)

            def high_job1(j):
                if j >= 2:
                    job1_read(act, j - 2)
                for key, raw, hi, lo in job1_parts(j):
                    weights(act, key)
                    ins = high(act.copy, hi, raw)
                ins.then_inc(hi1_ready, 1)

            for j in range(3):
                high_job1(j)
            for n in (0, 2):
                if n == 2:
                    for j in range(3, 7):
                        high_job1(j)
                w = min(512, TEND - 512 * n)
                for t in range(5):
                    want_filled(act, ("in", n, t))
                    dst, src = pj[0:TM[t], t, 512 * n:512 * n + w], ps(("in", n, t))[0:TM[t], 0:w]
                    if n == 0:
                        dst = dst.rearrange("p (g k d) -> p g k d", g=4, k=2)
                        src = src.rearrange("p (k g d) -> p g k d", k=2, g=4)
                    frees(act.copy(dst, src), ("in", n, t))
            high_job1(7)
            for m in range(4):
                if m == 2:
                    high_job1(8)
                for h in range(2):
                    want_filled(act, ("cv", 0, m, h))
                    frees(act.copy(hcT[:, m, HALF * h:HALF * h + HALF], ps(("cv", 0, m, h))[:, 0:HALF]), ("cv", 0, m, h))
            for j in range(9, 12):
                high_job1(j)
            for m in range(4):
                act.wait_ge(y_ready, m + 1)
                act.activation(hcT[:, m, :], vT[:, m, :], ACT.Square).then_inc(y_square, 1)
            want_filled(act, ("ulast",))
            frees(act.copy(ulr, ps(("ulast",))[0:18, :]), ("ulast",))
            def nrm(group):
                act.wait_ge(nrm_square, NORM_GROUP[group][-1] + 1)
                c0, c1 = norm_cols(group)
                act.activation(hrt[:, c0:c1], hss[:, c0:c1], ACT.Sqrt, bias=epst[:, 0:1], scale=1.0 / HD
                               ).then_inc(nrm_root, 1)

            def spread(u):
                for i in (0, 2):
                    if u >= 2:
                        want_filled(act, ("pre", u - 2))
                    want_filled(act, ("xt", u, i))
                    spread_chunks(act.copy, u, i, CH if u < 16 else PCH)

            spread(0)
            for h in range(2):
                want_filled(act, ("yss", h))
                frees(act.activation(yrs[:, HALF * h:HALF * h + HALF], ps(("yss", h))[:, 0:HALF], ACT.Sqrt,
                                     bias=epst[:, 0:1], scale=1.0 / 512), ("yss", h))
            for u in range(18):
                n, m = (CH, NC) if u < 16 else (PCH, PNC)
                if u < 17:
                    spread(u + 1)
                if u in ROOT_AT:
                    nrm(ROOT_AT.index(u))
                want_filled(act, ("pre", u))
                if u:
                    act.wait_ge(silu_ready, u)
                act.copy(half[:, :, 0:m], ps(("pre", u))[64:128, 0:2 * n].rearrange("p (k c) -> p k c", k=2)[:, :, 1:n]
                         ).then_inc(half_ready, 1)
                want_emptied(act, ("pre", u))
                if u:
                    want_filled(act, ("cmp", u - 1))
                x = u % 2
                act.activation(slu[:, :, 0:m], half[:, :, 0:m], ACT.Silu, bias=pebt[:, x:x + 1]).then_inc(silu_ready, 1)
            for g in range(G):
                want_filled(act, ("qT", g, 0))
                frees(act.copy(qTp[:, g, :], ps(("qT", g, 0))[:, :]), ("qT", g, 0))
            for x in range(2):
                want_filled(act, ("kT", x))
                frees(act.copy(kTp[:, x, :], ps(("kT", x))[:, :]), ("kT", x))
            def key_part(gp, c):
                want_filled(act, ("T", gp, c, 0))
                if c >= 2:
                    want_filled(act, ("S", gp, c - 2))
                elif gp:
                    want_filled(act, ("S", gp - 1, c + 3))
                frees(act.copy(kTc[:, 0, c % 2, :], ps(("T", gp, c, 0))[:, :]), ("T", gp, c, 0))

            key_part(0, 0)
            key_part(0, 1)
            nrm(3)
            act.activation(gat[:, 0:96].rearrange("p (t n) -> p t n", t=4), pj[:, 0:4, TG:TEND], ACT.Exp, scale=-1.0).then_inc(gate_exp, 1)
            act.activation(gat[0:TS, 96:120], pj[0:TS, 4, TG:TEND], ACT.Exp, scale=-1.0).then_inc(gate_exp, 1)
            for i in range(3):
                want_filled(act, ("kct", i))
                nb, m = (4, NC) if i < 2 else (1, PNC)
                frees(act.copy(kcT[:, 4 * i:4 * i + nb, 0:m],
                               ps(("kct", i))[:, :].rearrange("p (b n) -> p b n", b=4)[:, 0:nb, 0:m]), ("kct", i))

            def cmp_exp(gp):
                want_emptied(act, ("cS", gp))
                act.activation(csb, csb, ACT.Exp, bias=small[:, 100:101], scale=-1.0, accum_out=small[:, 101:102]).then_inc(c_exp, 1)

            def cmp_turned(gp):
                want_filled(act, ("cPT", gp))
                if gp:
                    want_filled(act, ("cO", gp - 1))
                frees(act.copy(ctb, ps(("cPT", gp))[0:NC, 0:128]), ("cPT", gp))

            def cmp_rows(gp):
                want_filled(act, ("cO", gp))
                for i in range(4):
                    r = slice(32 * i, 32 * i + 32)
                    ins = act.copy(orow[r, gp, 0, :], ps(("cO", gp))[r, 64 * (i % 2):64 * (i % 2) + 64])
                frees(ins, ("cO", gp))

            def cmp_prob(t):
                act.wait_ge(p_in, t + 1)
                act.activation(pct[:, :], pct[:, :], ACT.Exp, scale=QS).then_inc(p_exp, 1)

            cmp_exp(0)
            cmp_turned(0)
            cmp_rows(0)
            for gp in range(4):
                more = gp < 3
                key_part(gp, 2)
                if more:
                    cmp_exp(gp + 1)
                key_part(gp, 3)
                key_part(gp, 4)
                if more:
                    cmp_turned(gp + 1)
                act.wait_ge(s_min, gp + 1)
                act.activation(ssb, ssb, ACT.Exp, bias=small[:, 112:113], scale=-1.0, accum_out=small[:, 114:115]).then_inc(s_exp, 1)
                act.activation(wsb, wsb, ACT.Exp, bias=small[:, 113:114], scale=-1.0, accum_out=small[:, 115:116]).then_inc(s_exp, 1)
                for i in (0, 2, 4):
                    want_filled(act, ("PT", gp, i))
                    dst = pTw if i == 4 else pT[:, 4 * i:4 * i + 4, :]
                    frees(act.copy(dst, ps(("PT", gp, i))[:, :].rearrange("p (s n) -> p s n", s=4)), ("PT", gp, i))
                if more:
                    key_part(gp + 1, 0)
                    key_part(gp + 1, 1)
                    cmp_rows(gp + 1)
                else:
                    cmp_prob(0)
            def out_square(t):
                P = TM[t]
                act.wait_ge(attn_ready, OUT_ORDER.index(t) + 1)
                link(act.activation(sqo[0:P, :], pj[0:P, t, 0:512], ACT.Square, accum_out=small[0:P, t:t + 1]))

            def out_root():
                act.activation(small[:, 8:13], small[:, 0:5], ACT.Sqrt, bias=epst[:, 0:1], scale=1.0 / 512).then_inc(a_root, 1)

            for g in range(NG + LAG):
                t, br, i = head(g)
                if g < NG:
                    want_emptied(act, ("pS", g))
                    w, c0 = 128 * (t + 1), 128 + 8 * br + i
                    act.activation(psb[g % 5][:, 0:w], psb[g % 5][:, 0:w], ACT.Exp, bias=small[:, 144 + i:145 + i],
                                   scale=-1.0, accum_out=small[:, c0:c0 + 1]).then_inc(p_soft, 1)
                    if br == 0 and i == 0:
                        for hh in range(2):
                            want_filled(act, ("pcPT", t, hh))
                            frees(act.copy(ppTc[:, 4 * hh:4 * hh + 4, :],
                                           ps(("pcPT", t, hh))[0:PNC, :].rearrange("p (h n) -> p h n", h=4)), ("pcPT", t, hh))
                if g >= LAG:
                    v = g - LAG
                    key, n = ("pPT", v), head(v)[0] + 1
                    want_filled(act, key)
                    frees(act.copy(ppT[v % 4][:, 0:n, :], ps(key)[:, 0:128 * n].rearrange("p (k n) -> p k n", n=128)), key)
                if g < NG:
                    if t < 3 and br and i == 1:
                        cmp_prob(t + 1)
                    if i == 5 and (t, br) in SQUARE:
                        out_square(SQUARE[t, br])
                        if t == 3:
                            out_root()
            out_square(3)
            out_root()

            def second_half(t):
                want_filled(act, ("hT", t, 1))
                cols = slice(128 * t, 128 * t + 128)
                for k in range(4, 8):
                    ins = act.activation(hraw[k][:, cols], ps(("hT", t, 1))[:, 128 * (k - 4):128 * (k - 3)],
                                         ACT.Identity, bias=mod[:, 1, 1, k, 0:1], scale=mod[:, 1, 0, k, 0:1])
                frees(ins, ("hT", t, 1))
                want_emptied(act, ("hT", t, 1))
                for k0, n, z, _ in hlo_at[1:]:
                    ins = high(act.copy, hhi[:, k0:k0 + n, cols], z[:, :, cols])
                ins.then_inc(h_high, 1)

            def high_job(j):
                if j >= 2:
                    reads_job(j - 2)(act)
                keys = [("gu", j // 2, kh) for kh in range(2)] if j < NFT else [("dn",) + divmod(j - NFT, 6)]
                for key, (raw, hi, lo) in zip(keys, job_parts(j)):
                    weights(act, key)
                    ins = high(act.copy, hi, raw)
                if j >= NFT:
                    kc = (j - NFT) % 6
                    if j == NFT:
                        ins.then_inc(hi_ready, 1)
                    if j < NFT + 2:
                        want_filled(act, ("gu", NFT - 1, 1, 1))
                    for k in range(4 * kc, min(4 * kc + 4, NFT)):
                        for h in range(2):
                            want_emptied(act, ("gu", k, 1, h))
                    if j == NFT:
                        for k in range(4):
                            ins = high(act.copy, hhi[:, k], actT[:, k])
                            ins.then_inc(first_high, 1)
                        return
                    for raw, hi, lo in job_acts(j):
                        ins = high(act.copy, hi, raw)
                ins.then_inc(hi_ready, 1)

            for t in range(6):
                if t < 5:
                    act.wait_ge(x1_ready, 5 + t + 1)
                    if t:
                        act.wait_ge(x1_square, t)
                    act.activation(late[0:TM[t], 0:D], xs[0:TM[t], t, :], ACT.Square, accum_out=small[0:TM[t], 16 + t:17 + t]
                                   ).then_inc(x1_square, 1)
                    act.wait_ge(x1_square, t + 1)
                    act.activation(small[0:TM[t], 24 + t:25 + t], small[0:TM[t], 16 + t:17 + t], ACT.Sqrt,
                                   bias=epst[0:TM[t], 0:1], scale=1.0 / D).then_inc(x1_root, 1)
                if t == 4:
                    want_filled(act, ("wo", 1, 4))
                    high_job(1)
                if 1 <= t < 5:
                    second_half(t - 1)
                if t == 1:
                    high_job(0)
            for i, h in GU_ORDER:
                want_filled(act, ("gu", i, 0, h))
                if i >= 2:
                    want_emptied(act, ("gu", i - 2, 1, h))
                frees(act.activation(sgb[:, i % 2, HALF * h:HALF * h + HALF], ps(("gu", i, 0, h))[:, 0:HALF], ACT.Silu),
                      ("gu", i, 0, h))
                if (i, h) == (0, 1):
                    high_job(2)
                if i > 1 and h == 0:
                    high_job(i + 1)
            for j in range(NFT + 1, NFT + 12):
                high_job(j)

        @block.vector
        def _(dve):
            steps = [0]

            def link(ins):
                steps[0] += 1
                ins.then_inc(dve_step, 1)
                dve.wait_ge(dve_step, steps[0])

            link(dve.memset(epst[:, :], EPS))
            link(dve.memset(small[:, :], 1.0))
            link(dve.memset(hss[:, :], 1.0))
            dve.memset(sel32[:, :], 0.0).then_inc(cleared, 1)
            dve.wait_ge(cleared, 1)
            dve.wait_ge(ident_loaded, 16)
            def evac(key, dst, src):
                want_filled(dve, key)
                frees(dve.tensor_copy(dst, src), key)

            evac(("cT",), cT[:, :], ps(("cT",))[:, 0:72])
            dve.wait_ge(x_root, 1)
            link(dve.reciprocal(small[:, 16:21], small[:, 8:13]))
            for t in range(5):
                dve.tensor_scalar(xs[0:TM[t], t, :], xs[0:TM[t], t, :], small[0:TM[t], 16 + t:17 + t], None, ALU.mult
                                  ).then_inc(xn_ready, 1)
            dve.wait_ge(pages_loaded, 128)
            dve.scalar_tensor_tensor(idx[:, :], pti[:, :], 8.0, cst[:, C_P8:C_P8 + 1].to_broadcast([128, 8]), ALU.mult, ALU.add
                                     ).then_inc(idx_ready, 1)

            dve.wait_ge(bias_loaded, 64)

            def mod_cols(l):
                key = ("mod", l)
                want_filled(dve, key)
                v = ps(key)[:, 0:144].rearrange("p (x k b) -> p x k b", x=2, k=8)
                link(dve.tensor_copy(mod[:, l, 1], v[:, 0]))
                frees(dve.scalar_tensor_tensor(mod[:, l, 0], v[:, 1], 1.0,
                                               colT[:, 8 * l:8 * l + 8].unsqueeze(2).to_broadcast([128, 8, 9]),
                                               ALU.add, ALU.mult), key)

            def ada_rows(n):
                tensor, c0 = (modss, modss, grow, modss2, modss2, grow)[n // 2], 512 * n - (0, 0, 2048, 3072, 3072, 4096)[n // 2]
                dst = tensor[:, c0:c0 + 512]
                want_filled(dve, ("ada", n))
                frees(dve.tensor_tensor(dst, ps(("ada", n))[0:9, :], dst, ALU.add), ("ada", n))

            for n in range(ADA_FIRST):
                ada_rows(n)
                if n == 1:
                    evac(("rows",), colT[:, :], ps(("rows",))[:, 0:52])
                    for t in range(5):
                        evac(("xT", t, 0), hT[:, 0:4, 128 * t:128 * t + TM[t]],
                             ps(("xT", t, 0))[:, 0:4 * TM[t]].rearrange("p (k n) -> p k n", k=4))
                if n == 3:
                    mod_cols(0)
                    evac(("sconv",), stT[:, :], ps(("sconv",))[:, 0:64])
                    for t in range(5):
                        want_emptied(dve, ("xT", t, 0))
                        want_emptied(dve, ("xT", t, 1))
                    want_emptied(dve, ("mod", 0))
                    sv = hT[:, :, SEQ:TOK].rearrange("p k (b q) -> p k b q", b=8)
                    link(dve.tensor_tensor(sv, sv, mod[:, 0, 0, :, 1:9].unsqueeze(3).to_broadcast([128, 8, 8, 8]), ALU.mult))
                    link(dve.tensor_tensor(sv, sv, mod[:, 0, 1, :, 1:9].unsqueeze(3).to_broadcast([128, 8, 8, 8]), ALU.add))
                    dve.tensor_copy(small[:, 249:250], sv[:, 0, 0, 0:1]).then_inc(h1_sample, 1)
                    for k in range(4):
                        dve.tensor_scalar(hT[:, k, 0:SEQ], hT[:, k, 0:SEQ], mod[:, 0, 0, k, 0:1], mod[:, 0, 1, k, 0:1],
                                          ALU.mult, ALU.add).then_inc(h1_mod, 1)
                    for k in range(8):
                        dve.wait_ge(h1_hi, k + 1)
                        low(dve, h1lo[k], hT[:, k], h1hi[k]).then_inc(hT_ready, 1)
            for x in range(2):
                evac(("peb", x), pebt[:, x:x + 1], ps(("peb", x))[0:64, 0:1])

            def low_job1(j):
                dve.wait_ge(hi1_ready, j + 1)
                for key, raw, hi, lo in job1_parts(j):
                    ins = low(dve, lo, raw, hi)
                ins.then_inc(lo1_ready, 1)

            for j in range(5):
                low_job1(j)
            dve.wait_ge(consts_loaded, 16)
            for t in range(5):
                evac(("in", 1, t), pj[0:TM[t], t, 512:1024], ps(("in", 1, t))[0:TM[t], :])

            for j in range(5, 10):
                low_job1(j)

            def conv(m):
                w = [colT[:, 24 + 4 * k + m:25 + 4 * k + m] for k in range(3)]
                y, u = vT[:, m, :], uT[:, m, :]
                ys, us = (z[:, SEQ:TOK].rearrange("p (b q) -> p b q", b=8) for z in (y, u))
                st = stT[:, 16 * m:16 * m + 16].rearrange("p (b r) -> p b r", b=8)

                def tap(dst, src, k):
                    link(dve.scalar_tensor_tensor(dst, src, w[k], dst, ALU.mult, ALU.add))

                link(dve.tensor_scalar(y, u, w[2], None, ALU.mult))
                tap(y[:, 1:SEQ], u[:, 0:SEQ - 1], 1)
                tap(y[:, 2:SEQ], u[:, 0:SEQ - 2], 0)
                tap(ys[:, :, 1:8], us[:, :, 0:7], 1)
                tap(ys[:, :, 2:8], us[:, :, 0:6], 0)
                tap(ys[:, :, 0:1], st[:, :, 1:2], 1)
                tap(ys[:, :, 0:2], st, 0)

            for m in range(4):
                for h in range(2):
                    key = ("cv", 1, m, h)
                    want_filled(dve, key)
                    want_emptied(dve, ("cv", 0, m, h))
                    frees(dve.tensor_tensor(uT[:, m, HALF * h:HALF * h + HALF], ps(key)[:, 0:HALF],
                                            hcT[:, m, HALF * h:HALF * h + HALF], ALU.mult), key)
                want_emptied(dve, ("cv", 1, m, 0))
                want_emptied(dve, ("cv", 1, m, 1))
                conv(m)
                if m % 2:
                    low_job1(10 + m // 2)
            ul = ulast[:, :].rearrange("p (m c) -> p m c", m=4)
            link(dve.tensor_copy(ul[:, :, 0:2], uT[:, :, SEQ - 2:SEQ]))
            for m in range(4):
                dve.tensor_copy(ul[:, m, 2:18].rearrange("p (b r) -> p b r", b=8),
                                uT[:, m, SEQ:TOK].rearrange("p (b q) -> p b q", b=8)[:, :, 6:8]).then_inc(u_end_ready, 1)
            for m in range(4):
                for h in range(2):
                    key = ("cv", 2, m, h)
                    want_filled(dve, key)
                    y = vT[:, m, HALF * h:HALF * h + HALF]
                    frees(dve.tensor_tensor(y, ps(key)[:, 0:HALF], y, ALU.mult), key)
                want_emptied(dve, ("cv", 2, m, 1))
                dve.tensor_copy(small[:, 250:251], vT[:, m, 0:1]).then_inc(y_ready, 1)
                dve.wait_ge(y_ready, m + 1)
            def scale_conv():
                want_emptied(dve, ("yss", 0))
                want_emptied(dve, ("yss", 1))
                link(dve.reciprocal(yrs, yrs))
                for m in range(4):
                    dve.scalar_tensor_tensor(vT[:, m, :], vT[:, m, :], colT[:, 20 + m:21 + m], yrs, ALU.mult, ALU.mult
                                             ).then_inc(vT_ready, 1)
                dve.wait_ge(vT_ready, 4)

            def norm_view(i):
                name, P, n, t0, nt, nh, gain = NORMS[i]
                if name == "kcm":
                    for b in range(t0, t0 + nt):
                        want_emptied(dve, ("cmp", 2 * b))
                    v = kcm[0:P, t0:t0 + nt, :]
                else:
                    for t in range(t0, t0 + nt):
                        want_emptied(dve, ("in", {"q": 0, "ks": 1, "kw": 2}[name], t))
                    c0 = {"q": TQ, "ks": TKS, "kw": TKW}[name]
                    v = pj[0:P, t0:t0 + nt, c0:c0 + 64 * nh]
                return v.rearrange("p t (h d) -> p t h d", h=nh)

            def norm_sum(i):
                name, P, n, t0, nt, nh, gain = NORMS[i]
                v, q = norm_view(i), sqb[0:P, 0:64 * n].rearrange("p (t h d) -> p t h d", t=nt, h=nh)
                link(dve.tensor_tensor(q, v, v, ALU.mult))
                dve.tensor_reduce(hss[0:P, NORM_COL[i]:NORM_COL[i] + n], q, AX, ALU.add).then_inc(nrm_square, 1)
                dve.wait_ge(nrm_square, i + 1)

            def norm_inverse(group):
                c0, c1 = norm_cols(group)
                dve.wait_ge(nrm_root, group + 1)
                link(dve.reciprocal(hss[:, c0:c1], hrt[:, c0:c1]))

            def norm_apply(i):
                name, P, n, t0, nt, nh, gain = NORMS[i]
                v = norm_view(i)
                rs = hss[0:P, NORM_COL[i]:NORM_COL[i] + n].rearrange("p (t h) -> p t h", t=nt).unsqueeze(3).to_broadcast([P, nt, nh, 64])
                link(dve.tensor_tensor(v, v, rs, ALU.mult))
                gn = gains[0:P, 64 * gain:64 * gain + 64].unsqueeze(1).unsqueeze(1).to_broadcast([P, nt, nh, 64])
                link(dve.tensor_tensor(v, v, gn, ALU.mult))
                if name == "kcm":
                    cs = cst[0:P, C_ROPEC:C_ROPEC + 16].unsqueeze(1).to_broadcast([P, nt, 16])
                else:
                    cs = cst[0:P, C_ROPE + 16 * t0:C_ROPE + 16 * (t0 + nt)].rearrange("p (t c) -> p t c", t=nt)
                cos, sin = (cs[:, :, x:x + 8].unsqueeze(2).to_broadcast([P, nt, nh, 8]) for x in (0, 8))
                x1, x2 = v[:, :, :, 0:8], v[:, :, :, 8:16]
                r = [ropb[0:P, 256 * j:256 * j + 8 * n].rearrange("p (t h d) -> p t h d", t=nt, h=nh) for j in range(4)]
                dve.tensor_tensor(r[0], x1, cos, ALU.mult)
                dve.tensor_tensor(r[1], x2, sin, ALU.mult)
                dve.tensor_tensor(r[2], x2, cos, ALU.mult)
                link(dve.tensor_tensor(r[3], x1, sin, ALU.mult))
                dve.tensor_tensor(x1, r[0], r[1], ALU.subtract)
                dve.tensor_tensor(x2, r[2], r[3], ALU.add).then_inc(nrm_done, 1)
                dve.wait_ge(nrm_done, i + 1)

            want_filled(dve, ("cv", 2, 3, 1))
            link(dve.memset(qblk, 0.0))

            def cmp_evac(u):
                b, x, m = u // 2, u % 2, (NC if u < 16 else PNC)
                evac(("cmp", u), (vcm if x else kcm)[0:m, b, :], ps(("cmp", u))[0:m, 0:128])

            def spread(u):
                for i in (1, 3):
                    if u >= 2:
                        want_filled(dve, ("pre", u - 2))
                    want_filled(dve, ("xt", u, i))
                    spread_chunks(dve.tensor_copy, u, i, CH if u < 16 else PCH)

            spread(0)
            for u in range(18):
                n, m = (CH, NC) if u < 16 else (PCH, PNC)
                if u < 17:
                    spread(u + 1)
                if u >= 2:
                    cmp_evac(u - 2)
                if u == 0:
                    scale_conv()
                for i in SUM_AT.get(u, ()):
                    norm_sum(i)
                if u in ROOT_AT:
                    norm_inverse(ROOT_AT.index(u))
                for i in APPLY_AT.get(u, ()):
                    norm_apply(i)
                want_filled(dve, ("pre", u))
                dve.wait_ge(half_ready, u + 1)
                frees(dve.tensor_tensor(half[:, :, 0:m], half[:, :, 0:m],
                                        ps(("pre", u))[0:64, 0:2 * n].rearrange("p (k c) -> p k c", k=2)[:, :, 0:m], ALU.add),
                      ("pre", u))
            cmp_evac(16)
            qv = qblk.rearrange("p (b k g q) -> p b k g q", b=8, k=2, g=4)
            for g in range(G):
                key = ("qT", g, 1)
                want_filled(dve, key)
                for k in range(2):
                    r = slice(64 * k, 64 * k + 64)
                    ins = dve.tensor_copy(qv[r, :, k, g, :], ps(key)[r, 0:TS].rearrange("p (b q) -> p b q", b=8))
                frees(ins, key)
            evac(("kTn",), kTn, ps(("kTn",))[:, 0:128].rearrange("p (x n) -> p x n", x=2))
            cmp_evac(17)
            def key_part(gp, c):
                if c >= 2:
                    want_filled(dve, ("S", gp, c - 2))
                elif gp:
                    want_filled(dve, ("S", gp - 1, c + 3))
                evac(("T", gp, c, 1), kTc[:, 1, c % 2, :], ps(("T", gp, c, 1))[:, :])

            key_part(0, 0)
            key_part(0, 1)
            norm_sum(11)
            norm_inverse(3)
            norm_apply(11)
            dve.wait_ge(gate_exp, 2)
            for z in (gat[:, 0:96], gat[0:TS, 96:120]):
                link(dve.tensor_scalar(z, z, 1.0, None, ALU.add))
                link(dve.reciprocal(z, z))
            def cmp_scores(gp):
                key = ("cS", gp)
                want_filled(dve, key)
                if gp:
                    want_filled(dve, ("cPT", gp - 1))
                frees(dve.tensor_tensor_reduce(csb, ps(key)[:, 0:NC], cst[:, C_CAUS:C_CAUS + NC], -QS, 3e38, ALU.add, ALU.min,
                                               small[:, 100:101]), key)

            def cmp_probs(gp):
                dve.wait_ge(c_exp, gp + 1)
                link(dve.reciprocal(small[:, 102:103], small[:, 101:102]))
                dve.tensor_scalar(csb, csb, small[:, 102:103], None, ALU.mult).then_inc(c_prob, 1)

            def cmp_groups(gp):
                want_emptied(dve, ("cPT", gp))
                link(dve.tensor_reduce(cpg, ctb.rearrange("p (a g q) -> p a q g", a=4, g=4), AX, ALU.add))
                dve.tensor_copy(cpx.rearrange("p (a g q) -> p a g q", a=4, g=4), cpg.unsqueeze(2).to_broadcast([NC, 4, 4, 8])
                                ).then_inc(c_group, 1)

            def cmp_importance(gp):
                evac(("imp", gp), imps[:, :], ps(("imp", gp))[:, 1:31])

            def cmp_select(gp):
                want_emptied(dve, ("imp", gp))
                vi = imps[:, :].unsqueeze(1).to_broadcast([128, NC1, NC1])
                vj = imps[:, :].unsqueeze(2).to_broadcast([128, NC1, NC1])
                r1, r2 = (z.rearrange("p (j i) -> p j i", j=NC1) for z in (rk1, rk2))
                dve.tensor_tensor(r1, vi, vj, ALU.is_gt)
                link(dve.tensor_tensor(r2, vi, vj, ALU.is_equal))
                link(dve.tensor_tensor(rk2, rk2, cst[:, C_TRI:C_TRI + 900], ALU.mult))
                link(dve.tensor_tensor(rk1, rk1, rk2, ALU.add))
                link(dve.tensor_reduce(sel32[:, 1:31], r1, AX, ALU.add))
                link(dve.tensor_scalar(sel32[:, 1:31], sel32[:, 1:31], NSEL_FREE - 0.5, NEG, ALU.is_gt, ALU.mult))
                link(dve.tensor_copy(selb[:, 128 * gp:128 * gp + 128].rearrange("p (j c) -> p j c", j=32),
                                     sel32[:, :].unsqueeze(2).to_broadcast([128, 32, 4])))

            def masked(key, dst, src, mask, col):
                want_filled(dve, key)
                return dve.tensor_tensor_reduce(dst, src, mask, -QS, 3e38, ALU.add, ALU.min, small[:, 104 + col:105 + col])

            def scores(gp, c):
                key = ("S", gp, c)
                if c < 4:
                    m = selb[:, 128 * gp:128 * gp + 128].unsqueeze(1).to_broadcast([128, 4, 128])
                    ins = masked(key, ssb[:, 512 * c:512 * c + 512].rearrange("p (s n) -> p s n", s=4),
                                 ps(key)[:, :].rearrange("p (s n) -> p s n", s=4), m, c)
                else:
                    ins = masked(key, wsb[:, 0:512], ps(key)[:, :], cst[:, C_WIN:C_WIN + 512], 5)
                frees(ins, key)

            def cmp_shifted(t):
                if t:
                    want_filled(dve, ("pcPT", t - 1, 1))
                mb = cst[:, C_CMB + PNC * t:C_CMB + PNC * (t + 1)].unsqueeze(1).to_broadcast([128, 4, PNC])
                for k in range(NKV):
                    key = ("pcS", t, k)
                    want_filled(dve, key)
                    frees(dve.tensor_tensor(pcp[:, 4 * k:4 * k + 4, :], ps(key)[:, 0:4 * PNC].rearrange("p (h n) -> p h n", h=4),
                                            mb, ALU.add), key)
                    want_emptied(dve, key)
                link(dve.tensor_reduce(small[:, 160:168], pcp, AX, ALU.max))
                dve.tensor_tensor(pcp, pcp, small[:, 160:168].unsqueeze(2).to_broadcast([128, 8, PNC]), ALU.subtract
                                  ).then_inc(p_in, 1)

            def cmp_normed(t):
                dve.wait_ge(p_exp, t + 1)
                m01 = cst[:, C_CM01 + PNC * t:C_CM01 + PNC * (t + 1)].unsqueeze(1).to_broadcast([128, 8, PNC])
                link(dve.tensor_tensor(pcp, pcp, m01, ALU.mult))
                link(dve.tensor_reduce(small[:, 160:168], pcp, AX, ALU.add))
                link(dve.tensor_scalar(small[:, 160:168], small[:, 160:168], 1e-30, None, ALU.max))
                link(dve.reciprocal(small[:, 160:168], small[:, 160:168]))
                dve.tensor_tensor(pcp, pcp, small[:, 160:168].unsqueeze(2).to_broadcast([128, 8, PNC]), ALU.mult
                                  ).then_inc(p_prob, 1)

            dve.wait_ge(stored, 16 * N_STORED)
            cmp_scores(0)
            cmp_probs(0)
            cmp_groups(0)
            cmp_importance(0)
            cmp_select(0)
            for gp in range(4):
                more = gp < 3
                if gp:
                    want_filled(dve, ("PT", gp - 1, 5))
                scores(gp, 0)
                key_part(gp, 2)
                scores(gp, 1)
                if more:
                    cmp_scores(gp + 1)
                key_part(gp, 3)
                scores(gp, 2)
                key_part(gp, 4)
                if more:
                    cmp_probs(gp + 1)
                scores(gp, 3)
                scores(gp, 4)
                nm = cst[:, C_NEW + 64 * gp:C_NEW + 64 * gp + 64]
                masked(("Sn", gp), ssb[:, 2048:2112], ps(("Sn", gp))[:, 0:64], nm, 4)
                frees(masked(("Sn", gp), wsb[:, 512:576], ps(("Sn", gp))[:, 64:128], nm, 6), ("Sn", gp))
                want_emptied(dve, ("Sn", gp))
                dve.tensor_reduce(small[:, 112:113], small[:, 104:109], AX, ALU.min)
                dve.tensor_reduce(small[:, 113:114], small[:, 109:111], AX, ALU.min).then_inc(s_min, 1)
                if gp == 3:
                    ada_rows(ADA_FIRST)
                if more:
                    cmp_groups(gp + 1)
                    cmp_importance(gp + 1)
                for i in (1, 3, 5):
                    key = ("PT", gp, i)
                    if i == 5:
                        evac(key, pTn, ps(key)[0:TS, 0:256].rearrange("p (x n) -> p x n", x=2))
                    else:
                        evac(key, pT[:, 4 * i:4 * i + 4, :], ps(key)[:, :].rearrange("p (s n) -> p s n", s=4))
                if more:
                    key_part(gp + 1, 0)
                    key_part(gp + 1, 1)
                    cmp_select(gp + 1)
                else:
                    cmp_shifted(0)
                    cmp_normed(0)
                dve.wait_ge(s_exp, 2 * gp + 2)
                link(dve.reciprocal(small[:, 116:118], small[:, 114:116]))
                for x in range(2):
                    key = ("O", gp, x)
                    want_filled(dve, key)
                    for i in range(4):
                        r = slice(32 * i, 32 * i + 32)
                        ins = dve.tensor_scalar(orow[r, gp, 1 + x, :], ps(key)[r, 64 * (i % 2):64 * (i % 2) + 64],
                                                small[r, 116 + x:117 + x], None, ALU.mult)
                    frees(ins, key)
                want_emptied(dve, ("cO", gp))
                want_emptied(dve, ("O", gp, 1))
                dve.tensor_copy(small[:, 251:252], orow[:, gp, 2, 0:1]).then_inc(o_row, 1)

            def add_branch(t, x):
                key = ("pO", t, x)
                ov = pj[:, t, 0:512].rearrange("p (h d) -> p h d", h=8)
                ot = otmp.rearrange("p (h d) -> p h d", h=8)
                cf = small[:, 168 + 8 * x:176 + 8 * x]
                if x:
                    dve.wait_ge(p_soft, 8 * (2 * t + x))
                    link(dve.reciprocal(cf, small[:, 120 + 8 * x:128 + 8 * x]))
                    link(dve.tensor_tensor(cf, cf, gate[:, t, :, x], ALU.mult))
                    cf = cf.unsqueeze(2).to_broadcast([128, 8, 64])
                else:
                    cf = gate[:, t, :, 0:1].to_broadcast([128, 8, 64])
                want_filled(dve, key)
                frees(dve.tensor_tensor(ot if x else ov, ps(key)[:, :].rearrange("p (h d) -> p h d", h=8), cf, ALU.mult), key)
                want_emptied(dve, key)
                if x == 1:
                    link(dve.tensor_tensor(ov, ov, ot, ALU.add))
                if x == 2:
                    dve.tensor_tensor(ov, ov, ot, ALU.add).then_inc(attn_ready, 1)

            def sample_out():
                dve.wait_ge(rows_back, 128)
                ov = pj[0:TS, 4, 0:512].rearrange("p (h d) -> p h d", h=8)
                ot = otmp[0:TS, :].rearrange("p (h d) -> p h d", h=8)
                for x in range(3):
                    cf = gate[0:TS, 4, :, x:x + 1].to_broadcast([TS, 8, 64])
                    link(dve.tensor_tensor(ot if x else ov, osm[:, :, x, :], cf, ALU.mult))
                    if x == 1:
                        link(dve.tensor_tensor(ov, ov, ot, ALU.add))
                    if x == 2:
                        dve.tensor_tensor(ov, ov, ot, ALU.add).then_inc(attn_ready, 1)
                        dve.wait_ge(attn_ready, 2)

            def out_scaled(tiles, n):
                dve.wait_ge(a_root, n)
                link(dve.reciprocal(small[:, 16:21], small[:, 8:13]))
                for t in tiles:
                    P = TM[t]
                    dve.tensor_scalar(pj[0:P, t, 0:512], pj[0:P, t, 0:512], small[0:P, 16 + t:17 + t], None, ALU.mult
                                      ).then_inc(a_ready, 1)

            def out_turned(t):
                key = ("oT", t)
                want_filled(dve, key)
                frees(dve.tensor_tensor(oT[:, :, 128 * t:128 * t + TM[t]],
                                        ps(key)[:, 0:4 * TM[t]].rearrange("p (k n) -> p k n", k=4),
                                        colT[:, 16:20].unsqueeze(2).to_broadcast([128, 4, TM[t]]), ALU.mult), key)

            for g in range(NG):
                t, br, i = head(g)
                w, key = 128 * (t + 1), ("pS", g)
                want_filled(dve, key)
                if g >= 5:
                    want_filled(dve, ("pPT", g - 5))
                frees(dve.tensor_tensor_reduce(psb[g % 5][:, 0:w], ps(key)[:, 0:w], cst[:, C_CAUS + 512 - w:C_CAUS + 512],
                                               -QS, 3e38, ALU.add, ALU.min, small[:, 144 + i:145 + i]), key)
                n, step = divmod(g, ADA_STEPS)
                if step == 8 and ADA_PROMPT + n < 12:
                    ada_rows(ADA_PROMPT + n)
                if t < 3 and br and i == 0:
                    cmp_shifted(t + 1)
                if br == 0 and i == 2:
                    add_branch(t, 0)
                if i == 4 and br:
                    add_branch(t, 1)
                elif i == 4 and t:
                    add_branch(t - 1, 2)
                if t < 3 and br and i == 5:
                    cmp_normed(t + 1)
                if (t, br, i) == (1, 0, 6):
                    sample_out()
                if (t, br, i) == (3, 0, 6):
                    dve.wait_ge(rows_out, 64)
                    out_scaled(OUT_ORDER[:4], 1)
                if g and head(g - 1) in FINISH:
                    out_turned(FINISH[head(g - 1)])
            add_branch(3, 2)
            out_scaled([3], 2)
            out_turned(3)
            mod_cols(1)
            def second_norm(t):
                P = TM[t]
                dve.wait_ge(x1_root, t + 1)
                if t >= 2:
                    want_filled(dve, ("hT", t - 2, 1))
                link(dve.reciprocal(small[0:P, 24 + t:25 + t], small[0:P, 24 + t:25 + t]))
                dve.tensor_scalar(xnb[0:P, t % 2, :], xs[0:P, t, :], small[0:P, 24 + t:25 + t], None, ALU.mult
                                  ).then_inc(x1n_ready, 1)

            def first_half(t):
                key, cols, (_, _, z, zl) = ("hT", t, 0), slice(128 * t, 128 * t + 128), hlo_at[0]
                want_filled(dve, key)
                for k in range(4):
                    ins = dve.tensor_scalar(hraw[k][:, cols], ps(key)[:, 128 * k:128 * k + 128],
                                            mod[:, 1, 0, k, 0:1], mod[:, 1, 1, k, 0:1], ALU.mult, ALU.add)
                frees(ins, key)
                want_emptied(dve, key)
                link(high(dve.tensor_copy, hhi[:, 0:4, cols], z[:, :, cols]))
                low(dve, zl[:, :, cols], z[:, :, cols], hhi[:, 0:4, cols]).then_inc(h_low, 1)

            def low_job(j):
                dve.wait_ge(hi_ready, j + 1)
                for raw, hi, lo in job_parts(j):
                    ins = low(dve, lo, raw, hi)
                if j == NFT:
                    ins.then_inc(lo_ready, 1)
                    for k in range(4):
                        dve.wait_ge(first_high, k + 1)
                        low(dve, hhi[:, 4 + k], actT[:, k], hhi[:, k]).then_inc(first_low, 1)
                    return
                if j > NFT:
                    for raw, hi, lo in job_acts(j):
                        ins = low(dve, lo, raw, hi)
                ins.then_inc(lo_ready, 1)

            dve.wait_ge(stored, 16 * N_STORED)
            dve.wait_ge(kvc_stored, 32)
            dve.wait_ge(xin_loaded, 80)
            for n in range(2):
                cols = slice(512 * n, 512 * n + 512)
                for t in range(6):
                    if n and t:
                        second_norm(t - 1)
                    if t < 5:
                        key, i, P = ("wo", n, t), 5 * n + t, TM[t]
                        want_filled(dve, key)
                        dve.wait_ge(gates_in, 32)
                        frees(dve.tensor_tensor(x1t[0:P, i % 2, :], ps(key)[0:P, :], gbc[0:P, t // 4, cols], ALU.mult), key)
                        want_emptied(dve, key)
                        dve.tensor_tensor(xs[0:P, t, cols], x1t[0:P, i % 2, :], xin[0:P, t, cols], ALU.add).then_inc(x1_ready, 1)
                    if n and 1 <= t < 5:
                        first_half(t - 1)
            dve.wait_ge(lo_ready, 1)
            low_job(1)
            for h in range(2):
                key = ("hT", 4, h)
                want_filled(dve, key)
                dst = [hlo_at[0:1], hlo_at[1:]][h]
                for k0, n, z, zl in dst:
                    v = z[:, :, SEQ:TOK].rearrange("p k (b q) -> p k b q", b=8)
                    A, B = (mod[:, 1, x, k0:k0 + n, 1:9].unsqueeze(3).to_broadcast([128, n, 8, 8]) for x in range(2))
                    src = ps(key)[:, 64 * (k0 % 4):64 * (k0 % 4) + 64 * n].rearrange("p (k b q) -> p k b q", k=n, b=8)
                    ins = dve.tensor_tensor(v, src, A, ALU.mult)
                    if k0 + n in (4, 8):
                        frees(ins, key)
                        want_emptied(dve, key)
                    else:
                        link(ins)
                    link(dve.tensor_tensor(v, v, B, ALU.add))
                    w = z[:, :, SEQ:TOK]
                    link(high(dve.tensor_copy, hhi[:, k0:k0 + n, SEQ:TOK], w))
                    ins = low(dve, zl[:, :, SEQ:TOK], w, hhi[:, k0:k0 + n, SEQ:TOK])
                ins.then_inc(h_low, 1)

            for i, h in GU_ORDER:
                key = ("gu", i, 1, h)
                want_filled(dve, key)
                want_emptied(dve, ("gu", i, 0, h))
                frees(dve.tensor_tensor(actT[:, i, HALF * h:HALF * h + HALF], ps(key)[:, 0:HALF],
                                        sgb[:, i % 2, HALF * h:HALF * h + HALF], ALU.mult), key)
                if (i, h) == (0, 1):
                    low_job(2)
                if i > 1 and h == 0:
                    low_job(i + 1)
            for j in range(NFT + 1, NFT + 7):
                low_job(j)
            for n in range(2):
                cols = slice(512 * n, 512 * n + 512)
                for t in range(5):
                    key, i, P = ("dn", n, t), 5 * n + t, TM[t]
                    want_filled(dve, key)
                    dve.wait_ge(gates_in, 64)
                    frees(dve.tensor_tensor(yt[0:P, i % 2, :], ps(key)[0:P, :], gbc[0:P, t // 4, cols], ALU.mult), key)
                    want_emptied(dve, key)
                    dve.tensor_tensor(xs[0:P, t, cols], yt[0:P, i % 2, :], xs[0:P, t, cols], ALU.add).then_inc(out_ready, 1)
                if n == 0:
                    for j in range(NFT + 7, NFT + 12):
                        low_job(j)

        @block.tensor
        def _(pe):
            def turn(dst, src):
                P = src.shape[0]
                return pe.transpose(dst, src, ident[0:P, 0:P])

            def products(dst, pairs, first, last):
                for k, ((sh, sl), (mh, ml)) in enumerate(pairs):
                    pe.matmul(dst, sh, ml, start=first and k == 0, stop=False)
                    pe.matmul(dst, sl, mh, start=False, stop=False)
                    ins = pe.matmul(dst, sh, mh, start=False, stop=last and k == len(pairs) - 1)
                return ins

            pe.wait_ge(ident_loaded, 16)
            pe.wait_ge(scrow_ready, 1)
            for k in range(8):
                ins = turn(ps(("cT",))[:, 9 * k:9 * k + 9], scrow[:, 128 * k:128 * k + 128])
            fills(ins, ("cT",))

            def mod_turn(l):
                key = ("mod", l)
                want_free(pe, key)
                for n in range(4):
                    want_emptied(pe, ("ada", n + 6 * l))
                src, eye = (modss, ident[0:9, 0:9]) if l == 0 else (modss2, ident[32:41, 32:41])
                for i in range(16):
                    ins = pe.transpose(ps(key)[:, 9 * i:9 * i + 9], src[:, 128 * i:128 * i + 128], eye)
                fills(ins, key)

            def ada_product(n, kk):
                key = ("ada", n)
                if kk == 0:
                    want_free(pe, key)
                w = weights(pe, ("ada", n, kk // 4))
                ins = pe.matmul(ps(key)[0:9, :], cT[:, 9 * kk:9 * kk + 9], w[:, kk % 4, :], start=kk == 0, stop=kk == 7)
                if kk == 7:
                    fills(ins, key)

            def ada(n):
                for kk in range(8):
                    ada_product(n, kk)

            want_emptied(pe, ("cT",))
            ada(0)
            ada(1)
            pe.wait_ge(gains_loaded, 160)
            fills(turn(ps(("rows",))[:, 0:52], rowb[:, :]), ("rows",))
            for t in range(5):
                pe.wait_ge(xn_ready, t + 1)
                for h in range(2):
                    key = ("xT", t, h)
                    want_free(pe, key)
                    for k in range(4):
                        f = 128 * (4 * h + k)
                        ins = turn(ps(key)[:, TM[t] * k:TM[t] * k + TM[t]], xs[0:TM[t], t, f:f + 128])
                    fills(ins, key)
            ada(2)
            ada(3)
            mod_turn(0)
            pe.wait_ge(conv_state_loaded, 16)
            want_free(pe, ("sconv",))
            for m in range(4):
                ins = turn(ps(("sconv",))[:, 16 * m:16 * m + 16], stc[:, 128 * m:128 * m + 128])
            fills(ins, ("sconv",))
            for n in range(4, ADA_FIRST):
                ada(n)
            pe.wait_ge(comp_w_loaded, 96)
            want_emptied(pe, ("rows",))
            for x in range(2):
                key = ("peb", x)
                want_free(pe, key)
                for i in range(16):
                    ins = pe.matmul(ps(key)[0:64, 0:1], w1v[:, x, i % 8, i // 8, :], colT[:, 36 + i:37 + i],
                                    start=i == 0, stop=i == 15)
                fills(ins, key)
            pe.wait_ge(consts_loaded, 16)

            for n in range(3):
                w = min(512, TEND - 512 * n)
                for kh in range(2):
                    j = 2 * n + kh
                    pe.wait_ge(lo1_ready, j + 1)
                    pe.wait_ge(hT_ready, 8 if kh else 4)
                    wv = ws1[j % 2].rearrange("p x (k c) -> p x k c", k=4)
                    for t in range(5):
                        key, cols = ("in", n, t), slice(128 * t, 128 * t + TM[t])
                        if kh == 0:
                            want_free(pe, key)
                        ins = products(ps(key)[0:TM[t], 0:w],
                                       [((h1hi[4 * kh + k][:, cols], h1lo[4 * kh + k][:, cols]),
                                         (wv[:, 0, k, 0:w], wv[:, 1, k, 0:w])) for k in range(4)], kh == 0, kh == 1)
                        if kh:
                            fills(ins, key)
                    if kh == 0:
                        ins.then_inc(in_read, 1)
            for n in range(3):
                for m in range(4):
                    j = 6 + 2 * n + m // 2
                    pe.wait_ge(lo1_ready, j + 1)
                    wv = ws1[j % 2].rearrange("p x (k c) -> p x k c", k=8)
                    for h in range(2):
                        key, cols, f = ("cv", n, m, h), slice(HALF * h, HALF * h + HALF), 128 * (m % 2)
                        want_free(pe, key)
                        fills(products(ps(key)[:, 0:HALF], [((wv[:, 0, k, f:f + 128], wv[:, 1, k, f:f + 128]),
                                                             (h1hi[k][:, cols], h1lo[k][:, cols])) for k in range(8)],
                                       True, True), key)
            pe.wait_ge(u_end_ready, 4)
            want_free(pe, ("ulast",))
            for m in range(4):
                ins = turn(ps(("ulast",))[0:18, 128 * m:128 * m + 128], ulast[:, 18 * m:18 * m + 18])
            fills(ins, ("ulast",))
            def turn_chunks(u):
                n = CH if u < 16 else PCH
                xc = cache(pe, u)
                for i in range(4):
                    key = ("xt", u, i)
                    want_free(pe, key)
                    for jj in range(4):
                        ins = turn(ps(key)[:, 128 * jj:128 * jj + n], xc[0:n, 2 * (4 * (i // 2) + jj) + i % 2, :])
                    fills(ins, key)

            def turn_queries():
                pe.wait_ge(nrm_done, 9)
                for g in range(G):
                    for s in range(2):
                        key = ("qT", g, s)
                        want_free(pe, key)
                        for t in (range(4), (4,))[s]:
                            c0 = 128 * (t % 4)
                            ins = turn(ps(key)[:, c0:c0 + TM[t]],
                                       pj[0:TM[t], t, 128 * g:128 * g + 128])
                        fills(ins, key)
                for x, c in enumerate((TKS, TKW)):
                    key = ("kT", x)
                    want_free(pe, key)
                    for t in range(4):
                        ins = turn(ps(key)[:, 128 * t:128 * t + 128], pj[:, t, c:c + 128])
                    fills(ins, key)
                want_free(pe, ("kTn",))
                for x, c in enumerate((TKS, TKW)):
                    ins = turn(ps(("kTn",))[:, 64 * x:64 * x + 64], pj[0:TS, 4, c:c + 128])
                fills(ins, ("kTn",))


            turn_chunks(0)
            pe.wait_ge(y_square, 4)
            for h in range(2):
                key = ("yss", h)
                want_free(pe, key)
                for m in range(4):
                    ins = pe.matmul(ps(key)[:, 0:HALF], cst[:, C_ONE:C_ONE + 128], hcT[:, m, HALF * h:HALF * h + HALF],
                                    start=m == 0, stop=m == 3)
                fills(ins, key)
            for u in range(19):
                if u < 17:
                    turn_chunks(u + 1)
                if u < 18:
                    n, key = (CH if u < 16 else PCH), ("pre", u)
                    want_free(pe, key)
                    for i in range(4):
                        want_emptied(pe, ("xt", u, i))
                    for j in range(8):
                        ins = pe.matmul(ps(key)[:, 0:2 * n], w1v[:, u % 2, j].rearrange("p r h -> p (r h)"),
                                        xcmp[:, u % 2, j, :, 0:n], start=j == 0, stop=j == 7)
                    fills(ins, key)
                if u == 18:
                    turn_queries()
                if u:
                    key, m, x = ("cmp", u - 1), (NC if u <= 16 else PNC), (u - 1) % 2
                    want_free(pe, key)
                    pe.wait_ge(silu_ready, u)
                    for k in range(2):
                        ins = pe.matmul(ps(key)[0:m, 64 * k:64 * k + 64], slu[:, k, 0:m], w2[:, 64 * x:64 * x + 64],
                                        start=True, stop=True)
                    fills(ins, key)
            def turn_keys(gp, c):
                for b in range(2):
                    key = ("T", gp, c, b)
                    want_free(pe, key)
                    if c < 4:
                        kk = cache(pe, 18 + 4 * gp + b)[:, 4 * c:4 * c + 4, :]
                    else:
                        pe.wait_ge(win_loaded[0], 32 * (gp + 1))
                        kk = wnd[:, 0, b, :].rearrange("p (s n) -> p s n", s=4)
                    for i in range(4):
                        ins = turn(ps(key)[:, 128 * i:128 * i + 128], kk[:, i, :])
                    fills(ins, key)

            turn_keys(0, 0)
            turn_keys(0, 1)
            for i in range(3):
                ada_product(ADA_FIRST, i)
            for i in range(3):
                pe.wait_ge(nrm_done, 12 if i == 2 else 11)
                key = ("kct", i)
                want_free(pe, key)
                for b in range(4 * i, min(4 * i + 4, 9)):
                    m = NC if b < 8 else PNC
                    c0 = 128 * (b - 4 * i)
                    ins = turn(ps(key)[:, c0:c0 + m], kcm[0:m, b, :])
                fills(ins, key)
            for g in range(G):
                want_emptied(pe, ("qT", g, 1))
            for i in range(3):
                want_emptied(pe, ("kct", i))

            def cmp_scores(gp):
                key = ("cS", gp)
                want_free(pe, key)
                for b in range(2):
                    bb = 2 * gp + b
                    ins = pe.matmul(ps(key)[64 * b:64 * b + 64, 0:NC], qblk[:, 64 * bb:64 * bb + 64], kcT[:, bb, 0:NC],
                                    start=True, stop=True)
                fills(ins, key)

            def cmp_turn(gp):
                key = ("cPT", gp)
                want_free(pe, key)
                pe.wait_ge(c_prob, gp + 1)
                fills(turn(ps(key)[0:NC, 0:128], csb), key)

            def cmp_values(gp):
                key = ("imp", gp)
                want_free(pe, key)
                pe.wait_ge(c_group, gp + 1)
                fills(pe.matmul(ps(key)[:, 0:32], cpx, cst[0:NC, C_OVL:C_OVL + 32],
                                start=True, stop=True), key)
                key = ("cO", gp)
                want_free(pe, key)
                want_emptied(pe, ("cPT", gp))
                for b in range(2):
                    ins = pe.matmul(ps(key)[64 * b:64 * b + 64, 0:128], ctb[:, 64 * b:64 * b + 64], vcm[0:NC, 2 * gp + b, :],
                                    start=True, stop=True)
                fills(ins, key)

            def score(gp, c):
                key = ("S", gp, c)
                want_free(pe, key)
                for b in range(2):
                    want_emptied(pe, ("T", gp, c, b))
                for b in range(2):
                    bb = 2 * gp + b
                    ins = pe.matmul(ps(key)[64 * b:64 * b + 64, :], qblk[:, 64 * bb:64 * bb + 64], kTc[:, b, c % 2, :],
                                    start=True, stop=True)
                fills(ins, key)

            def score_new(gp):
                key = ("Sn", gp)
                want_free(pe, key)
                for b in range(2):
                    bb = 2 * gp + b
                    ins = pe.matmul(ps(key)[64 * b:64 * b + 64, 0:128], qblk[:, 64 * bb:64 * bb + 64],
                                    kTn.rearrange("p x n -> p (x n)"), start=True, stop=True)
                fills(ins, key)

            def turn_probs(gp):
                for i in range(6):
                    key = ("PT", gp, i)
                    want_free(pe, key)
                    pe.wait_ge(s_exp, 2 * gp + (1 if i < 4 else 2))
                    if i < 5:
                        src = wsb[:, 0:512] if i == 4 else ssb[:, 512 * i:512 * i + 512]
                        for s in range(4):
                            ins = turn(ps(key)[:, 128 * s:128 * s + 128], src[:, 128 * s:128 * s + 128])
                    else:
                        turn(ps(key)[0:TS, 0:128], ssb[:, 2048:2112])
                        ins = turn(ps(key)[0:TS, 128:256], wsb[:, 512:576])
                    fills(ins, key)

            def values(gp):
                for i in range(6):
                    want_emptied(pe, ("PT", gp, i))
                for x in range(2):
                    key = ("O", gp, x)
                    want_free(pe, key)
                    if x:
                        pe.wait_ge(win_loaded[1], 32 * (gp + 1))
                    for b in range(2):
                        r = slice(64 * b, 64 * b + 64)
                        if x:
                            vv, pp, ns, vc = wnd[:, 1, b, :].rearrange("p (s n) -> p s n", s=4), pTw, 4, TVW
                        else:
                            vv, pp, ns, vc = cache(pe, 20 + 4 * gp + b), pT, 16, TVS
                        for s in range(ns):
                            pe.matmul(ps(key)[r, 0:128], pp[:, s, r], vv[:, s, :], start=s == 0, stop=False)
                        ins = pe.matmul(ps(key)[r, 0:128], pTn[:, x, r], pj[0:TS, 4, vc:vc + 128], start=False, stop=True)
                    fills(ins, key)

            for g in range(G):
                want_emptied(pe, ("qT", g, 0))
            for x in range(2):
                want_emptied(pe, ("kT", x))
            def rows(h):
                return slice(64 * (h // G), 64 * (h // G) + 64)

            def q_of(t, h):
                return qTp[rows(h), h % G, 128 * t:128 * t + 128]

            def prompt_cmp_products(t):
                for k in range(NKV):
                    key = ("pcS", t, k)
                    want_free(pe, key)
                    for g in range(G):
                        ins = pe.matmul(ps(key)[:, PNC * g:PNC * g + PNC], q_of(t, G * k + g), kcT[rows(G * k), 8, 0:PNC],
                                        start=True, stop=True)
                    fills(ins, key)

            want_emptied(pe, ("kTn",))
            cmp_scores(0)
            ada_product(ADA_FIRST, 3)
            ada_product(ADA_FIRST, 4)
            cmp_turn(0)
            ada_product(ADA_FIRST, 5)
            cmp_values(0)
            for gp in range(4):
                more = gp < 3
                score(gp, 0)
                turn_keys(gp, 2)
                score(gp, 1)
                if more:
                    cmp_scores(gp + 1)
                turn_keys(gp, 3)
                score(gp, 2)
                turn_keys(gp, 4)
                score(gp, 3)
                if more:
                    cmp_turn(gp + 1)
                score(gp, 4)
                score_new(gp)
                if gp == 1:
                    ada_product(ADA_FIRST, 6)
                    ada_product(ADA_FIRST, 7)
                if more:
                    cmp_values(gp + 1)
                turn_probs(gp)
                if more:
                    turn_keys(gp + 1, 0)
                    turn_keys(gp + 1, 1)
                else:
                    prompt_cmp_products(0)
                values(gp)

            def out_turn(t):
                key = ("oT", t)
                want_free(pe, key)
                pe.wait_ge(a_ready, OUT_ORDER.index(t) + 1)
                for k in range(4):
                    ins = turn(ps(key)[:, TM[t] * k:TM[t] * k + TM[t]], pj[0:TM[t], t, 128 * k:128 * k + 128])
                fills(ins, key)

            for g in range(NG + LAG + 1):
                t, br, i = head(g)
                if g < NG:
                    key = ("pS", g)
                    want_free(pe, key)
                    fills(pe.matmul(ps(key)[:, 0:128 * (t + 1)], q_of(t, i), kTp[rows(i), br, 0:128 * (t + 1)],
                                    start=True, stop=True), key)
                    n, kk = divmod(g, ADA_STEPS)
                    if kk < 8 and ADA_PROMPT + n < 12:
                        ada_product(ADA_PROMPT + n, kk)
                    if br == 0 and i == 0:
                        pe.wait_ge(p_prob, t + 1)
                        for hh in range(2):
                            key = ("pcPT", t, hh)
                            want_free(pe, key)
                            for j in range(4):
                                ins = turn(ps(key)[0:PNC, 128 * j:128 * j + 128], pcp[:, 4 * hh + j, :])
                            fills(ins, key)
                    if br == 0 and i == 1:
                        key = ("pO", t, 0)
                        want_free(pe, key)
                        for hh in range(2):
                            want_emptied(pe, ("pcPT", t, hh))
                        for h in range(NH):
                            ins = pe.matmul(ps(key)[:, 64 * h:64 * h + 64], ppTc[:, h, :], vcm[0:PNC, 8, rows(h)],
                                            start=True, stop=True)
                        fills(ins, key)
                if LAG <= g < NG + LAG:
                    v = g - LAG
                    key = ("pPT", v)
                    want_free(pe, key)
                    pe.wait_ge(p_soft, v + 1)
                    for k in range(head(v)[0] + 1):
                        ins = turn(ps(key)[:, 128 * k:128 * k + 128], psb[v % 5][:, 128 * k:128 * k + 128])
                    fills(ins, key)
                if g > LAG:
                    v = g - LAG - 1
                    tv, bv, h = head(v)
                    okey = ("pO", tv, 1 + bv)
                    if h == 0:
                        want_free(pe, okey)
                    want_emptied(pe, ("pPT", v))
                    c0 = (TVS, TVW)[bv] + 64 * (h // G)
                    for k in range(tv + 1):
                        ins = pe.matmul(ps(okey)[:, 64 * h:64 * h + 64], ppT[v % 4][:, k, :], pj[:, k, c0:c0 + 64],
                                        start=k == 0, stop=k == tv)
                    if h == NH - 1:
                        fills(ins, okey)
                if g < NG:
                    if (t, br, i) in FINISH:
                        out_turn(FINISH[t, br, i])
                    if t < 3 and br == 0 and i == 7:
                        prompt_cmp_products(t + 1)
            mod_turn(1)
            pe.wait_ge(vT_ready, 4)
            def project_out(n, t):
                key = ("wo", n, t)
                want_free(pe, key)
                want_emptied(pe, ("oT", t))
                for kk in range(8):
                    wt = weights(pe, ("wo", n, kk // 4))
                    src = oT if kk < 4 else vT
                    ins = pe.matmul(ps(key)[0:TM[t], :], src[:, kk % 4, 128 * t:128 * t + TM[t]], wt[:, kk % 4, :],
                                    start=kk == 0, stop=kk == 7)
                fills(ins, key)

            def turn_normed(t):
                pe.wait_ge(x1n_ready, t + 1)
                for h in range(2):
                    key = ("hT", t, h)
                    want_free(pe, key)
                    for k in range(4):
                        f = 128 * (4 * h + k)
                        ins = turn(ps(key)[:, TM[t] * k:TM[t] * k + TM[t]], xnb[0:TM[t], t % 2, f:f + 128])
                    fills(ins, key)
            def gate_up(i, h):
                pe.wait_ge(h_low, 6 if h else 3)
                pe.wait_ge(h_low2, 4 if h else 3)
                pe.wait_ge(lo_ready, i + 1)
                wv = ws[:, (i + 1) % 2].rearrange("p y (k x c) -> p y k x c", k=8, x=2)
                for x in range(2):
                    key = ("gu", i, x, h)
                    want_free(pe, key)
                    cols = slice(HALF * h, HALF * h + HALF)
                    fills(products(ps(key)[:, 0:HALF], [((wv[:, 0, k, x], wv[:, 1, k, x]), (hhi[:, k, cols], hlo[k][:, cols]))
                                                        for k in range(8)], True, True), key)

            for t in range(5):
                if t == 2:
                    out_turn(3)
                project_out(0, t)
            for t in range(6):
                if t < 5:
                    project_out(1, t)
                else:
                    gate_up(0, 0)
                if t:
                    turn_normed(t - 1)
            for i, h in GU_ORDER[1:]:
                gate_up(i, h)
            for n in range(2):
                for kc in range(6):
                    j = NFT + 6 * n + kc
                    pe.wait_ge(lo_ready, j + 1)
                    acts, wv = act_pairs(j), ws[:, (j + 1) % 2]
                    if j == NFT:
                        for t in range(5):
                            want_free(pe, ("dn", n, t))
                        for k, (hi, lo) in enumerate(acts):
                            pe.wait_ge(first_low, k + 1)
                            for t in range(5):
                                cols = slice(128 * t, 128 * t + TM[t])
                                ins = products(ps(("dn", n, t))[0:TM[t], :],
                                               [((hi[:, cols], lo[:, cols]),
                                                 (wv[:, 0, 512 * k:512 * k + 512], wv[:, 1, 512 * k:512 * k + 512]))],
                                               k == 0, False)
                        ins.then_inc(dn_read, 1)
                        continue
                    for t in range(5):
                        key, cols = ("dn", n, t), slice(128 * t, 128 * t + TM[t])
                        if kc == 0:
                            want_free(pe, key)
                        ins = products(ps(key)[0:TM[t], :],
                                       [((hi[:, cols], lo[:, cols]), (wv[:, 0, 512 * k:512 * k + 512], wv[:, 1, 512 * k:512 * k + 512]))
                                        for k, (hi, lo) in enumerate(acts)], kc == 0, kc == 5)
                        if kc == 5:
                            fills(ins, key)
                    if kc < 5:
                        ins.then_inc(dn_read, 1)


NORMS = [("q", 128, 8, t, 1, 8, 0) for t in range(4)]
NORMS += [("q", TS, 8, 4, 1, 8, 0), ("ks", 128, 8, 0, 4, 2, 2), ("ks", TS, 2, 4, 1, 2, 2), ("kw", 128, 8, 0, 4, 2, 3),
          ("kw", TS, 2, 4, 1, 2, 3), ("kcm", NC, 8, 0, 4, 2, 1), ("kcm", NC, 8, 4, 4, 2, 1), ("kcm", PNC, 2, 8, 1, 2, 1)]
NORM_COL = [sum(x[2] for x in NORMS[:i]) for i in range(len(NORMS) + 1)]
NORM_GROUP = [range(0, 9), range(9, 10), range(10, 11), range(11, 12)]
SUM_AT = {1: (0, 1), 2: (2, 3), 3: (4, 5, 6), 4: (7, 8), 11: (9,), 17: (10,)}
ROOT_AT = [5, 11, 17]
APPLY_AT = {5: (0,), 6: (1,), 7: (2,), 8: (3,), 9: (4, 5), 10: (6, 7, 8), 11: (9,), 17: (10,)}


def norm_cols(group):
    return NORM_COL[NORM_GROUP[group][0]], NORM_COL[NORM_GROUP[group][-1] + 1]


N_STORED = 3 + 1 + 1 + 2 + 8 + 2 + 1 + 8 + 2

_INS = ["x_prompt", "x_sample", "cache_k_cmp", "cache_v_cmp", "cache_k_slc", "cache_v_slc", "state_k_win", "state_v_win",
        "state_conv", "page_table", "c_prompt", "c_sample", "w_ada", "b_ada", "ln1_g", "w_in", "q_norm_g", "k_norm_g",
        "pe_cmp", "w_ck1", "w_ck2", "w_cv1", "w_cv2", "w_conv", "attn_out_g", "conv_out_g", "w_o", "ln2_g", "w_gu", "w_down"]
_OUTS = [("y_prompt", (1, SEQ, D)), ("y_sample", (NB, NQ, D))]
_OUTS += [(f"p_{n}", (1, 1, SEQ, NKV, HD)) for n in ("k_cmp", "v_cmp", "k_slc", "v_slc", "k_win", "v_win")]
_OUTS += [("p_conv", (1, 1, 2, 512))]
_OUTS += [(f"s_{n}", (1, NB, NQ, NKV, HD)) for n in ("k_cmp", "v_cmp", "k_slc", "v_slc")]
_OUTS += [(f"s_{n}", (1, NB, SEQ, NKV, HD)) for n in ("k_win", "v_win")]
_OUTS += [("s_conv", (1, NB, 2, 512))]


def kernel(**inputs):
    import numpy as _np
    import concourse.bacc as _bacc
    from concourse import mybir as _mybir
    from concourse.bass_utils import run_bass_kernel_spmd as _run

    nc = _bacc.Bacc("TRN2", target_bir_lowering=False, num_devices=1)
    arrays, ins, outs = {}, {}, {}
    given = {name: _np.ascontiguousarray(inputs[name]) for name in _INS}
    given["consts"] = constants()
    for name, x in given.items():
        arrays[f"in_{name}"] = x
        ins[name] = nc.dram_tensor(f"in_{name}", x.shape, _mybir.dt.from_np(x.dtype), kind="ExternalInput").ap()
    for name, shape in _OUTS:
        outs[name] = nc.dram_tensor(f"out_{name}", shape, F32, kind="ExternalOutput").ap()
    decoder_kernel(nc, ins, outs)
    r = _run(nc, [arrays], core_ids=[0])
    return tuple(r.results[0][f"out_{name}"] for name, _ in _OUTS)
```
